# Optimizing a Trainium2 kernel written in Bass

```python
import math
import jax, jax.numpy as jnp
from jax import lax
import numpy as np

D_MODEL = 1024
BATCH = 1
SEQ = 256
DEPTH = 2

N_A_LAYERS = (DEPTH + 1) // 2
N_B_LAYERS = DEPTH // 2
DIFF_HEAD_DIM = 64
DIFF_V_DIM = 2 * DIFF_HEAD_DIM
DIFF_HEADS = D_MODEL // DIFF_V_DIM
MOBA_HEAD_DIM = 64
MOBA_HEADS = D_MODEL // MOBA_HEAD_DIM
MOBA_BLOCK = 256
MOBA_TOPK = 3
D_FF = 4 * D_MODEL
REL_BUCKETS = 32
REL_MAX_DIST = 128
REL_HEADS = 2 * DIFF_HEADS
Q_BLOCK = 128
DEEPNORM_ALPHA = (2 * DEPTH) ** 0.25
DEEPNORM_BETA = (8 * DEPTH) ** -0.25
LN_EPS = 1e-5


def rel_bucket(rel):
    n = jnp.maximum(rel, 0)
    max_exact = REL_BUCKETS // 2
    nf = jnp.maximum(n, max_exact).astype(jnp.float32)
    large = max_exact + (jnp.log(nf / max_exact) / math.log(REL_MAX_DIST / max_exact)
                         * (REL_BUCKETS - max_exact)).astype(jnp.int32)
    large = jnp.minimum(large, REL_BUCKETS - 1)
    return jnp.where(n < max_exact, n, large)

def layer_norm(x, g, b):
    xf = x.astype(jnp.float32)
    mu = jnp.mean(xf, axis=-1, keepdims=True)
    var = jnp.mean(jnp.square(xf - mu), axis=-1, keepdims=True)
    y = (xf - mu) * lax.rsqrt(var + LN_EPS) * g.astype(jnp.float32) + b.astype(jnp.float32)
    return y.astype(x.dtype)

def diff_lambda_init(layer):
    return 0.8 - 0.6 * math.exp(-0.3 * layer)

def squared_relu_mlp(x, w_up, w_down):
    return jnp.square(jax.nn.relu(x @ w_up)) @ w_down

def diff_attention(x, w_in, lam_p, subln_g, w_out, rel_bias, lam_init):
    B, S, _ = x.shape
    H, dh, dv = DIFF_HEADS, DIFF_HEAD_DIM, DIFF_V_DIM
    qkv = x @ w_in
    q, k, v = jnp.split(qkv, [2 * H * dh, 4 * H * dh], axis=-1)
    q = q.reshape(B, S, H, 2, dh) * (dh ** -0.5)
    k = k.reshape(B, S, H, 2, dh)
    v = v.reshape(B, S, H, dv)
    lf = lam_p.astype(jnp.float32)
    lam = jnp.exp(jnp.sum(lf[0] * lf[1])) - jnp.exp(jnp.sum(lf[2] * lf[3])) + lam_init
    kpos = jnp.arange(S)

    def block(i):
        q_blk = lax.dynamic_slice_in_dim(q, i * Q_BLOCK, Q_BLOCK, axis=1)
        qpos = i * Q_BLOCK + jnp.arange(Q_BLOCK)
        rel = qpos[:, None] - kpos[None, :]
        bias = rel_bias[rel_bucket(rel)].astype(jnp.float32)
        bias = bias.reshape(Q_BLOCK, S, H, 2).transpose(2, 3, 0, 1)
        s = jnp.einsum('bqhmd,bkhmd->bhmqk', q_blk, k).astype(jnp.float32) + bias
        s = jnp.where(rel >= 0, s, -jnp.inf)
        p = jax.nn.softmax(s, axis=-1)
        a = p[:, :, 0] - lam * p[:, :, 1]
        return jnp.einsum('bhqk,bkhe->bqhe', a.astype(v.dtype), v)

    o = lax.map(block, jnp.arange(S // Q_BLOCK))
    o = o.transpose(1, 0, 2, 3, 4).reshape(B, S, H, dv).astype(jnp.float32)
    o = o * lax.rsqrt(jnp.mean(o * o, axis=-1, keepdims=True) + LN_EPS)
    o = o * subln_g.astype(jnp.float32) * (1.0 - lam_init)
    return o.reshape(B, S, H * dv).astype(x.dtype) @ w_out

def shared_kv(x, w_kv):
    B, S, _ = x.shape
    H, dh, L = MOBA_HEADS, MOBA_HEAD_DIM, MOBA_BLOCK
    k, v = jnp.split(x @ w_kv, 2, axis=-1)
    k = k.reshape(B, S, H, dh).transpose(0, 2, 1, 3)
    v = v.reshape(B, S, H, dh).transpose(0, 2, 1, 3)
    n_blk = -(-S // L)
    pad = n_blk * L - S
    k = jnp.pad(k, ((0, 0), (0, 0), (0, pad), (0, 0)))
    v = jnp.pad(v, ((0, 0), (0, 0), (0, pad), (0, 0)))
    k_blocks = k.reshape(B, H, n_blk, L, dh)
    v_blocks = v.reshape(B, H, n_blk, L, dh)
    k_mean = jnp.mean(k_blocks.astype(jnp.float32), axis=3)
    return k_blocks, v_blocks, k_mean

def moba_attention(x, w_q, w_out, k_blocks, v_blocks, k_mean, rel_bias):
    B, S, _ = x.shape
    H, dh, L = MOBA_HEADS, MOBA_HEAD_DIM, MOBA_BLOCK
    n_blk = k_blocks.shape[2]
    topk = min(MOBA_TOPK, n_blk)
    scale = dh ** -0.5
    q = (x @ w_q).reshape(B, S, H, dh).transpose(0, 2, 1, 3)
    bi = jnp.arange(B)[:, None, None]
    hi = jnp.arange(H)[None, :, None]
    blk_ids = jnp.arange(n_blk)
    offs = jnp.arange(L)

    def block(i):
        q_c = lax.dynamic_slice_in_dim(q, i * Q_BLOCK, Q_BLOCK, axis=2)
        qpos = i * Q_BLOCK + jnp.arange(Q_BLOCK)
        own = (i * Q_BLOCK) // L
        g = jnp.einsum('bhqd,bhnd->bhqn', q_c.astype(jnp.float32), k_mean)
        past = blk_ids[None, :] < (qpos // L)[:, None]
        g = jnp.where(past, g, -jnp.inf)
        g_val, sel = lax.top_k(g, topk)
        sel_ok = jnp.isfinite(g_val)
        k_own = lax.dynamic_index_in_dim(k_blocks, own, axis=2, keepdims=False)
        v_own = lax.dynamic_index_in_dim(v_blocks, own, axis=2, keepdims=False)
        rel_own = qpos[:, None] - (own * L + offs)[None, :]
        b_own = rel_bias[rel_bucket(rel_own)].astype(jnp.float32).transpose(2, 0, 1)
        s_own = jnp.einsum('bhqd,bhkd->bhqk', q_c, k_own).astype(jnp.float32) * scale + b_own
        logits = [jnp.where(rel_own >= 0, s_own, -jnp.inf)]
        for j in range(topk):
            idx = sel[..., j]
            k_sel = k_blocks[bi, hi, idx]
            rel = qpos[:, None] - (idx[..., None] * L + offs)
            b_sel = rel_bias[rel_bucket(rel), hi[..., None]].astype(jnp.float32)
            s = jnp.einsum('bhqd,bhqkd->bhqk', q_c, k_sel).astype(jnp.float32) * scale + b_sel
            logits.append(jnp.where(sel_ok[..., j, None], s, -jnp.inf))
        p = jax.nn.softmax(jnp.concatenate(logits, axis=-1), axis=-1).astype(v_blocks.dtype)
        o = jnp.einsum('bhqk,bhkd->bhqd', p[..., :L], v_own)
        for j in range(topk):
            v_sel = v_blocks[bi, hi, sel[..., j]]
            o = o + jnp.einsum('bhqk,bhqkd->bhqd', p[..., (j + 1) * L:(j + 2) * L], v_sel)
        return o

    o = lax.map(block, jnp.arange(S // Q_BLOCK))
    o = o.transpose(1, 0, 3, 2, 4).reshape(B, S, H * dh)
    return o @ w_out

def first_inputs(seed: int = 0) -> dict:
    key = jax.random.key(seed)
    ks = jax.random.split(key, 20)
    f32 = jnp.float32
    D = D_MODEL
    s_in = D ** -0.5
    w_qk_a = jax.random.normal(ks[1], (N_A_LAYERS, D, 4 * D_MODEL // 2), f32) * s_in
    w_v_a = jax.random.normal(ks[2], (N_A_LAYERS, D, DIFF_HEADS * DIFF_V_DIM), f32) * s_in * DEEPNORM_BETA
    w_k_sh = jax.random.normal(ks[5], (D, MOBA_HEADS * MOBA_HEAD_DIM), f32) * s_in
    w_v_sh = jax.random.normal(ks[6], (D, MOBA_HEADS * MOBA_HEAD_DIM), f32) * s_in * DEEPNORM_BETA
    return {
        'x': jax.random.normal(ks[0], (BATCH, SEQ, D), f32),
        'w_in_a': jnp.concatenate([w_qk_a, w_v_a], axis=-1),
        'lam_a': jax.random.normal(ks[3], (N_A_LAYERS, 4, DIFF_HEAD_DIM), f32) * 0.1,
        'subln_a': 1.0 + 0.02 * jax.random.normal(ks[4], (N_A_LAYERS, DIFF_V_DIM), f32),
        'w_out_a': jax.random.normal(ks[7], (N_A_LAYERS, D, D), f32) * s_in * DEEPNORM_BETA,
        'w_kv_shared': jnp.concatenate([w_k_sh, w_v_sh], axis=-1),
        'w_q_b': jax.random.normal(ks[8], (N_B_LAYERS, D, MOBA_HEADS * MOBA_HEAD_DIM), f32) * s_in,
        'w_out_b': jax.random.normal(ks[9], (N_B_LAYERS, D, D), f32) * s_in * DEEPNORM_BETA,
        'rel_bias': jax.random.normal(ks[10], (REL_BUCKETS, REL_HEADS), f32) * 0.5,
        'ln1_g': 1.0 + 0.02 * jax.random.normal(ks[11], (DEPTH, D), f32),
        'ln1_b': 0.02 * jax.random.normal(ks[12], (DEPTH, D), f32),
        'ln2_g': 1.0 + 0.02 * jax.random.normal(ks[13], (DEPTH, D), f32),
        'ln2_b': 0.02 * jax.random.normal(ks[14], (DEPTH, D), f32),
        'w_up': jax.random.normal(ks[15], (DEPTH, D, D_FF), f32) * s_in,
        'w_down': jax.random.normal(ks[16], (DEPTH, D_FF, D), f32) * (D_FF ** -0.5) * DEEPNORM_BETA,
    }

def first_block(x, w_in_a, lam_a, subln_a, w_out_a, w_kv_shared, w_q_b, w_out_b, rel_bias,
              ln1_g, ln1_b, ln2_g, ln2_b, w_up, w_down):
    h = x
    kv = None
    for layer in range(DEPTH):
        if layer < N_A_LAYERS:
            mix = diff_attention(h, w_in_a[layer], lam_a[layer], subln_a[layer], w_out_a[layer],
                                 rel_bias, diff_lambda_init(layer))
        else:
            if kv is None:
                kv = shared_kv(h, w_kv_shared)
            j = layer - N_A_LAYERS
            mix = moba_attention(h, w_q_b[j], w_out_b[j], kv[0], kv[1], kv[2], rel_bias)
        h = layer_norm(DEEPNORM_ALPHA * h + mix, ln1_g[layer], ln1_b[layer])
        h = layer_norm(DEEPNORM_ALPHA * h + squared_relu_mlp(h, w_up[layer], w_down[layer]),
                       ln2_g[layer], ln2_b[layer])
    return h


DEPTH_2 = 1

EPS = 1e-6
NEG_INF = -1e30
FORCE_SCORE = 1e9
ROPE_THETA = 500000.0

A_HEADS = 8
A_KV_HEADS = 2
A_HEAD_DIM = 64
A_ROPE_DIM = A_HEAD_DIM // 4
CMP_LEN = 32
CMP_STRIDE = 16
CMP_HIDDEN = 256
SLC_LEN = 64
SLC_TOPK = 16
WINDOW = 512
A_WIDTH = A_HEADS * A_HEAD_DIM
A_KV_WIDTH = A_KV_HEADS * A_HEAD_DIM

B_HEADS = 8
Q_LORA = 256
KV_LORA = 128
B_NOPE = 64
B_ROPE = 32
B_V = 64
B_QK = B_NOPE + B_ROPE
B_WIDTH = B_HEADS * B_V

MIX_WIDTH = A_WIDTH + B_WIDTH
IN_SIZES = (A_WIDTH, A_KV_WIDTH, A_KV_WIDTH, A_KV_WIDTH, A_KV_WIDTH, A_KV_WIDTH, A_KV_WIDTH,
            3 * A_HEADS, Q_LORA, KV_LORA, B_ROPE)
IN_WIDTH = sum(IN_SIZES)

P_HEADS = 8
N_KEYS = 128
N_EXPERTS = N_KEYS * N_KEYS
P_KEY_DIM = 256
P_TOPK = 16
P_CHUNK = 128


def _rms(x):
    xf = x.astype(jnp.float32)
    return xf * lax.rsqrt(jnp.mean(xf * xf, axis=-1, keepdims=True) + EPS)

def rmsnorm(x, gain):
    return (_rms(x) * gain.astype(jnp.float32)).astype(x.dtype)

def rope_tables(pos, rot_dim):
    inv_freq = ROPE_THETA ** (-jnp.arange(0, rot_dim, 2, dtype=jnp.float32) / rot_dim)
    ang = pos.astype(jnp.float32)[..., None] * inv_freq
    return jnp.cos(ang), jnp.sin(ang)

def apply_rope(x, cos, sin):
    half = cos.shape[-1]
    xf = x.astype(jnp.float32)
    x1, x2, rest = xf[..., :half], xf[..., half:2 * half], xf[..., 2 * half:]
    out = jnp.concatenate([x1 * cos - x2 * sin, x2 * cos + x1 * sin, rest], axis=-1)
    return out.astype(x.dtype)

def masked_softmax(s, mask):
    s = jnp.where(mask, s.astype(jnp.float32), NEG_INF)
    p = jax.nn.softmax(s, axis=-1)
    return jnp.where(mask, p, 0.0)

def nsa_mixer(q, k_cmp, v_cmp, k_slc, v_slc, k_win, v_win, gates, positions,
              q_gain, kc_gain, ks_gain, kw_gain, cmp_pos, cmp_k_w1, cmp_k_w2, cmp_v_w1, cmp_v_w2):
    B, S = q.shape[:2]
    G, R, dk = A_KV_HEADS, A_HEADS // A_KV_HEADS, A_HEAD_DIM
    scale = dk ** -0.5
    cos, sin = rope_tables(positions, A_ROPE_DIM)
    cos_h, sin_h = cos[:, :, None, :], sin[:, :, None, :]
    q = apply_rope(rmsnorm(q, q_gain), cos_h, sin_h)
    k_slc = apply_rope(rmsnorm(k_slc, ks_gain), cos_h, sin_h)
    k_win = apply_rope(rmsnorm(k_win, kw_gain), cos_h, sin_h)

    n_cmp = (S - CMP_LEN) // CMP_STRIDE + 1
    cmp_idx = jnp.arange(n_cmp)[:, None] * CMP_STRIDE + jnp.arange(CMP_LEN)[None, :]
    cmp_start, cmp_end = cmp_idx[:, 0], cmp_idx[:, -1]

    def compress(t, w1, w2):
        blk = t[:, cmp_idx] + cmp_pos[:, None, :]
        blk = blk.transpose(0, 1, 3, 2, 4).reshape(B, n_cmp, G, CMP_LEN * dk)
        return jax.nn.gelu(blk @ w1) @ w2

    kc = compress(k_cmp, cmp_k_w1, cmp_k_w2)
    vc = compress(v_cmp, cmp_v_w1, cmp_v_w2)
    cos_c, sin_c = rope_tables(positions[:, cmp_end], A_ROPE_DIM)
    kc = apply_rope(rmsnorm(kc, kc_gain), cos_c[:, :, None, :], sin_c[:, :, None, :])

    n_slc = S // SLC_LEN
    topk = min(SLC_TOPK, n_slc)
    slc_start = jnp.arange(n_slc) * SLC_LEN
    overlap = ((cmp_start[:, None] < slc_start[None, :] + SLC_LEN)
               & (cmp_end[:, None] >= slc_start[None, :])).astype(jnp.float32)
    ks_blocks = k_slc.reshape(B, n_slc, SLC_LEN, G, dk).transpose(0, 3, 1, 2, 4)
    vs_blocks = v_slc.reshape(B, n_slc, SLC_LEN, G, dk).transpose(0, 3, 1, 2, 4)

    pad = ((0, 0), (WINDOW, 0), (0, 0), (0, 0))
    kw_pad, vw_pad = jnp.pad(k_win, pad), jnp.pad(v_win, pad)

    def block(qb):
        q0 = qb * Q_BLOCK
        t = q0 + jnp.arange(Q_BLOCK)
        qblk = lax.dynamic_slice_in_dim(q, q0, Q_BLOCK, axis=1).reshape(B, Q_BLOCK, G, R, dk)
        gblk = lax.dynamic_slice_in_dim(gates, q0, Q_BLOCK, axis=1).reshape(B, Q_BLOCK, G, R, 3)

        s_c = jnp.einsum('bqgrd,bngd->bgrqn', qblk, kc) * scale
        p_c = masked_softmax(s_c, cmp_end[None, :] <= t[:, None])
        o_c = jnp.einsum('bgrqn,bngd->bqgrd', p_c.astype(vc.dtype), vc)

        imp = jnp.einsum('bgrqn,nj->bgqj', p_c, overlap)
        j = jnp.arange(n_slc)
        forced = (j[None, :] == (t // SLC_LEN)[:, None]) | (j[None, :] == 0)
        causal_blk = slc_start[None, :] <= t[:, None]
        imp = jnp.where(forced, FORCE_SCORE, jnp.where(causal_blk, imp, NEG_INF))
        _, sel = lax.top_k(imp, topk)
        flat = sel.reshape(B, G, Q_BLOCK * topk)[..., None, None]
        ks = jnp.take_along_axis(ks_blocks, flat, axis=2).reshape(B, G, Q_BLOCK, topk * SLC_LEN, dk)
        vs = jnp.take_along_axis(vs_blocks, flat, axis=2).reshape(B, G, Q_BLOCK, topk * SLC_LEN, dk)
        tok = (sel[..., None] * SLC_LEN + jnp.arange(SLC_LEN)).reshape(B, G, Q_BLOCK, topk * SLC_LEN)
        mask_s = (tok <= t[:, None])[:, :, None]
        s_s = jnp.einsum('bqgrd,bgqsd->bgrqs', qblk, ks) * scale
        p_s = masked_softmax(s_s, mask_s)
        o_s = jnp.einsum('bgrqs,bgqsd->bqgrd', p_s.astype(vs.dtype), vs)

        kw = lax.dynamic_slice_in_dim(kw_pad, q0, Q_BLOCK + WINDOW, axis=1)
        vw = lax.dynamic_slice_in_dim(vw_pad, q0, Q_BLOCK + WINDOW, axis=1)
        s_pos = q0 - WINDOW + jnp.arange(Q_BLOCK + WINDOW)
        mask_w = ((s_pos[None, :] <= t[:, None]) & (s_pos[None, :] > t[:, None] - WINDOW)
                  & (s_pos[None, :] >= 0))
        s_w = jnp.einsum('bqgrd,bsgd->bgrqs', qblk, kw) * scale
        p_w = masked_softmax(s_w, mask_w)
        o_w = jnp.einsum('bgrqs,bsgd->bqgrd', p_w.astype(vw.dtype), vw)

        return gblk[..., 0:1] * o_c + gblk[..., 1:2] * o_s + gblk[..., 2:3] * o_w

    out = lax.map(block, jnp.arange(S // Q_BLOCK))
    return out.transpose(1, 0, 2, 3, 4, 5).reshape(B, S, A_WIDTH)

def mla_mixer(c_q, c_kv, k_rope, positions, q_lora_gain, w_uq, kv_lora_gain, w_ukv, q_gain, k_gain):
    B, S = c_q.shape[:2]
    H = B_HEADS
    cos, sin = rope_tables(positions, B_ROPE)
    cos_h, sin_h = cos[:, :, None, :], sin[:, :, None, :]
    q = (rmsnorm(c_q, q_lora_gain) @ w_uq).reshape(B, S, H, B_QK)
    kv = (rmsnorm(c_kv, kv_lora_gain) @ w_ukv).reshape(B, S, H, B_NOPE + B_V)
    k_nope, v = kv[..., :B_NOPE], kv[..., B_NOPE:]
    k = jnp.concatenate([k_nope, jnp.broadcast_to(k_rope[:, :, None, :], (B, S, H, B_ROPE))], axis=-1)
    q, k = rmsnorm(q, q_gain), rmsnorm(k, k_gain)
    q = jnp.concatenate([q[..., :B_NOPE], apply_rope(q[..., B_NOPE:], cos_h, sin_h)], axis=-1)
    k = jnp.concatenate([k[..., :B_NOPE], apply_rope(k[..., B_NOPE:], cos_h, sin_h)], axis=-1)
    scale = B_QK ** -0.5
    key_idx = jnp.arange(S)

    def block(qb):
        q0 = qb * Q_BLOCK
        t = q0 + jnp.arange(Q_BLOCK)
        qblk = lax.dynamic_slice_in_dim(q, q0, Q_BLOCK, axis=1)
        s = jnp.einsum('bqhd,bshd->bhqs', qblk, k) * scale
        p = masked_softmax(s, key_idx[None, :] <= t[:, None])
        return jnp.einsum('bhqs,bshd->bqhd', p.astype(v.dtype), v)

    out = lax.map(block, jnp.arange(S // Q_BLOCK))
    return out.transpose(1, 0, 2, 3, 4).reshape(B, S, B_WIDTH)

def peer_ffn(x, w_q, sub_keys, expert_u, expert_v):
    B, S, D = x.shape
    T = B * S
    xt = x.reshape(T, D)
    q = _rms((xt @ w_q).reshape(T, P_HEADS, P_KEY_DIM)).astype(x.dtype)
    half = P_KEY_DIM // 2
    s1 = jnp.einsum('thd,hnd->thn', q[..., :half], sub_keys[:, 0]).astype(jnp.float32)
    s2 = jnp.einsum('thd,hnd->thn', q[..., half:], sub_keys[:, 1]).astype(jnp.float32)
    v1, i1 = lax.top_k(s1, P_TOPK)
    v2, i2 = lax.top_k(s2, P_TOPK)
    cand = (v1[..., :, None] + v2[..., None, :]).reshape(T, P_HEADS, P_TOPK * P_TOPK)
    vals, ci = lax.top_k(cand, P_TOPK)
    e = (jnp.take_along_axis(i1, ci // P_TOPK, axis=-1) * N_KEYS
         + jnp.take_along_axis(i2, ci % P_TOPK, axis=-1))
    g = jax.nn.softmax(vals, axis=-1)
    n_chunks = T // P_CHUNK

    def chunk(args):
        xc, ec, gc = args
        a = jnp.einsum('cd,ckd->ck', xc, expert_u[ec])
        w = (gc * jax.nn.gelu(a.astype(jnp.float32))).astype(x.dtype)
        return jnp.einsum('ck,ckd->cd', w, expert_v[ec])

    y = lax.map(chunk, (xt.reshape(n_chunks, P_CHUNK, D),
                        e.reshape(n_chunks, P_CHUNK, P_HEADS * P_TOPK),
                        g.reshape(n_chunks, P_CHUNK, P_HEADS * P_TOPK)))
    return y.reshape(B, S, D)

def hybrid_layer(x, positions, norm1_gain, w_in,
                 nsa_q_gain, nsa_kc_gain, nsa_ks_gain, nsa_kw_gain,
                 cmp_pos, cmp_k_w1, cmp_k_w2, cmp_v_w1, cmp_v_w2,
                 mla_q_lora_gain, mla_w_uq, mla_kv_lora_gain, mla_w_ukv, mla_q_gain, mla_k_gain,
                 out_gain_a, out_gain_b, w_out,
                 norm2_gain, peer_w_q, peer_sub_keys, peer_u, peer_v):
    B, S, _ = x.shape
    proj = rmsnorm(x, norm1_gain) @ w_in
    pts = [int(p) for p in np.cumsum(IN_SIZES)[:-1]]
    (a_q, a_kc, a_vc, a_ks, a_vs, a_kw, a_vw, a_gate, b_cq, b_ckv, b_kr) = jnp.split(proj, pts, axis=-1)
    kvs = lambda t: t.reshape(B, S, A_KV_HEADS, A_HEAD_DIM)
    gates = jax.nn.sigmoid(a_gate).reshape(B, S, A_HEADS, 3)
    o_a = nsa_mixer(a_q.reshape(B, S, A_HEADS, A_HEAD_DIM), kvs(a_kc), kvs(a_vc), kvs(a_ks), kvs(a_vs),
                    kvs(a_kw), kvs(a_vw), gates, positions,
                    nsa_q_gain, nsa_kc_gain, nsa_ks_gain, nsa_kw_gain,
                    cmp_pos, cmp_k_w1, cmp_k_w2, cmp_v_w1, cmp_v_w2)
    o_b = mla_mixer(b_cq, b_ckv, b_kr, positions, mla_q_lora_gain, mla_w_uq,
                    mla_kv_lora_gain, mla_w_ukv, mla_q_gain, mla_k_gain)
    mixed = jnp.concatenate([rmsnorm(o_a, out_gain_a), rmsnorm(o_b, out_gain_b)], axis=-1) @ w_out
    h = x + mixed
    return h + peer_ffn(rmsnorm(h, norm2_gain), peer_w_q, peer_sub_keys, peer_u, peer_v)

def second_inputs(seed: int = 0) -> dict:
    key = jax.random.key(seed)
    ks = jax.random.split(key, 32)
    L = DEPTH_2
    nrm = lambda k, shape, s: jax.random.normal(k, shape, jnp.float32) * s
    gain = lambda k, n: 1.0 + 0.02 * jax.random.normal(k, (L, n), jnp.float32)
    start = jax.random.randint(ks[1], (BATCH, 1), 0, 4096, dtype=jnp.int32)
    return {
        'x': nrm(ks[0], (BATCH, SEQ, D_MODEL), 1.0),
        'positions': (start + jnp.arange(SEQ, dtype=jnp.int32)[None, :]).astype(jnp.int32),
        'norm1_gain': gain(ks[2], D_MODEL),
        'w_in': nrm(ks[3], (L, D_MODEL, IN_WIDTH), D_MODEL ** -0.5),
        'nsa_q_gain': gain(ks[4], A_HEAD_DIM),
        'nsa_kc_gain': gain(ks[5], A_HEAD_DIM),
        'nsa_ks_gain': gain(ks[6], A_HEAD_DIM),
        'nsa_kw_gain': gain(ks[7], A_HEAD_DIM),
        'cmp_pos': nrm(ks[8], (L, CMP_LEN, A_HEAD_DIM), 0.1),
        'cmp_k_w1': nrm(ks[9], (L, CMP_LEN * A_HEAD_DIM, CMP_HIDDEN), (CMP_LEN * A_HEAD_DIM) ** -0.5),
        'cmp_k_w2': nrm(ks[10], (L, CMP_HIDDEN, A_HEAD_DIM), CMP_HIDDEN ** -0.5),
        'cmp_v_w1': nrm(ks[11], (L, CMP_LEN * A_HEAD_DIM, CMP_HIDDEN), (CMP_LEN * A_HEAD_DIM) ** -0.5),
        'cmp_v_w2': nrm(ks[12], (L, CMP_HIDDEN, A_HEAD_DIM), CMP_HIDDEN ** -0.5),
        'mla_q_lora_gain': gain(ks[13], Q_LORA),
        'mla_w_uq': nrm(ks[14], (L, Q_LORA, B_HEADS * B_QK), Q_LORA ** -0.5),
        'mla_kv_lora_gain': gain(ks[15], KV_LORA),
        'mla_w_ukv': nrm(ks[16], (L, KV_LORA, B_HEADS * (B_NOPE + B_V)), KV_LORA ** -0.5),
        'mla_q_gain': gain(ks[17], B_QK),
        'mla_k_gain': gain(ks[18], B_QK),
        'out_gain_a': gain(ks[19], A_WIDTH),
        'out_gain_b': gain(ks[20], B_WIDTH),
        'w_out': nrm(ks[21], (L, MIX_WIDTH, D_MODEL), MIX_WIDTH ** -0.5),
        'norm2_gain': gain(ks[22], D_MODEL),
        'peer_w_q': nrm(ks[23], (L, D_MODEL, P_HEADS * P_KEY_DIM), D_MODEL ** -0.5),
        'peer_sub_keys': nrm(ks[24], (L, P_HEADS, 2, N_KEYS, P_KEY_DIM // 2), (P_KEY_DIM // 2) ** -0.5),
        'peer_u': nrm(ks[25], (L, N_EXPERTS, D_MODEL), D_MODEL ** -0.5),
        'peer_v': nrm(ks[26], (L, N_EXPERTS, D_MODEL), D_MODEL ** -0.5),
    }

def second_block(x, positions, norm1_gain, w_in,
              nsa_q_gain, nsa_kc_gain, nsa_ks_gain, nsa_kw_gain,
              cmp_pos, cmp_k_w1, cmp_k_w2, cmp_v_w1, cmp_v_w2,
              mla_q_lora_gain, mla_w_uq, mla_kv_lora_gain, mla_w_ukv, mla_q_gain, mla_k_gain,
              out_gain_a, out_gain_b, w_out,
              norm2_gain, peer_w_q, peer_sub_keys, peer_u, peer_v):
    h = x
    for l in range(DEPTH_2):
        h = hybrid_layer(h, positions, norm1_gain[l], w_in[l],
                         nsa_q_gain[l], nsa_kc_gain[l], nsa_ks_gain[l], nsa_kw_gain[l],
                         cmp_pos[l], cmp_k_w1[l], cmp_k_w2[l], cmp_v_w1[l], cmp_v_w2[l],
                         mla_q_lora_gain[l], mla_w_uq[l], mla_kv_lora_gain[l], mla_w_ukv[l],
                         mla_q_gain[l], mla_k_gain[l],
                         out_gain_a[l], out_gain_b[l], w_out[l],
                         norm2_gain[l], peer_w_q[l], peer_sub_keys[l], peer_u[l], peer_v[l])
    return h


def setup_inputs(seed=0):
    out = dict(first_inputs(seed))
    for name, value in second_inputs(seed + 1).items():
        if name != "x":
            out[name + "_2"] = value
    return out


def reference(
    x, w_in_a, lam_a, subln_a, w_out_a, w_kv_shared, w_q_b, w_out_b, rel_bias, ln1_g, ln1_b,
    ln2_g, ln2_b, w_up, w_down, positions_2, norm1_gain_2, w_in_2, nsa_q_gain_2, nsa_kc_gain_2,
    nsa_ks_gain_2, nsa_kw_gain_2, cmp_pos_2, cmp_k_w1_2, cmp_k_w2_2, cmp_v_w1_2, cmp_v_w2_2,
    mla_q_lora_gain_2, mla_w_uq_2, mla_kv_lora_gain_2, mla_w_ukv_2, mla_q_gain_2, mla_k_gain_2,
    out_gain_a_2, out_gain_b_2, w_out_2, norm2_gain_2, peer_w_q_2, peer_sub_keys_2, peer_u_2,
    peer_v_2,
):
    x = first_block(
        x, w_in_a, lam_a, subln_a, w_out_a, w_kv_shared, w_q_b, w_out_b, rel_bias, ln1_g, ln1_b,
        ln2_g, ln2_b, w_up, w_down,
    )
    return second_block(
        x, positions_2, norm1_gain_2, w_in_2, nsa_q_gain_2, nsa_kc_gain_2, nsa_ks_gain_2,
        nsa_kw_gain_2, cmp_pos_2, cmp_k_w1_2, cmp_k_w2_2, cmp_v_w1_2, cmp_v_w2_2,
        mla_q_lora_gain_2, mla_w_uq_2, mla_kv_lora_gain_2, mla_w_ukv_2, mla_q_gain_2,
        mla_k_gain_2, out_gain_a_2, out_gain_b_2, w_out_2, norm2_gain_2, peer_w_q_2,
        peer_sub_keys_2, peer_u_2, peer_v_2,
    )


_drawn_inputs = setup_inputs


def setup_inputs(seed=0):
    import zlib

    import numpy as np

    out = dict(_drawn_inputs(seed))
    spreads = {}
    factors = {'lam_a': 8.0,
     'subln_a': 8.0,
     'norm1_gain_2': 3.508,
     'nsa_q_gain_2': 8.0,
     'nsa_kc_gain_2': 8.0,
     'nsa_ks_gain_2': 8.0,
     'nsa_kw_gain_2': 8.0,
     'mla_q_lora_gain_2': 8.0,
     'mla_kv_lora_gain_2': 6.851,
     'mla_q_gain_2': 8.0,
     'mla_k_gain_2': 8.0,
     'out_gain_a_2': 5.706,
     'out_gain_b_2': 5.029,
     'norm2_gain_2': 8.0,
     'peer_w_q_2': 5.319,
     'peer_sub_keys_2': 5.234,
     'peer_u_2': 5.833,
     'peer_v_2': 5.228}
    for name, (base, spread) in spreads.items():
        noise = np.random.default_rng([zlib.crc32(name.encode()), seed]).standard_normal(out[name].shape)
        drawn = base * np.exp(spread * noise) if base else spread * noise
        out[name] = __import__('jax').numpy.asarray(drawn.astype(out[name].dtype))
    for name, factor in factors.items():
        out[name] = (out[name] * factor).astype(out[name].dtype)
    return out
```

```python
from contextlib import ExitStack, contextmanager
import math

import numpy as np

import concourse.bass as bass
from concourse import mybir

F32 = mybir.dt.float32
U32 = mybir.dt.uint32
I32 = mybir.dt.int32
ALU = mybir.AluOpType
ACT = mybir.ActivationFunctionType
X = mybir.AxisListType.X

P = 128
D = 1024
S = 256
NT = S // P
NB = D // P
HALF = 512
HEADS = 16
HD = 64
DFF = 4 * D
N_CHUNK = DFF // 256
ALPHA = 4 ** 0.25
LN_EPS = 1e-5
EPS = 1e-6
LAM_INIT = 0.8 - 0.6 * math.exp(-0.3 * 0)
BIG = 1e30

N_SMALL = 20
C_Q, C_KC, C_VC, C_KS, C_VS, C_KW, C_VW, C_GATE, C_CQ, C_CKV, C_KR, C_END = np.cumsum(
    [0, 512, 128, 128, 128, 128, 128, 128, 24, 256, 128, 32]).tolist()
N_CMP = 15
MLA_HEADS = 8
QK = 96

P_HEADS = 8
TOPK = 16
N_KEYS = 128
RING = 8
N_UNITS = P_HEADS * NT
CHOOSE_STEPS = 49
PEER_SLOT = 2


def bucket_table():
    rel = 255 - np.arange(384)
    n = np.maximum(rel, 0)
    nf = np.maximum(n, 16).astype(np.float32)
    large = np.minimum(16 + (np.log(nf / 16) / math.log(8) * 16).astype(np.int32), 31)
    bucket = np.where(n < 16, n, large)
    table = np.zeros((33, 384), np.float32)
    table[bucket[rel >= 0], np.flatnonzero(rel >= 0)] = 1.0
    table[32, rel < 0] = 1.0
    return table


def rope_frequencies():
    return np.concatenate([
        (500000.0 ** (-np.arange(0, dim, 2) / dim)).astype(np.float32) for dim in (16, 32)])


def shape_constants():
    t = np.arange(S)
    causal = np.where(t[None, :] > t[:, None], BIG, 0.0)
    causal = np.concatenate([causal[:P, :P], causal[P:, :]], axis=1)
    end = 16 * np.arange(N_CMP) + 31
    seen = end[None, :] <= t[:, None]
    cmp_mask = np.full((P, 2, NT, 2, N_CMP), BIG)
    for g in range(2):
        for tile in range(NT):
            cmp_mask[:, g, tile, g, :] = np.where(seen[tile * P:(tile + 1) * P], 0.0, BIG)
    row_seen = seen.any(axis=1).reshape(NT, P).T
    count = np.broadcast_to(np.arange(TOPK), (P, TOPK))
    return np.concatenate([np.eye(P), causal, cmp_mask.reshape(P, -1), row_seen, count],
                          axis=1).astype(np.float32)


CO_ID, CO_CAUSAL, CO_CMP, CO_SEEN, CO_COUNT, CO_END = np.cumsum(
    [0, P, 384, 2 * NT * 2 * N_CMP, NT, TOPK]).tolist()


class Count:

    def __init__(self, engine):
        self.engine = engine
        self.seen, self.trip, self.per = {}, None, {}

    def skip(self, name, n=1):
        self.seen[name] = self.seen.get(name, 0) + n

    def take(self, name, n=1):
        self.skip(name, n)
        return self.seen[name] if self.trip is None else self.trip * self.per[name] + self.seen[name]

    @contextmanager
    def loop(self, trips, **per):
        before = dict(self.seen)
        with self.engine.Fori(0, trips) as i:
            self.trip, self.per = i, per
            yield i
            self.trip = None
        for name in self.seen:
            taken = self.seen[name] - before.get(name, 0)
            assert taken == per.get(name, 0), (name, taken)
            self.seen[name] += taken * (trips - 1)


def spread(ap, *dims):
    return bass.AP(ap.tensor, ap.offset, [list(ap.ap[0])] + [list(d) for d in dims])


def to_partitions(row, n=P):
    return bass.AP(row.tensor, row.offset, [[0, n]] + [list(d) for d in row.ap])


def build(nc, T, out):
    with ExitStack() as ctx:
        sems = {}

        def sem(name):
            if name not in sems:
                sems[name] = ctx.enter_context(nc.semaphore(name))
            return sems[name]

        def sb(name, shape, dt=F32):
            return ctx.enter_context(nc.sbuf_tensor(name, shape, dt))

        const = sb("const", [P, CO_END])
        ident = const[:, CO_ID:CO_CAUSAL]
        causal = const[:, CO_CAUSAL:CO_CMP]
        cmp_mask = const[:, CO_CMP:CO_SEEN]
        row_seen = const[:, CO_SEEN:CO_COUNT]
        counter = const[:, CO_COUNT:CO_END]
        h = sb("h", [P, NT, D])
        nat = sb("nat", [P, NT, D])
        hT = sb("hT", [P, NB, S])
        val = sb("val", [P, NT, D])
        ring = sb("ring", [P, 4, 2048])
        qkring = sb("qkring", [P, 2, 2048])
        qkT = sb("qkT", [P, 2, 2, S])
        act = sb("act", [P, 2, HALF])
        relu = sb("relu", [P, 2, HALF])
        sco = sb("sco", [P, 2, 2, 384])
        prob = sb("prob", [P, 2, 2, 384])
        probT = sb("probT", [P, 2, 384])
        peak = sb("peak", [P, 2, 2, NT])
        total = sb("total", [P, 2, 2, NT])
        share = sb("share", [P, 2, 2, NT])
        omap = sb("omap", [P, NT, P])
        arena_u = sb("arena_u", [P, RING, D])
        ln_gb = arena_u[:, :, :].rearrange("p (s g) d -> p s g d", g=2)
        arena_v = sb("arena_v", [P, RING, D])
        av = arena_v[:, :, :].rearrange("p r d -> p (r d)")
        bias = av[:, 0:HEADS * 384].rearrange("p (m k) -> p m k", m=HEADS)
        tmp = av[:, HEADS * 384:HEADS * 384 + 2048].rearrange("p (t d) -> p t d", t=NT)
        bucket_sb = tmp[0:33, 0, 0:384]
        relb_sb = tmp[0:33, 0, 384:400]
        bias_rows = tmp[0:HEADS, 0, 512:896]
        small = sb("small", [P, 1952])
        small_at = [0]

        def piece(n):
            small_at[0] += n
            return small[:, small_at[0] - n:small_at[0]]

        lam_in, lam_prod = tmp[:, 1, 0:256], tmp[:, 1, 256:320]
        lam_sum, lam_exp = piece(2), piece(3)
        stats, moments, var_eps, rstd = piece(24), piece(4), piece(2), piece(2)
        subln = piece(128)
        ms_in, ms_out = piece(24 * NT), piece(24 * NT)
        sq_sum = piece(24 * NT)
        neg_half = piece(24 * NT)
        wide_gain = sb("wide_gain", [P, 3, D])
        proj = sb("proj", [P, NT, C_END])
        pos_i = sb("pos_i", [P, 3], I32)
        pos_f, freqs = piece(3), piece(24)
        angle, trig = piece(72), piece(144)
        cos, sin = trig[:, 0:72], trig[:, 72:144]
        gain_q, gain_ks, gain_kw, gain_kc = piece(64), piece(64), piece(64), piece(64)
        gain_mq, gain_mk, gain_cq, gain_ckv = piece(QK), piece(QK), piece(256), piece(128)
        cmp_posT = piece(16)
        cmp_w2 = piece(256).rearrange("p (a b n) -> p a b n", a=2, b=2)
        gates = piece(24 * NT)
        c_peak, c_total, c_share = piece(16), piece(16), piece(16)
        sq = av[:, 0:2 * C_END].rearrange("p (t n) -> p t n", t=NT)
        flow_x0 = av[:, 3440:3952].rearrange("p (a r i) -> p a r i", a=2, r=2)
        flow_x = av[:, 3952:4464].rearrange("p (a g i) -> p a g i", a=2, g=2)
        blocks = av[:, 4464:5424].rearrange("p (a j n) -> p a j n", a=2, j=16)
        hidden = av[:, 5424:5544].rearrange("p (a b n) -> p a b n", a=2, b=2)
        kcv = av[0:30, 5544:5672]
        kc_twice = av[0:30, 5672:5800]
        kc_sq = av[0:30, 5800:5864]
        kcT = av[:, 5864:5894]
        c_sco = av[:, 5894:6374]
        c_prob = av[:, 6374:6854]
        lora = av[:, 6854:7622].rearrange("p (t n) -> p t n", t=NT)
        au = arena_u[:, :, :].rearrange("p r d -> p (r d)")
        c_probT = au[0:30, 0:2048]
        mq = au[:, 2048:3584].rearrange("p (t h n) -> p t h n", t=NT, n=QK)
        mk = au[:, 3584:5120].rearrange("p (t h n) -> p t h n", t=NT, n=QK)
        rope_tmp = au[:, 5120:6144].rearrange("p (k n) -> p k n", k=4)
        cycles, reduced = au[:, 6144:6288], au[:, 6288:6432]
        loraT = relu[:, :, :].rearrange("p a n -> p (a n)")[:, 0:768].rearrange("p (c s) -> p c s", c=3)
        mqT = qkring[0:QK, 0, :].rearrange("p (h s) -> p h s", s=S)
        mkT = qkring[0:QK, 1, :].rearrange("p (h s) -> p h s", s=S)

        ones, settled = piece(1), piece(1)
        keysT = qkring[:, 0, :]
        keys = qkring[:, 1, :].rearrange("p (b d) -> p b d", d=P)
        pq, pq_sq = act[:, 0, :], act[:, 1, :]
        zeros = omap[:, 0, :]
        flat_sco = sco[:, :, :, :].rearrange("p a b n -> p (a b n)")
        diag = flat_sco[:, 0:512].rearrange("p (s n) -> p s n", s=4)
        key_sco = flat_sco[:, 512:1024].rearrange("p (t n) -> p t n", t=NT)
        pairs = flat_sco[:, 1024:1280]
        pairs_left = flat_sco[:, 1280:1536]
        flat_prob = prob[:, :, :, :].rearrange("p a b n -> p (a b n)")
        key_left, match = flat_prob[:, 0:256], flat_prob[:, 256:512]
        pool_of = [flat_prob[:, 512:].rearrange("p n -> p n"), 0]

        def bit(n, dt=F32):
            at = pool_of[1]
            pool_of[1] += n
            part = pool_of[0][:, at:at + n]
            return part if dt is F32 else part.bitcast(dt)

        best, best_key, best_key_f = bit(32), bit(32, U32), bit(32)
        top, top_pair, place, place_f, picked = bit(16), bit(16, U32), bit(32, U32), bit(32), bit(32)
        neg_top, mass = bit(1), bit(2)
        expert_u, expert_v = bit(32, U32), bit(32, U32)
        gate_w, dots, gelu, weight = bit(32), bit(16), bit(16), bit(32)
        ps = [ctx.enter_context(nc.psum_tensor(f"ps{i}", [P, HALF], F32)) for i in range(8)]

        def rows(w, j, n=2):
            return w[j * n * P:(j + 1) * n * P, :].rearrange("(c p) n -> p c n", p=P)

        def cols(w, at, n=256):
            return w[:, at:at + n].rearrange("(c p) n -> p c n", p=P)

        def cols_dyn(w, at, n):
            return w.rearrange("(c p) n -> p c n", p=P)[:, :, bass.ds(at, n)]

        x_t = T["x"][0].rearrange("(t p) d -> p t d", p=P)
        scratch = nc.dram_tensor("bias_scratch", (HEADS, 384), F32, kind="Internal").ap()
        shifted = nc.dram_tensor("bias_shifted", (P * (HEADS * 384 + 1),), F32, kind="Internal").ap()
        w_in, w_out_a = T["w_in_a"][0], T["w_out_a"][0]
        w_kv, w_q, w_out_b = T["w_kv_shared"], T["w_q_b"][0], T["w_out_b"][0]

        block = ctx.enter_context(nc.Block())

        @block.sync
        def _(sp):
            count = Count(sp)
            turn = [0]
            used = {}

            def chunk(dst, *srcs):
                slot = turn[0] % 4
                turn[0] += 1
                load(ring, slot, f"ring{slot}", dst, *srcs)

            def load(where, slot, name, dst, *srcs):
                if used.get(name):
                    sp.wait_ge(sem(name + "_used"), count.take(name + "_used"))
                used[name] = True
                for n, src in enumerate(srcs):
                    sp.dma_start(dst(where[:, slot, :], n), src).then_inc(sem(name + "_landed"), 16)

            def as_blocks(n):
                return lambda s, i: s.rearrange("p (c n) -> p c n", n=n)

            def two_columns(s, i):
                return s[:, i * 1024:(i + 1) * 1024].rearrange("p (c n) -> p c n", n=P)

            def nat_chunks(w, at=0):
                for j in range(4):
                    chunk(as_blocks(D), rows(w[:, at:at + D], j))

            def qk_chunk(wq, wk, f):
                at = f * P
                name = f"qk{f % 2}" if isinstance(f, int) else None
                load(qkring, f % 2, name, two_columns, cols(wq, at, P), cols(wk, at, P))

            def qk_chunks(wq, wk):
                with count.loop(3, qk0_used=1, qk1_used=1) as i:
                    for b in range(2):
                        load(qkring, b, f"qk{b}", two_columns,
                             cols_dyn(wq, i * 256 + 256 + b * P, P), cols_dyn(wk, i * 256 + 256 + b * P, P))

            def mlp_chunks(layer):
                up, down = T["w_up"][layer], T["w_down"][layer]
                load(ring, 0, "ring0", as_blocks(256), cols(up, 0))
                load(ring, 2, "ring2", as_blocks(256), cols(up, 256))
                load(ring, 1, "ring1", as_blocks(D), rows(down, 0))
                with count.loop((N_CHUNK - 2) // 2, ring0_used=1, ring1_used=1, ring2_used=1, ring3_used=1) as i:
                    for b in range(2):
                        load(ring, 2 * b, f"ring{2 * b}", as_blocks(256), cols_dyn(up, i * 512 + (512 + 256 * b), 256))
                        load(ring, 3 - 2 * b, f"ring{3 - 2 * b}", as_blocks(D), down_rows(down, i * 2 + (1 + b)))
                load(ring, 3, "ring3", as_blocks(D), rows(down, N_CHUNK - 1))

            def down_rows(down, j):
                return down.rearrange("(j c p) n -> p j c n", p=P, c=2)[:, bass.ds(j, 1), :, :].rearrange(
                    "p j c n -> p (j c) n")

            for t in range(NT):
                sp.dma_start(h[:, t, :], x_t[:, t, :]).then_inc(sem("x_landed"), 16)
            sp.dma_start(const[:, :], T["const"]).then_inc(sem("const_landed"), 16)
            nat_chunks(w_in, 2 * D)
            qk_chunk(w_in, w_in[:, D:], 0)
            qk_chunk(w_in, w_in[:, D:], 1)
            nat_chunks(w_out_a)
            qk_chunks(w_in, w_in[:, D:])
            mlp_chunks(0)
            nat_chunks(w_kv, D)
            qk_chunk(w_q, w_kv, 0)
            qk_chunk(w_q, w_kv, 1)
            nat_chunks(w_out_b)
            qk_chunks(w_q, w_kv)
            mlp_chunks(1)
            for j in range(8):
                chunk(lambda s, i: s[:, 0:C_END], T["w_in_2"][0][j * P:(j + 1) * P, :])
            chunk(lambda s, i: s[:, 0:1536].rearrange("p (c n) -> p c n", c=2),
                  T["mla_w_uq_2"][0].rearrange("(c p) n -> p c n", p=P))
            chunk(lambda s, i: s[:, 0:D], T["mla_w_ukv_2"][0])
            for w1 in (T["cmp_k_w1_2"][0], T["cmp_v_w1_2"][0]):
                for j in range(2):
                    chunk(as_blocks(256), w1[j * D:(j + 1) * D, :].rearrange("(c p) n -> p c n", p=P))
            nat_chunks(T["w_out_2"][0])
            sp.wait_ge(sem("attention_done"), count.take("attention_done"))
            sp.dma_start(keys, T["peer_sub_keys_2"][0].rearrange("h t n d -> n (h t) d")).then_inc(sem("keys_landed"), 16)
            for j in range(P_HEADS):
                load(ring, PEER_SLOT, f"ring{PEER_SLOT}", as_blocks(256), cols(T["peer_w_q_2"][0], 256 * j))
            for t in range(NT):
                sp.wait_ge(sem("y_ready"), count.take("y_ready"))
                sp.dma_start(out[0, t * P:(t + 1) * P, :], h[:, t, :]).then_inc(sem("stored"), 16)
            sp.wait_ge(sem("stored"), count.take("stored", 32))

        @block.tensor
        def _(pe):
            count = Count(pe)
            turn = [0]

            def landed(name):
                pe.wait_ge(sem(name + "_landed"), count.take(name + "_landed", 32 if name.startswith("qk") else 16))

            def slot_of_turn():
                slot = turn[0] % 4
                turn[0] += 1
                landed(f"ring{slot}")
                return slot

            def turn_over(src, blocks=NB, ready=None):
                for t in range(NT):
                    if ready:
                        pe.wait_ge(sem(ready), count.take(ready))
                    for c in range(blocks):
                        last = pe.transpose(ps[4 + c // 2][:, (c % 2) * S + t * P:(c % 2) * S + t * P + P],
                                            src[:, t, c * P:(c + 1) * P], ident)
                        if t == NT - 1 and c % 2:
                            last.then_inc(sem("turned_v" if c < 4 else "turned_a"), 1)

            def hT_ready():
                pe.wait_ge(sem("hT_v"), count.take("hT_v", 2))
                pe.wait_ge(sem("hT_a"), count.take("hT_a", 2))

            def natural(ready=True):
                if ready:
                    hT_ready()
                for j in range(4):
                    slot = slot_of_turn()
                    w = ring[:, slot, :].rearrange("p (c n) -> p c n", c=2)
                    order = [(cc, k) for k in range(4) for cc in range(2)] if j == 3 else \
                            [(cc, k) for cc in range(2) for k in range(4)]
                    for cc, k in order:
                        c = 2 * j + cc
                        last = pe.matmul(ps[k][:, :], hT[:, c, (k // 2) * P:(k // 2) * P + P],
                                         w[:, cc, (k % 2) * HALF:(k % 2 + 1) * HALF],
                                         start=(c == 0), stop=(c == NB - 1))
                        if c == NB - 1:
                            last.then_inc(sem("acc_ready"), 1)
                    if j < 3:
                        last.then_inc(sem(f"ring{slot}_used"), 1)
                pe.wait_ge(sem("acc_ready"), count.take("acc_ready", 4))
                pe.sem_inc(sem(f"ring{slot}_used"), 1)

            def project(b, part):
                if part == 0:
                    landed(f"qk{b}")
                w = qkring[:, b, :].rearrange("p (q c n) -> p q c n", q=2, c=NB)
                for c in range(NB):
                    last = pe.matmul(ps[4 + part][:, 0:S], w[:, part, c, :], hT[:, c, :],
                                     start=(c == 0), stop=(c == NB - 1))
                last.then_inc(sem("proj_ready"), 1)
                if part == 1:
                    pe.wait_ge(sem("proj_ready"), count.take("proj_ready", 2))
                    pe.sem_inc(sem(f"qk{b}_used"), 1)

            def scores(q, k, banks, rows_of=lambda m: slice(64 * m, 64 * m + 64)):
                for m in range(2):
                    bank = ps[banks[m]]
                    pe.matmul(bank[:, 0:P], q(m)[:, 0:P], k(m)[:, 0:P], start=True, stop=True)
                    pe.matmul(bank[:, P:384], q(m)[:, P:S], k(m)[:, 0:S], start=True, stop=True)\
                        .then_inc(sem("scores_ready"), 1)

            def turn_probs(b):
                for m in range(2):
                    pe.wait_ge(sem("probs_ready"), count.take("probs_ready", 2))
                    for k in range(3):
                        last = pe.transpose(ps[2 + m][:, k * P:(k + 1) * P], prob[:, b, m, k * P:(k + 1) * P], ident)
                    last.then_inc(sem("probT_v_turned" if m == 0 else "probT_a_turned"), 1)

            def weigh(b, v, dv):
                for m in range(2):
                    pe.wait_ge(sem("probT_v" if m == 0 else "probT_a"), count.take("probT_v" if m == 0 else "probT_a"))
                    o = ps[6 + b]
                    at = 2 * m * dv
                    pe.matmul(o[:, at:at + dv], probT[:, m, 0:P], v(m, 0), start=True, stop=True)
                    pe.matmul(o[:, at + dv:at + 2 * dv], probT[:, m, P:2 * P], v(m, 0), start=True, stop=False)
                    last = pe.matmul(o[:, at + dv:at + 2 * dv], probT[:, m, 2 * P:3 * P], v(m, 1),
                                     start=False, stop=True)
                last.then_inc(sem("weighed"), 1)

            def attend_block(f, b, dv, more=True):
                pe.wait_ge(sem("qkT_ready"), count.take("qkT_ready", 2))
                scores(lambda m: qkT[64 * m:64 * m + 64, b, 0, :], lambda m: qkT[64 * m:64 * m + 64, b, 1, :], (0, 1))
                if more:
                    project(1 - b, 0)
                turn_probs(b)
                if more:
                    project(1 - b, 1)
                weigh(b, lambda m, t: val[:, t, bass.ds(f * P + (m * 64 if dv == 64 else 0), dv)], dv)

            def attention_layer(dv):
                natural()
                project(0, 0)
                project(0, 1)
                pe.wait_ge(sem("val_v"), count.take("val_v", 2))
                pe.wait_ge(sem("val_a"), count.take("val_a", 2))
                with count.loop(3, qk0_landed=32, qk1_landed=32, qkT_ready=4, proj_ready=4, probs_ready=8,
                            probT_v=2, probT_a=2) as i:
                    for b in range(2):
                        attend_block(i * 2 + b, b, dv)
                attend_block(6, 0, dv)
                attend_block(7, 1, dv, more=False)

            def up(b):
                landed(f"ring{2 * b}")
                w = ring[:, 2 * b, :].rearrange("p (c n) -> p c n", n=256)
                for fb in range(2):
                    for c in range(NB):
                        last = pe.matmul(ps[4 + b][:, fb * S:(fb + 1) * S], w[:, c, fb * P:(fb + 1) * P], hT[:, c, :],
                                         start=(c == 0), stop=(c == NB - 1))
                last.then_inc(sem("up_ready"), 1)
                pe.wait_ge(sem("up_ready"), count.take("up_ready"))
                pe.sem_inc(sem(f"ring{2 * b}_used"), 1)

            def down(b, first=False, final=False):
                pe.wait_ge(sem("act_ready"), count.take("act_ready"))
                landed(f"ring{2 * b + 1}")
                w = ring[:, 2 * b + 1, :].rearrange("p (c n) -> p c n", c=2)
                order = [(fb, k) for k in range(4) for fb in range(2)] if final else \
                        [(fb, k) for fb in range(2) for k in range(4)]
                for fb, k in order:
                    last = pe.matmul(ps[k][:, :], act[:, b, fb * S + (k // 2) * P:fb * S + (k // 2) * P + P],
                                     w[:, fb, (k % 2) * HALF:(k % 2 + 1) * HALF],
                                     start=(first and fb == 0), stop=(final and fb == 1), skip_group_check=True)
                    if final and fb == 1:
                        last.then_inc(sem("acc_ready"), 1)
                if final:
                    pe.wait_ge(sem("acc_ready"), count.take("acc_ready", 4))
                    pe.sem_inc(sem(f"ring{2 * b + 1}_used"), 1)
                else:
                    last.then_inc(sem(f"ring{2 * b + 1}_used"), 1)

            def mlp():
                hT_ready()
                up(0)
                up(1)
                down(0, first=True)
                with count.loop((N_CHUNK - 2) // 2, ring0_landed=16, ring1_landed=16, ring2_landed=16, ring3_landed=16,
                            up_ready=2, act_ready=2):
                    up(0)
                    down(1)
                    up(1)
                    down(0)
                down(1, final=True)

            def key_scores(j, more=True):
                landed(f"ring{PEER_SLOT}")
                w = ring[:, PEER_SLOT, :].rearrange("p (c n) -> p c n", n=256)
                for half in range(2):
                    for c in range(NB):
                        last = pe.matmul(ps[4 + half][:, 0:S], w[:, c, half * P:(half + 1) * P], hT[:, c, :],
                                         start=(c == 0), stop=(c == NB - 1))
                    last.then_inc(sem("peer_q_done"), 1)
                pe.wait_ge(sem("pq_ready"), count.take("pq_ready", 4))
                pe.sem_inc(sem(f"ring{PEER_SLOT}_used"), 1)
                for t in range(NT):
                    for half in range(2):
                        last = pe.matmul(ps[7][:, t:t + 1], pq_sq[:, half * S + t * P:half * S + t * P + P], ones,
                                         start=(half == 0), stop=(half == 1))
                last.then_inc(sem("peer_sq_done"), 1)
                for t in range(NT):
                    for half in range(2):
                        last = pe.matmul(ps[6][:, (2 * t + half) * P:(2 * t + half + 1) * P],
                                         pq[:, half * S + t * P:half * S + t * P + P],
                                         keysT[:, bass.ds(j * (2 * P) + half * P, P)], start=True, stop=True)
                last.then_inc(sem("key_scores_done"), 1)

            def add_experts(t, ks, final=False):
                for k in ks:
                    pe.wait_ge(sem(f"v{k % RING}_landed"), count.take(f"v{k % RING}_landed", 16))
                    pe.wait_ge(sem("diag_ready"), count.take("diag_ready"))
                    for n in range(2):
                        last = pe.matmul(ps[2 * t + n][:, :], diag[:, k % 4, :], arena_v[:, k % RING, n * HALF:(n + 1) * HALF],
                                         start=False, stop=(final and k == TOPK - 1), skip_group_check=True)
                    last.then_inc(sem("v_used"), 1)

            def unit(t, head=None):
                add_experts(1 - t, range(8))
                if head is not None:
                    pe.wait_ge(sem("key_scores_taken"), count.take("key_scores_taken"))
                    key_scores(head)
                add_experts(1 - t, range(8, TOPK))

            def peer():
                hT_ready()
                pe.wait_ge(sem("peer_set"), count.take("peer_set"))
                for k in range(4):
                    pe.matmul(ps[k][:, :], zeros, hT[:, 0:2, :].rearrange("p c s -> p (c s)"), start=True, stop=False,
                              skip_group_check=True)
                key_scores(0)
                pe.wait_ge(sem("key_scores_taken"), count.take("key_scores_taken"))
                key_scores(1)
                per = {f"v{k}_landed": 64 for k in range(RING)}
                with count.loop(P_HEADS - 2, diag_ready=32, key_scores_taken=1, pq_ready=4, ring2_landed=16, **per) as i:
                    unit(1)
                    unit(0, i + 2)
                unit(1)
                unit(0)
                unit(1)
                add_experts(1, range(TOPK), final=True)

            def nsa_unit(branch, f):
                g = f // 2
                at = (C_VS, C_VW)[branch] + g * HD
                return (lambda m: hT[64 * m:64 * m + 64, f, :], lambda m: hT[64 * m:64 * m + 64, 4 + 2 * branch + g, :],
                        lambda m, t: proj[:, t, at:at + HD])

            def mla_unit(f):
                return (lambda m: mqT[:, 2 * f + m, :], lambda m: mkT[:, 2 * f + m, :],
                        lambda m, t: val[:, t, (2 * f + m) * HD:(2 * f + m + 1) * HD])

            def hybrid_attention():
                hT_ready()
                for c in range(NB):
                    slot = slot_of_turn()
                    for k in range(8):
                        a = (k % 4) * HALF
                        z = min(a + HALF, C_END)
                        last = pe.matmul(ps[k][:, 0:z - a], hT[:, c, (k // 4) * P:(k // 4) * P + P],
                                         ring[:, slot, a:z], start=(c == 0), stop=(c == NB - 1))
                        if c == NB - 1:
                            last.then_inc(sem("proj_v_done" if k < 4 else "proj_a_done"), 1)
                    if c < NB - 1:
                        last.then_inc(sem(f"ring{slot}_used"), 1)
                pe.wait_ge(sem("proj_a_done"), count.take("proj_a_done", 4))
                pe.sem_inc(sem(f"ring{slot}_used"), 1)
                pe.wait_ge(sem("proj_v"), count.take("proj_v", 4))
                pe.wait_ge(sem("proj_a"), count.take("proj_a", 4))
                for a in range(2):
                    for t in range(NT):
                        last = pe.transpose(ps[0][:, a * S + t * P:a * S + t * P + P],
                                            proj[:, t, C_KC + a * P:C_KC + a * P + P], ident)
                last.then_inc(sem("flow_turned"), 1)
                pe.wait_ge(sem("lora_ready"), count.take("lora_ready"))
                for c in range(3):
                    for t in range(NT):
                        last = pe.transpose(ps[1 + c // 2][:, (c % 2) * S + t * P:(c % 2) * S + t * P + P],
                                            lora[:, t, c * P:(c + 1) * P], ident)
                    if c:
                        last.then_inc(sem("lora_turned"), 1)
                pe.wait_ge(sem("loraT_ready"), count.take("loraT_ready", 2))
                slot = slot_of_turn()
                for t in range(NT):
                    for n, (a, z) in enumerate(((0, HALF), (HALF, 768))):
                        for c in range(2):
                            last = pe.matmul(ps[4 + 2 * t + n][:, 0:z - a], loraT[:, c, t * P:(t + 1) * P],
                                             ring[:, slot, c * 768 + a:c * 768 + z], start=(c == 0), stop=(c == 1))
                    last.then_inc(sem("mq_v_done" if t == 0 else "mq_a_done"), 1)
                pe.wait_ge(sem("mq_a_done"), count.take("mq_a_done"))
                pe.sem_inc(sem(f"ring{slot}_used"), 1)
                slot = slot_of_turn()
                pe.wait_ge(sem("flow_x0_ready"), count.take("flow_x0_ready"))
                for t in range(NT):
                    for n in range(2):
                        last = pe.matmul(ps[2 * t + n][:, :], loraT[:, 2, t * P:(t + 1) * P],
                                         ring[:, slot, n * HALF:(n + 1) * HALF], start=True, stop=True)
                    last.then_inc(sem("mkv_v_done" if t == 0 else "mkv_a_done"), 1)
                pe.wait_ge(sem("mkv_a_done"), count.take("mkv_a_done"))
                pe.sem_inc(sem(f"ring{slot}_used"), 1)
                pe.wait_ge(sem("mq_v"), count.take("mq_v"))
                pe.wait_ge(sem("mq_a"), count.take("mq_a"))
                turn_over(nat, ready="nat_ready")
                pe.wait_ge(sem("mkv_v"), count.take("mkv_v"))
                pe.wait_ge(sem("mkv_a"), count.take("mkv_a"))
                pe.wait_ge(sem("blocks_ready"), count.take("blocks_ready", 4))
                for a in range(2):
                    slots = (slot_of_turn(), slot_of_turn())
                    for b in range(2):
                        for j in range(16):
                            w = ring[:, slots[j // 8], :].rearrange("p (c n) -> p c n", c=8)[:, j % 8, :]
                            last = pe.matmul(ps[0][:, (2 * a + b) * 30:(2 * a + b + 1) * 30], w[:, b * P:(b + 1) * P],
                                             blocks[:, a, j, :], start=(j == 0), stop=(j == 15))
                    last.then_inc(sem("hidden_done"), 1)
                    pe.wait_ge(sem("hidden_done"), count.take("hidden_done"))
                    for slot in slots:
                        pe.sem_inc(sem(f"ring{slot}_used"), 1)
                pe.wait_ge(sem("hidden_ready"), count.take("hidden_ready"))
                for a in range(2):
                    for b in range(2):
                        last = pe.matmul(ps[1][0:30, a * HD:(a + 1) * HD], hidden[:, a, b, :], cmp_w2[:, a, b, :],
                                         start=(b == 0), stop=(b == 1))
                last.then_inc(sem("kcv_done"), 1)
                pe.wait_ge(sem("kc_ready"), count.take("kc_ready"))
                pe.transpose(ps[2][:, 0:30], kc_twice, ident[0:30, 0:30]).then_inc(sem("kc_turned"), 1)
                hT_ready()
                pe.wait_ge(sem("kcT_ready"), count.take("kcT_ready"))
                for half in range(2):
                    at = slice(64 * half, 64 * half + 64)
                    for n in range(4 * NT):
                        last = pe.matmul(ps[2 + half][:, n * 30:(n + 1) * 30],
                                         hT[at, n // NT, (n % NT) * P:(n % NT + 1) * P], kcT[at, :],
                                         start=True, stop=True)
                last.then_inc(sem("c_scores_done"), 1)
                pe.wait_ge(sem("c_prob_ready"), count.take("c_prob_ready"))
                for n in range(8 * NT):
                    last = pe.transpose(ps[4 + n // 4][0:30, (n % 4) * P:(n % 4 + 1) * P],
                                        c_prob[:, n * 30:(n + 1) * 30], ident)
                    if n % 4 == 3:
                        last.then_inc(sem("c_turned_v" if n < 8 else "c_turned_a"), 1)
                pe.wait_ge(sem("c_probT_v"), count.take("c_probT_v", 2))
                pe.wait_ge(sem("c_probT_a"), count.take("c_probT_a", 2))
                for n in range(8 * NT):
                    last = pe.matmul(ps[n // 8][:, (n % 8) * HD:(n % 8 + 1) * HD], c_probT[:, n * P:(n + 1) * P],
                                     kcv[:, HD:2 * HD], start=True, stop=True)
                    if n % 8 == 7:
                        last.then_inc(sem("c_weighed"), 1)
                pe.wait_ge(sem("mqk_ready"), count.take("mqk_ready", 2))
                for n, bank in enumerate((2, 3, 4, 5, 6, 7, 0, 1)):
                    if bank == 0:
                        pe.wait_ge(sem("c_out"), count.take("c_out", 2))
                    src = (mq, mk)[n // 4]
                    for head in range(2):
                        for t in range(NT):
                            last = pe.transpose(ps[bank][0:QK, head * S + t * P:head * S + t * P + P],
                                                src[:, t, 2 * (n % 4) + head, :], ident)
                    last.then_inc(sem("m_turned_v" if n % 2 == 0 else "m_turned_a"), 1)
                pe.wait_ge(sem("mT_v"), count.take("mT_v", 4))
                pe.wait_ge(sem("mT_a"), count.take("mT_a", 4))
                units = [nsa_unit(branch, f) for branch in range(2) for f in range(4)] + [mla_unit(f) for f in range(4)]
                for u in range(len(units) + 1):
                    if u < len(units):
                        scores(units[u][0], units[u][1], ((0, 1), (4, 5))[u % 2])
                    if u:
                        turn_probs((u - 1) % 2)
                        weigh((u - 1) % 2, units[u - 1][2], HD)

            pe.wait_ge(sem("const_landed"), count.take("const_landed", 16))
            pe.wait_ge(sem("x_landed"), count.take("x_landed", 32))
            pe.wait_ge(sem("bias_in_landed"), count.take("bias_in_landed", 32))
            pe.wait_ge(sem("relb_set"), count.take("relb_set"))
            pe.matmul(ps[0][0:HEADS, 0:384], relb_sb, bucket_sb, start=True, stop=True).then_inc(sem("bias_rows_ready"), 1)
            turn_over(h)
            attention_layer(P)
            turn_over(nat, ready="nat_ready")
            natural()
            turn_over(h, ready="h_ready")
            mlp()
            turn_over(h, ready="h_ready")
            attention_layer(HD)
            turn_over(nat, ready="nat_ready")
            natural()
            turn_over(h, ready="h_ready")
            mlp()
            turn_over(nat, ready="nat_ready")
            hybrid_attention()
            turn_over(nat, ready="nat_ready")
            natural()
            pe.wait_ge(sem("keys_landed"), count.take("keys_landed", 16))
            for b in range(2 * P_HEADS):
                last = pe.transpose(ps[4 + b // 4][:, (b % 4) * P:(b % 4 + 1) * P], keys[:, b, :], ident)
                if b % 4 == 3:
                    last.then_inc(sem("keys_turned"), 1)
            pe.wait_ge(sem("keysT_ready"), count.take("keysT_ready", 4))
            turn_over(nat, ready="nat_ready")
            peer()

        @block.scalar
        def _(sc):
            count = Count(sc)

            def take_turned():
                for c in range(2, 4):
                    sc.wait_ge(sem("turned_a"), count.take("turned_a"))
                    sc.activation(hT[:, 2 * c:2 * c + 2, :], ps[4 + c][:, :].rearrange("p (c s) -> p c s", c=2), ACT.Copy)\
                        .then_inc(sem("hT_a"), 1)

            def exps(b):
                for m in range(2):
                    for t, (a, z) in enumerate(((0, P), (P, 384))):
                        sc.wait_ge(sem("sco_ready"), count.take("sco_ready"))
                        sc.activation(prob[:, b, m, a:z], sco[:, b, m, a:z], ACT.Exp, bias=peak[:, b, m, t:t + 1],
                                      scale=-1.0, accum_out=total[:, b, m, t:t + 1]).then_inc(sem("probs_ready"), 1)

            def take_probT():
                sc.wait_ge(sem("probT_a_turned"), count.take("probT_a_turned"))
                sc.activation(probT[:, 1, :], ps[3][:, 0:384], ACT.Copy).then_inc(sem("probT_a"), 1)

            def take_projection(b, part):
                sc.wait_ge(sem("proj_ready"), count.take("proj_ready"))
                sc.activation(qkT[:, b, part, :], ps[4 + part][:, 0:S], ACT.Copy,
                              scale=-(HD ** -0.5) if part == 0 else 1.0).then_inc(sem("qkT_ready"), 1)

            def attend_block(b, more=True):
                exps(b)
                if more:
                    take_projection(1 - b, 0)
                take_probT()
                if more:
                    take_projection(1 - b, 1)

            def attention_layer():
                count.skip("acc_ready", 2)
                for k in range(2):
                    sc.wait_ge(sem("acc_ready"), count.take("acc_ready"))
                    sc.activation(val[:, 1, k * HALF:(k + 1) * HALF], ps[2 + k][:, :], ACT.Copy).then_inc(sem("val_a"), 1)
                take_projection(0, 0)
                take_projection(0, 1)
                with count.loop(3, sco_ready=8, proj_ready=4, probT_a_turned=2):
                    attend_block(0)
                    attend_block(1)
                attend_block(0)
                attend_block(1, more=False)

            def mlp():
                def relu_of(b):
                    sc.wait_ge(sem("up_ready"), count.take("up_ready"))
                    sc.activation(relu[:, b, :], ps[4 + b][:, :], ACT.Relu).then_inc(sem("relu_ready"), 1)
                with count.loop(N_CHUNK // 2, up_ready=2):
                    relu_of(0)
                    relu_of(1)
                count.skip("acc_ready", 4)

            def take_queries():
                for half in range(2):
                    sc.wait_ge(sem("peer_q_done"), count.take("peer_q_done"))
                    for dst, func in ((pq, ACT.Copy), (pq_sq, ACT.Square)):
                        sc.activation(dst[:, half * S:(half + 1) * S], ps[4 + half][:, 0:S], func)\
                            .then_inc(sem("pq_ready"), 1)

            def diagonals(b, ks, first=False):
                for k in ks:
                    if k >= 4 or not first:
                        sc.wait_ge(sem("v_used"), count.take("v_used"))
                    sc.activation(diag[:, k % 4, :], ident, ACT.Copy, scale=weight[:, 16 * b + k:16 * b + k + 1])\
                        .then_inc(sem("diag_ready"), 1)

            def gates_of(b):
                sc.wait_ge(sem("top_ready"), count.take("top_ready"))
                sc.activation(gate_w[:, 16 * b:16 * b + 16], top, ACT.Exp, bias=neg_top, accum_out=mass[:, b:b + 1])\
                    .then_inc(sem("gate_w_ready"), 1)

            def gelu_of():
                sc.wait_ge(sem("dot_done"), count.take("dot_done", 16))
                sc.activation(gelu, dots, ACT.Gelu_apprx_tanh).then_inc(sem("gelu_ready"), 1)

            def unit(t, queries=False, ahead=True, first=False):
                sc.wait_ge(sem("weight_ready"), count.take("weight_ready"))
                diagonals(1 - t, range(8), first)
                if queries:
                    take_queries()
                if ahead:
                    gates_of(1 - t)
                diagonals(1 - t, range(8, TOPK))
                gelu_of()

            def peer():
                take_queries()
                gates_of(0)
                take_queries()
                gates_of(1)
                gelu_of()
                unit(1, first=True)
                unit(0, queries=True)
                with count.loop(P_HEADS - 3, weight_ready=2, v_used=32, peer_q_done=2, top_ready=2, dot_done=32):
                    unit(1)
                    unit(0, queries=True)
                unit(1)
                unit(0)
                unit(1, ahead=False)
                sc.wait_ge(sem("weight_ready"), count.take("weight_ready"))
                diagonals(1, range(TOPK))

            def hybrid_attention():
                sc.wait_ge(sem("reduced_ready"), count.take("reduced_ready"))
                sc.activation(trig, reduced, ACT.Sin).then_inc(sem("trig_ready"), 1)
                for k in range(4):
                    a = k * HALF
                    z = min(a + HALF, C_END)
                    sc.wait_ge(sem("proj_a_done"), count.take("proj_a_done"))
                    sc.activation(sq[:, 1, a:z], ps[4 + k][:, 0:z - a], ACT.Square).then_inc(sem("sq_a"), 1)
                    sc.activation(proj[:, 1, a:z], ps[4 + k][:, 0:z - a], ACT.Copy).then_inc(sem("proj_a"), 1)
                sc.wait_ge(sem("proj_v"), count.take("proj_v", 4))
                sc.wait_ge(sem("proj_a"), count.take("proj_a", 4))
                sc.activation(gates.rearrange("p (t n) -> p t n", t=NT), proj[:, :, C_GATE:C_CQ], ACT.Sigmoid)\
                    .then_inc(sem("gates_ready"), 1)
                sc.wait_ge(sem("lora_turned"), count.take("lora_turned", 2))
                sc.activation(loraT[:, 2, :], ps[2][:, 0:S], ACT.Copy).then_inc(sem("loraT_ready"), 1)
                sc.wait_ge(sem("mq_a_done"), count.take("mq_a_done"))
                q1 = mq[:, 1, :, :].rearrange("p h n -> p (h n)")
                sc.activation(q1[:, 0:HALF], ps[6][:, :], ACT.Copy)
                sc.activation(q1[:, HALF:768], ps[7][:, 0:256], ACT.Copy).then_inc(sem("mq_a"), 1)
                sc.wait_ge(sem("mkv_a_done"), count.take("mkv_a_done"))
                for n in range(2):
                    kv = ps[2 + n][:, :].rearrange("p (h n) -> p h n", n=P)
                    sc.activation(mk[:, 1, 4 * n:4 * n + 4, 0:HD], kv[:, :, 0:HD], ACT.Copy)
                    last = sc.activation(val[:, 1, n * 256:(n + 1) * 256].rearrange("p (h n) -> p h n", n=HD),
                                         kv[:, :, HD:P], ACT.Copy)
                last.then_inc(sem("mkv_a"), 1)
                take_turned()
                sc.wait_ge(sem("hidden_done"), count.take("hidden_done", 2))
                sc.activation(hidden.rearrange("p a b n -> p (a b n)"), ps[0][:, 0:120], ACT.Gelu_apprx_tanh)\
                    .then_inc(sem("hidden_ready"), 1)
                sc.wait_ge(sem("c_sco_ready"), count.take("c_sco_ready"))
                sc.activation(c_prob, c_sco, ACT.Exp, scale=-1.0).then_inc(sem("c_prob_ready"), 1)
                for n in range(2):
                    sc.wait_ge(sem("c_turned_a"), count.take("c_turned_a"))
                    sc.activation(c_probT[:, (2 + n) * HALF:(3 + n) * HALF], ps[6 + n][0:30, :], ACT.Copy)\
                        .then_inc(sem("c_probT_a"), 1)
                for n in (1, 3, 5, 7):
                    sc.wait_ge(sem("m_turned_a"), count.take("m_turned_a"))
                    bank = (2, 3, 4, 5, 6, 7, 0, 1)[n]
                    sc.activation((mqT, mkT)[n // 4][:, 2 * (n % 4):2 * (n % 4) + 2, :],
                                  ps[bank][0:QK, :].rearrange("p (h s) -> p h s", h=2), ACT.Copy).then_inc(sem("mT_a"), 1)
                for u in range(13):
                    if u < 12:
                        exps(u % 2)
                    if u:
                        take_probT()

            sc.wait_ge(sem("lam_summed"), count.take("lam_summed", 2))
            sc.activation(lam_exp[:, 0:2], lam_sum, ACT.Exp).then_inc(sem("lam_exp"), 1)
            sc.wait_ge(sem("bias_rows_ready"), count.take("bias_rows_ready"))
            sc.activation(bias_rows, ps[0][0:HEADS, 0:384], ACT.Copy).then_inc(sem("bias_rows_set"), 1)
            take_turned()
            attention_layer()
            take_turned()
            count.skip("acc_ready", 4)
            take_turned()
            mlp()
            take_turned()
            attention_layer()
            take_turned()
            count.skip("acc_ready", 4)
            take_turned()
            mlp()
            take_turned()
            hybrid_attention()
            take_turned()
            count.skip("acc_ready", 4)
            for n in range(4):
                sc.wait_ge(sem("keys_turned"), count.take("keys_turned"))
                sc.activation(keysT[:, n * HALF:(n + 1) * HALF], ps[4 + n][:, :], ACT.Copy)\
                    .then_inc(sem("keysT_ready"), 1)
            take_turned()
            peer()

        @block.gpsimd
        def _(po):
            count = Count(po)
            po.dma_start(bucket_sb, T["buckets"]).then_inc(sem("bias_in_landed"), 16)
            po.dma_start(relb_sb[0:32, :], T["rel_bias"]).then_inc(sem("bias_in_landed"), 16)
            po.dma_start(lam_in, to_partitions(T["lam_a"][0].rearrange("a d -> (a d)"))).then_inc(sem("lam_landed"), 16)
            po.dma_start(subln, to_partitions(T["subln_a"][0])).then_inc(sem("subln_landed"), 16)
            po.memset(neg_half, -0.5).then_inc(sem("neg_half_set"), 1)
            po.wait_ge(sem("neg_half_set"), count.take("neg_half_set"))
            po.memset(pos_i[:, :], 0).then_inc(sem("pos_cleared"), 1)
            po.wait_ge(sem("pos_cleared"), count.take("pos_cleared"))
            pos = T["positions_2"]
            loads = [(pos_i[:, 0:2], bass.AP(pos.tensor, 0, [[1, P], [P, NT]])),
                     (pos_i[0:15, 2:3], bass.AP(pos.tensor, 31, [[16, N_CMP], [1, 1]])),
                     (pos_i[15:30, 2:3], bass.AP(pos.tensor, 31, [[16, N_CMP], [1, 1]])),
                     (freqs, to_partitions(T["freqs"])), (gain_q, to_partitions(T["nsa_q_gain_2"][0])),
                     (gain_ks, to_partitions(T["nsa_ks_gain_2"][0])), (gain_kw, to_partitions(T["nsa_kw_gain_2"][0])),
                     (gain_kc, to_partitions(T["nsa_kc_gain_2"][0])), (gain_mq, to_partitions(T["mla_q_gain_2"][0])),
                     (gain_mk, to_partitions(T["mla_k_gain_2"][0])), (gain_cq, to_partitions(T["mla_q_lora_gain_2"][0])),
                     (gain_ckv, to_partitions(T["mla_kv_lora_gain_2"][0])),
                     (wide_gain[:, 0, :], to_partitions(T["norm1_gain_2"][0])),
                     (wide_gain[:, 1, 0:HALF], to_partitions(T["out_gain_a_2"][0])),
                     (wide_gain[:, 1, HALF:D], to_partitions(T["out_gain_b_2"][0])),
                     (wide_gain[:, 2, :], to_partitions(T["norm2_gain_2"][0])),
                     (cmp_posT[0:HD, :], bass.AP(T["cmp_pos_2"].tensor, 0, [[1, HD], [2 * HD, 16]])),
                     (cmp_posT[HD:P, :], bass.AP(T["cmp_pos_2"].tensor, HD, [[1, HD], [2 * HD, 16]])),
                     (cmp_w2[:, 0, :, :], T["cmp_k_w2_2"][0].rearrange("(b p) n -> p b n", p=P)),
                     (cmp_w2[:, 1, :, :], T["cmp_v_w2_2"][0].rearrange("(b p) n -> p b n", p=P))]
            assert len(loads) == N_SMALL
            for dst, src in loads:
                po.dma_start(dst, src, allow_slow_non_contiguous=True).then_inc(sem("small_landed"), 16)
            po.wait_ge(sem("bias_rows_set"), count.take("bias_rows_set"))
            po.dma_start(scratch, bias_rows).then_inc(sem("scratch_stored"), 16)
            po.wait_ge(sem("scratch_stored"), count.take("scratch_stored", 16))
            pitch = HEADS * 384
            po.dma_start(bass.AP(shifted.tensor, 0, [[pitch + 1, P], [1, pitch]]),
                         bass.AP(scratch.tensor, 0, [[0, P], [1, pitch]])).then_inc(sem("shifted_stored"), 16)
            po.wait_ge(sem("shifted_stored"), count.take("shifted_stored", 16))
            for first, n, at in ((255, P, 0), (127, S, P)):
                src = bass.AP(shifted.tensor, first, [[pitch, P], [384, HEADS], [1, n]])
                po.dma_start(bias[:, :, at:at + n], src).then_inc(sem("bias_landed"), 16)
            for s, (g, b, layer) in enumerate((("ln1_g", "ln1_b", 0), ("ln2_g", "ln2_b", 0), ("ln1_g", "ln1_b", 1),
                                               ("ln2_g", "ln2_b", 1))):
                po.dma_start(ln_gb[:, s, 0, :], to_partitions(T[g][layer])).then_inc(sem(f"ln{s}_landed"), 16)
                po.dma_start(ln_gb[:, s, 1, :], to_partitions(T[b][layer])).then_inc(sem(f"ln{s}_landed"), 16)

            def power(dst, src, ready, done):
                po.wait_ge(sem(ready), count.take(ready))
                po.tensor_tensor(dst, src, neg_half[:, 0:src.shape[-1]] if len(src.shape) == 2 else neg_half, ALU.pow)\
                    .then_inc(sem(done), 1)

            def layer_norm():
                for t in range(NT):
                    power(rstd[:, t:t + 1], var_eps[:, t:t + 1], "var_ready", "rstd_ready")

            power(ms_out[:, 0:16], ms_in[:, 0:16], "ms_ready", "rms_ready")
            layer_norm()
            layer_norm()
            layer_norm()
            layer_norm()
            def rms(n, w):
                power(ms_out[:, n:n + w], ms_in[:, n:n + w], "ms_ready", "rms_ready")

            po.wait_ge(sem("small_landed"), count.take("small_landed", 16 * N_SMALL))
            rms(0, 1)
            rms(1, 1)
            rms(0, 48)
            po.wait_ge(sem("flow_x0_ready"), count.take("flow_x0_ready"))
            for g in range(2):
                for r in range(2):
                    po.dma_start(flow_x[64 * r:64 * r + 64, :, g, :], flow_x0[64 * g:64 * g + 64, :, r, :])\
                        .then_inc(sem("flow_landed"), 16)
            po.wait_ge(sem("flow_landed"), count.take("flow_landed", 64))
            for a in range(2):
                for g in range(2):
                    po.tensor_tensor(blocks[:, a, :, 15 * g:15 * g + 15], spread(flow_x[:, a, g, :], (1, 16), (8, 15)),
                                     spread(cmp_posT, (1, 16), (0, 15)), ALU.add).then_inc(sem("blocks_ready"), 1)
            po.wait_ge(sem("kc_ms_ready"), count.take("kc_ms_ready"))
            po.tensor_tensor(rstd[0:30, 0:1], var_eps[0:30, 0:1], neg_half[0:30, 0:1], ALU.pow)\
                .then_inc(sem("kc_rms_ready"), 1)
            rms(0, 32)
            rms(0, 2)
            rms(2, 2)
            rms(0, 1)
            rms(1, 1)
            def gather(table, rows_of, k, ring_of, name, wait):
                if wait:
                    po.wait_ge(sem("dot_done" if name == "u" else "v_used"), count.take("dot_done" if name == "u" else "v_used"))
                    alone()
                po.indirect_dma_start(ring_of[:, k % RING, :], None, table,
                                      bass.IndirectOffsetOnAxis(ap=rows_of[:, k:k + 1], axis=0))\
                    .then_inc(sem(f"{name}{k % RING}_landed"), 16)

            def alone():
                po.sem_inc(sem("gathers_due"), 1)

            peer_u, peer_v = T["peer_u_2"][0], T["peer_v_2"][0]

            def unit(t, add=True, power_at=None, u_first=False, v_first=False, dot=True):
                if dot:
                    po.wait_ge(sem("experts_ready"), count.take("experts_ready"))
                    alone()
                if add:
                    po.wait_ge(sem("weight_ready"), count.take("weight_ready"))
                    alone()
                for k in range(TOPK):
                    if dot:
                        gather(peer_u, expert_u[:, 16 * t:16 * t + 16], k, arena_u, "u", k >= RING or not u_first)
                    if add:
                        gather(peer_v, expert_v[:, 16 * (1 - t):16 * (1 - t) + 16], k, arena_v, "v",
                               k >= RING or not v_first)
                    if k == power_at:
                        power(ms_out[:, 0:2], ms_in[:, 0:2], "ms_ready", "rms_ready")

            power(ms_out[:, 0:2], ms_in[:, 0:2], "ms_ready", "rms_ready")
            po.wait_ge(sem("keysT_ready"), count.take("keysT_ready", 4))
            unit(0, add=False, u_first=True)
            unit(1, power_at=3, v_first=True)
            unit(0)
            with count.loop(P_HEADS - 2, experts_ready=2, weight_ready=2, dot_done=32, v_used=32, ms_ready=1):
                unit(1, power_at=3)
                unit(0)
            unit(1)
            unit(0, dot=False)

        @block.vector
        def _(ve):
            count = Count(ve)

            def then(ins):
                ins.then_inc(sem("v_chain"), 1)
                ve.wait_ge(sem("v_chain"), count.take("v_chain"))

            def take_turned():
                for c in range(2):
                    ve.wait_ge(sem("turned_v"), count.take("turned_v"))
                    ve.tensor_copy(hT[:, 2 * c:2 * c + 2, :], ps[4 + c][:, :].rearrange("p (c s) -> p c s", c=2))\
                        .then_inc(sem("hT_v"), 1)

            def add_bias(b, banks, table):
                for m in range(2):
                    ve.wait_ge(sem("scores_ready"), count.take("scores_ready"))
                    for t, (a, z) in enumerate(((0, P), (P, 384))):
                        ve.tensor_tensor_reduce(sco[:, b, m, a:z], ps[banks[m]][:, a:z], table(m)[:, a:z], 1.0, 3e38,
                                                ALU.add, ALU.min, peak[:, b, m, t:t + 1]).then_inc(sem("sco_ready"), 1)

            def add_moving_bias(b, table):
                for m in range(2):
                    ve.wait_ge(sem("scores_ready"), count.take("scores_ready"))
                    then(ve.tensor_tensor(sco[:, b, m, :], ps[m][:, 0:384], table(m), ALU.add))
                    for t, (a, z) in enumerate(((0, P), (P, 384))):
                        ve.tensor_reduce(peak[:, b, m, t:t + 1], sco[:, b, m, a:z], X, ALU.min)\
                            .then_inc(sem("sco_ready"), 1)

            def take_probT(b):
                ve.wait_ge(sem("probT_v_turned"), count.take("probT_v_turned"))
                ve.tensor_copy(probT[:, 0, :], ps[2][:, 0:384]).then_inc(sem("probT_v"), 1)

            def differential(f, b):
                ve.wait_ge(sem("probs_ready"), count.take("probs_ready", 4))
                then(ve.reciprocal(share[:, b, :, :], total[:, b, :, :]))
                then(ve.tensor_scalar(share[:, b, 1, :], share[:, b, 1, :], lam_exp[:, 2:3], None, ALU.mult))
                ve.wait_ge(sem("weighed"), count.take("weighed"))
                for t in range(NT):
                    then(ve.tensor_scalar(omap[:, t, :], ps[6 + b][:, (2 + t) * P:(3 + t) * P], share[:, b, 1, t:t + 1],
                                          None, ALU.mult))
                for t in range(NT):
                    last = ve.scalar_tensor_tensor(out=nat[:, t, bass.ds(f * P, P)], in0=ps[6 + b][:, t * P:(t + 1) * P],
                                                   scalar=share[:, b, 0, t:t + 1], in1=omap[:, t, :], op0=ALU.mult,
                                                   op1=ALU.add)
                then(last)

            def plain(f, b):
                ve.wait_ge(sem("probs_ready"), count.take("probs_ready", 4))
                then(ve.reciprocal(share[:, b, :, :], total[:, b, :, :]))
                ve.wait_ge(sem("weighed"), count.take("weighed"))
                for m in range(2):
                    for t in range(NT):
                        last = ve.tensor_scalar(nat[:, t, bass.ds(f * P + m * HD, HD)],
                                                ps[6 + b][:, (2 * m + t) * HD:(2 * m + t + 1) * HD],
                                                share[:, b, m, t:t + 1], None, ALU.mult)
                then(last)

            def attend_block(f, b, finish):
                add_moving_bias(b, lambda m: bias[:, bass.ds(f * 2 + m, 1), :].rearrange("p a k -> p (a k)"))
                take_probT(b)
                finish(f, b)

            def attention_layer(finish, chained):
                for k in range(2):
                    ve.wait_ge(sem("acc_ready"), count.take("acc_ready"))
                    ve.tensor_copy(val[:, 0, k * HALF:(k + 1) * HALF], ps[k][:, :]).then_inc(sem("val_v"), 1)
                count.skip("acc_ready", 2)
                with count.loop(4, scores_ready=4, probs_ready=8, probT_v_turned=2, weighed=2, v_chain=chained) as i:
                    for b in range(2):
                        attend_block(i * 2 + b, b, finish)

            def add_residual(scale):
                for t in range(NT):
                    for k in range(2):
                        ve.wait_ge(sem("acc_ready"), count.take("acc_ready"))
                        part = h[:, t, k * HALF:(k + 1) * HALF]
                        then(ve.scalar_tensor_tensor(out=part, in0=part, scalar=scale, in1=ps[2 * t + k][:, :],
                                                     op0=ALU.mult, op1=ALU.add))

            def layer_norm(s):
                ve.wait_ge(sem(f"ln{s}_landed"), count.take(f"ln{s}_landed", 32))
                for t in range(NT):
                    for k in range(2):
                        ve.wait_ge(sem("acc_ready"), count.take("acc_ready"))
                        part = h[:, t, k * HALF:(k + 1) * HALF]
                        then(ve.scalar_tensor_tensor(out=part, in0=part, scalar=ALPHA, in1=ps[2 * t + k][:, :],
                                                     op0=ALU.mult, op1=ALU.add))
                        then(ve.bn_stats(stats[:, 6 * k:6 * k + 6], part))
                    then(ve.bn_aggr(moments[:, 2 * t:2 * t + 2], stats[:, 0:12].rearrange("p (k s) -> p k s", k=2)))
                    ve.tensor_scalar(var_eps[:, t:t + 1], moments[:, 2 * t + 1:2 * t + 2], LN_EPS, None, ALU.add)\
                        .then_inc(sem("var_ready"), 1)
                    then(ve.scalar_tensor_tensor(out=h[:, t, :], in0=h[:, t, :], scalar=moments[:, 2 * t:2 * t + 1],
                                                 in1=ln_gb[:, s, 0, :], op0=ALU.subtract, op1=ALU.mult))
                    ve.wait_ge(sem("rstd_ready"), count.take("rstd_ready"))
                    ve.scalar_tensor_tensor(out=h[:, t, :], in0=h[:, t, :], scalar=rstd[:, t:t + 1],
                                            in1=ln_gb[:, s, 1, :], op0=ALU.mult, op1=ALU.add).then_inc(sem("h_ready"), 1)

            def mlp():
                def square(b):
                    ve.wait_ge(sem("relu_ready"), count.take("relu_ready"))
                    ve.tensor_tensor(act[:, b, :], ps[4 + b][:, :], relu[:, b, :], ALU.mult).then_inc(sem("act_ready"), 1)
                with count.loop(N_CHUNK // 2, relu_ready=2):
                    square(0)
                    square(1)

            def rms_of(src, at, width, n_cols=1):
                for n in range(n_cols):
                    a = n * width
                    then(ve.tensor_tensor_reduce(tmp[:, 0, 0:width], src[:, a:a + width], src[:, a:a + width], 1.0, 0.0,
                                                 ALU.mult, ALU.add, sq_sum[:, at + n:at + n + 1]))
                ve.tensor_scalar(ms_in[:, at:at + n_cols], sq_sum[:, at:at + n_cols], 1.0 / width, EPS, ALU.mult,
                                 ALU.add).then_inc(sem("ms_ready"), 1)

            def wide_norm(gain):
                for t in range(NT):
                    rms_of(h[:, t, :], t, D)
                for t in range(NT):
                    ve.wait_ge(sem("rms_ready"), count.take("rms_ready"))
                    ve.scalar_tensor_tensor(out=nat[:, t, :], in0=h[:, t, :], scalar=ms_out[:, t:t + 1],
                                            in1=wide_gain[:, gain, :], op0=ALU.mult, op1=ALU.mult)\
                        .then_inc(sem("nat_ready"), 1)

            def rope(x1, x2, c, s, shape):
                n = shape[0] * shape[1] * shape[2]
                steps = (shape[1] * shape[2], shape[0]), (shape[2], shape[1]), (1, shape[2])
                t = [spread(rope_tmp[0:x1.shape[0], k, :], *steps) for k in range(4)]
                for k, (u, v) in enumerate(((x1, c), (x2, s), (x2, c), (x1, s))):
                    then(ve.tensor_tensor(t[k], u, v, ALU.mult))
                then(ve.tensor_tensor(x1, t[0], t[1], ALU.subtract))
                then(ve.tensor_tensor(x2, t[2], t[3], ALU.add))

            def angles():
                then(ve.tensor_copy(pos_f, pos_i[:, :]))
                then(ve.tensor_tensor(spread(angle, (24, 3), (1, 24)), spread(pos_f, (1, 3), (0, 24)),
                                      spread(freqs, (0, 3), (1, 24)), ALU.mult))
                for n, phase in enumerate((0.25, 0.0)):
                    then(ve.tensor_scalar(cycles[:, 72 * n:72 * n + 72], angle, 1 / (2 * math.pi), phase, ALU.mult, ALU.add))
                    then(ve.tensor_copy(reduced[:, 72 * n:72 * n + 72], angle))
                then(ve.tensor_scalar(cycles, cycles, 1.5 * 2 ** 23, None, ALU.add))
                then(ve.tensor_scalar(cycles, cycles, -1.5 * 2 ** 23, None, ALU.add))
                rest = 2 * math.pi
                for bits in (2, 10, 18, None):
                    part = rest if bits is None else math.floor(rest * 2 ** bits) / 2 ** bits
                    rest -= part
                    then(ve.scalar_tensor_tensor(out=reduced, in0=cycles, scalar=-part, in1=reduced, op0=ALU.mult,
                                                 op1=ALU.add))
                then(ve.tensor_scalar(reduced[:, 0:72], reduced[:, 0:72], math.pi / 2, None, ALU.add))
                limit = float(np.nextafter(np.float32(math.pi), np.float32(0)))
                ve.tensor_scalar(reduced, reduced, limit, -limit, ALU.min, ALU.max).then_inc(sem("reduced_ready"), 1)

            def hybrid_attention():
                for k in range(4):
                    a = k * HALF
                    z = min(a + HALF, C_END)
                    ve.wait_ge(sem("proj_v_done"), count.take("proj_v_done"))
                    ve.tensor_copy(proj[:, 0, a:z], ps[k][:, 0:z - a]).then_inc(sem("proj_v"), 1)
                    ve.wait_ge(sem("proj_v"), count.take("proj_v"))
                then(ve.tensor_tensor(sq[:, 0, :], proj[:, 0, :], proj[:, 0, :], ALU.mult))
                ve.wait_ge(sem("sq_a"), count.take("sq_a", 4))
                then(ve.memset(ms_in, 1.0))
                for t in range(NT):
                    at = 24 * t
                    ve.tensor_reduce(sq_sum[:, at:at + 20], sq[:, t, 0:C_GATE].rearrange("p (g d) -> p g d", d=HD), X, ALU.add)
                    ve.tensor_reduce(sq_sum[:, at + 20:at + 21], sq[:, t, C_CQ:C_CKV], X, ALU.add)
                    then(ve.tensor_reduce(sq_sum[:, at + 21:at + 22], sq[:, t, C_CKV:C_KR], X, ALU.add))
                    then(ve.tensor_scalar(ms_in[:, at:at + 20], sq_sum[:, at:at + 20], 1.0 / HD, EPS, ALU.mult, ALU.add))
                    then(ve.tensor_scalar(ms_in[:, at + 20:at + 21], sq_sum[:, at + 20:at + 21], 1.0 / 256, EPS, ALU.mult, ALU.add))
                    then(ve.tensor_scalar(ms_in[:, at + 21:at + 22], sq_sum[:, at + 21:at + 22], 1.0 / 128, EPS, ALU.mult, ALU.add))
                ve.sem_inc(sem("ms_ready"), 1)
                ve.wait_ge(sem("flow_turned"), count.take("flow_turned"))
                for a in range(2):
                    last = ve.tensor_copy(flow_x0[:, a, :, :].rearrange("p r i -> p i r"),
                                          ps[0][:, a * S:(a + 1) * S].rearrange("p (i r) -> p i r", r=2))
                then(last)
                ve.sem_inc(sem("flow_x0_ready"), 2)
                ve.wait_ge(sem("rms_ready"), count.take("rms_ready"))
                ve.wait_ge(sem("proj_a"), count.take("proj_a", 4))
                for t in range(NT):
                    ve.scalar_tensor_tensor(out=lora[:, t, 0:256], in0=proj[:, t, C_CQ:C_CKV],
                                            scalar=ms_out[:, 24 * t + 20:24 * t + 21], in1=gain_cq, op0=ALU.mult, op1=ALU.mult)
                    last = ve.scalar_tensor_tensor(out=lora[:, t, 256:384], in0=proj[:, t, C_CKV:C_KR],
                                                   scalar=ms_out[:, 24 * t + 21:24 * t + 22], in1=gain_ckv, op0=ALU.mult,
                                                   op1=ALU.mult)
                last.then_inc(sem("lora_ready"), 1)
                for t in range(NT):
                    q = nat[:, t, 0:HALF].rearrange("p (g d) -> p g d", d=HD)
                    then(ve.tensor_tensor(q, proj[:, t, C_Q:C_KC].rearrange("p (g d) -> p g d", d=HD),
                                          spread(ms_out[:, 24 * t:24 * t + 8], (1, 8), (0, HD)), ALU.mult))
                    then(ve.tensor_tensor(q, q, spread(gain_q, (0, 8), (1, HD)), ALU.mult))
                    for n, (at, group, gain) in enumerate(((C_KS, 12, gain_ks), (C_KW, 16, gain_kw))):
                        k = nat[:, t, HALF + 256 * n:HALF + 256 * n + 256].rearrange("p (g c d) -> p g c d", g=2, c=2)
                        then(ve.tensor_tensor(k[:, :, 0, :], proj[:, t, at:at + P].rearrange("p (g d) -> p g d", d=HD),
                                              spread(ms_out[:, 24 * t + group:24 * t + group + 2], (1, 2), (0, HD)), ALU.mult))
                        then(ve.tensor_tensor(k[:, :, 0, :], k[:, :, 0, :], spread(gain, (0, 2), (1, HD)), ALU.mult))
                        then(ve.tensor_copy(k[:, :, 1, :], k[:, :, 0, :]))
                ve.wait_ge(sem("lora_turned"), count.take("lora_turned"))
                ve.tensor_copy(loraT[:, 0:2, :], ps[1][:, :].rearrange("p (c s) -> p c s", c=2)).then_inc(sem("loraT_ready"), 1)
                count.skip("lora_turned")
                ve.wait_ge(sem("trig_ready"), count.take("trig_ready"))
                x = nat[:, :, :].rearrange("p t (g d) -> p t g d", d=HD)
                rope(x[:, :, :, 0:8], x[:, :, :, 8:16], spread(cos, (24, NT), (0, 16), (1, 8)),
                     spread(sin, (24, NT), (0, 16), (1, 8)), (NT, 16, 8))
                ve.sem_inc(sem("nat_ready"), 2)
                ve.wait_ge(sem("mq_v_done"), count.take("mq_v_done"))
                q0 = mq[:, 0, :, :].rearrange("p h n -> p (h n)")
                ve.tensor_copy(q0[:, 0:HALF], ps[4][:, :])
                ve.tensor_copy(q0[:, HALF:768], ps[5][:, 0:256]).then_inc(sem("mq_v"), 1)
                ve.wait_ge(sem("mkv_v_done"), count.take("mkv_v_done"))
                for n in range(2):
                    kv = ps[n][:, :].rearrange("p (h n) -> p h n", n=P)
                    ve.tensor_copy(mk[:, 0, 4 * n:4 * n + 4, 0:HD], kv[:, :, 0:HD])
                    last = ve.tensor_copy(val[:, 0, n * 256:(n + 1) * 256].rearrange("p (h n) -> p h n", n=HD),
                                          kv[:, :, HD:P])
                last.then_inc(sem("mkv_v"), 1)
                for t in range(NT):
                    then(ve.tensor_copy(mk[:, t, :, HD:QK], spread(proj[:, t, C_KR:C_END], (0, MLA_HEADS), (1, 32))))
                take_turned()
                ve.wait_ge(sem("kcv_done"), count.take("kcv_done"))
                then(ve.tensor_copy(kcv, ps[1][0:30, 0:P]))
                then(ve.tensor_tensor_reduce(kc_sq, kcv[:, 0:HD], kcv[:, 0:HD], 1.0, 0.0, ALU.mult, ALU.add,
                                             sq_sum[0:30, 0:1]))
                ve.tensor_scalar(var_eps[0:30, 0:1], sq_sum[0:30, 0:1], 1.0 / HD, EPS, ALU.mult, ALU.add)\
                    .then_inc(sem("kc_ms_ready"), 1)
                ve.wait_ge(sem("mkv_a"), count.take("mkv_a"))
                ve.wait_ge(sem("mq_a"), count.take("mq_a"))
                ve.wait_ge(sem("mkv_v"), count.take("mkv_v"))
                for n, src in enumerate((mq, mk)):
                    flat = src.rearrange("p t h n -> p (t h n)")
                    then(ve.tensor_tensor(av[:, 1536 * n:1536 * n + 1536], flat, flat, ALU.mult))
                    then(ve.tensor_reduce(sq_sum[:, 16 * n:16 * n + 16],
                                          av[:, 1536 * n:1536 * n + 1536].rearrange("p (g d) -> p g d", d=QK), X, ALU.add))
                ve.tensor_scalar(ms_in[:, 0:32], sq_sum[:, 0:32], 1.0 / QK, EPS, ALU.mult, ALU.add).then_inc(sem("ms_ready"), 1)
                ve.wait_ge(sem("kc_rms_ready"), count.take("kc_rms_ready"))
                kc = kc_twice[:, 0:HD]
                then(ve.scalar_tensor_tensor(out=kc, in0=kcv[:, 0:HD], scalar=rstd[0:30, 0:1], in1=gain_kc[0:30, :],
                                             op0=ALU.mult, op1=ALU.mult))
                rope(spread(kc[:, 0:8], (0, 1), (0, 1), (1, 8)), spread(kc[:, 8:16], (0, 1), (0, 1), (1, 8)),
                     spread(cos[0:30, 48:56], (0, 1), (0, 1), (1, 8)), spread(sin[0:30, 48:56], (0, 1), (0, 1), (1, 8)),
                     (1, 1, 8))
                ve.tensor_copy(kc_twice[:, HD:P], kc).then_inc(sem("kc_ready"), 1)
                ve.wait_ge(sem("kc_turned"), count.take("kc_turned"))
                ve.tensor_copy(kcT, ps[2][:, 0:30]).then_inc(sem("kcT_ready"), 1)
                ve.wait_ge(sem("rms_ready"), count.take("rms_ready"))
                for n, (src, gain) in enumerate(((mq, gain_mq), (mk, gain_mk))):
                    flat = src.rearrange("p t h n -> p (t h) n")
                    then(ve.tensor_tensor(flat, flat, spread(ms_out[:, 16 * n:16 * n + 16], (1, 16), (0, QK)), ALU.mult))
                    then(ve.tensor_tensor(flat, flat, spread(gain, (0, 16), (1, QK)), ALU.mult))
                    rope(src[:, :, :, HD:HD + 16], src[:, :, :, HD + 16:QK],
                         spread(cos[:, 8:72], (24, NT), (0, MLA_HEADS), (1, 16)),
                         spread(sin[:, 8:72], (24, NT), (0, MLA_HEADS), (1, 16)), (NT, MLA_HEADS, 16))
                    ve.sem_inc(sem("mqk_ready"), 1)
                ve.wait_ge(sem("c_scores_done"), count.take("c_scores_done"))
                for g in range(2):
                    for half in range(2):
                        ve.tensor_tensor(spread(c_sco[:, 240 * g + 60 * half:], (120, 2), (1, 60)),
                                         ps[2 + half][:, 120 * g:120 * g + 120].rearrange("p (f n) -> p f n", f=2),
                                         spread(cmp_mask[:, 60 * g:60 * g + 60], (0, 2), (1, 60)), ALU.add)\
                            .then_inc(sem("v_chain"), 1)
                        ve.wait_ge(sem("v_chain"), count.take("v_chain"))
                by_row = c_sco.rearrange("p (r n) -> p r n", n=30)
                then(ve.tensor_reduce(c_peak, by_row, X, ALU.min))
                ve.tensor_tensor(by_row, by_row, spread(c_peak, (1, 16), (0, 30)), ALU.subtract).then_inc(sem("c_sco_ready"), 1)
                ve.wait_ge(sem("c_prob_ready"), count.take("c_prob_ready"))
                then(ve.tensor_reduce(c_total, c_prob.rearrange("p (r n) -> p r n", n=30), X, ALU.add))
                then(ve.reciprocal(c_share, c_total))
                then(ve.tensor_tensor(spread(c_share, (2, 8), (1, 2)), spread(c_share, (2, 8), (1, 2)),
                                      spread(row_seen, (0, 8), (1, 2)), ALU.mult))
                ve.wait_ge(sem("gates_ready"), count.take("gates_ready"))
                then(ve.tensor_tensor(spread(c_share, (2, 8), (1, 2)), spread(c_share, (2, 8), (1, 2)),
                                      spread(gates, (3, 8), (24, 2)), ALU.mult))
                for n in range(2):
                    ve.wait_ge(sem("c_turned_v"), count.take("c_turned_v"))
                    ve.tensor_copy(c_probT[:, n * HALF:(n + 1) * HALF], ps[4 + n][0:30, :]).then_inc(sem("c_probT_v"), 1)
                for n in range(2):
                    ve.wait_ge(sem("c_weighed"), count.take("c_weighed"))
                    o = nat[:, :, 256 * n:256 * n + 256].rearrange("p t (h d) -> p h t d", d=HD)
                    ve.tensor_tensor(o, ps[n][:, :].rearrange("p (h t d) -> p h t d", h=4, t=NT),
                                     spread(c_share[:, 8 * n:8 * n + 8], (2, 4), (1, 2), (0, HD)), ALU.mult)\
                        .then_inc(sem("c_out"), 1)
                ve.wait_ge(sem("c_out"), count.take("c_out", 2))
                for n in (0, 2, 4, 6):
                    ve.wait_ge(sem("m_turned_v"), count.take("m_turned_v"))
                    bank = (2, 3, 4, 5, 6, 7, 0, 1)[n]
                    ve.tensor_copy((mqT, mkT)[n // 4][:, 2 * (n % 4):2 * (n % 4) + 2, :],
                                   ps[bank][0:QK, :].rearrange("p (h s) -> p h s", h=2)).then_inc(sem("mT_v"), 1)

                def finish(u, b):
                    ve.wait_ge(sem("probs_ready"), count.take("probs_ready", 4))
                    then(ve.reciprocal(share[:, b, :, :], total[:, b, :, :]))
                    f = u % 4
                    if u < 8:
                        gate = gates[:, 3 * 2 * f + 1 + u // 4:3 * 2 * f + 2 + u // 4]
                        then(ve.tensor_tensor(share[:, b, :, :], share[:, b, :, :], spread(gate, (3, 2), (24, 2)), ALU.mult))
                    ve.wait_ge(sem("weighed"), count.take("weighed"))
                    for m in range(2):
                        for t in range(NT):
                            src = ps[6 + b][:, (2 * m + t) * HD:(2 * m + t + 1) * HD]
                            at = (0 if u < 8 else HALF) + (2 * f + m) * HD
                            dst = nat[:, t, at:at + HD]
                            if u < 8:
                                last = ve.scalar_tensor_tensor(out=dst, in0=src, scalar=share[:, b, m, t:t + 1], in1=dst,
                                                               op0=ALU.mult, op1=ALU.add)
                            else:
                                last = ve.tensor_scalar(dst, src, share[:, b, m, t:t + 1], None, ALU.mult)
                    then(last)

                for u in range(13):
                    if u < 12:
                        add_bias(u % 2, ((0, 1), (4, 5))[u % 2], lambda m: causal)
                    if u:
                        take_probT((u - 1) % 2)
                        finish(u - 1, (u - 1) % 2)
                for t in range(NT):
                    rms_of(nat[:, t, :], 2 * t, HALF, 2)
                for t in range(NT):
                    ve.wait_ge(sem("rms_ready"), count.take("rms_ready"))
                    for n in range(2):
                        part = nat[:, t, n * HALF:(n + 1) * HALF]
                        last = ve.scalar_tensor_tensor(out=part, in0=part, scalar=ms_out[:, 2 * t + n:2 * t + n + 1],
                                                       in1=wide_gain[:, 1, n * HALF:(n + 1) * HALF], op0=ALU.mult,
                                                       op1=ALU.mult)
                    last.then_inc(sem("nat_ready"), 1)

            def settle():
                ve.memset(settled, 0.0)

            def query_rms():
                ve.wait_ge(sem("peer_sq_done"), count.take("peer_sq_done"))
                ve.tensor_scalar(ms_in[:, 0:2], ps[7][:, 0:2], 1.0 / 256, EPS, ALU.mult, ALU.add)\
                    .then_inc(sem("ms_ready"), 1)

            def choose(t):
                if t == 0:
                    ve.wait_ge(sem("rms_ready"), count.take("rms_ready"))
                    ve.wait_ge(sem("key_scores_done"), count.take("key_scores_done"))
                    for tile in range(NT):
                        last = ve.tensor_scalar(key_sco[:, tile, :], ps[6][:, tile * S:(tile + 1) * S],
                                                ms_out[:, tile:tile + 1], None, ALU.mult)
                    then(last)
                    ve.sem_inc(sem("key_scores_taken"), 1)
                s = [key_sco[:, t, half * P:(half + 1) * P] for half in range(2)]
                left = [key_left[:, half * P:(half + 1) * P] for half in range(2)]

                def eight(half, n):
                    return best[:, 16 * half + 8 * n:16 * half + 8 * n + 8]

                def eight_keys(half, n):
                    return best_key[:, 16 * half + 8 * n:16 * half + 8 * n + 8]

                settle()
                for half in range(2):
                    ve.max(eight(half, 0), s[half]).then_inc(sem("v_chain"), 1)
                ve.wait_ge(sem("v_chain"), count.take("v_chain", 2))
                settle()
                for half in range(2):
                    ve.max_index(eight_keys(half, 0), eight(half, 0), s[half])
                    ve.match_replace(left[half], eight(half, 0), s[half], -3e38).then_inc(sem("v_chain"), 1)
                ve.wait_ge(sem("v_chain"), count.take("v_chain", 2))
                settle()
                for half in range(2):
                    ve.max(eight(half, 1), left[half]).then_inc(sem("v_chain"), 1)
                ve.wait_ge(sem("v_chain"), count.take("v_chain", 2))
                settle()
                for half in range(2):
                    ve.max_index(eight_keys(half, 1), eight(half, 1), left[half]).then_inc(sem("v_chain"), 1)
                ve.wait_ge(sem("v_chain"), count.take("v_chain", 2))
                ve.tensor_copy(best_key_f, best_key)
                then(ve.tensor_tensor(spread(pairs, (16, 16), (1, 16)), spread(best[:, 0:16], (1, 16), (0, 16)),
                                      spread(best[:, 16:32], (0, 16), (1, 16)), ALU.add))
                settle()
                ve.max(top[:, 0:8], pairs).then_inc(sem("v_chain"), 1)
                ve.wait_ge(sem("v_chain"), count.take("v_chain"))
                settle()
                ve.max_index(top_pair[:, 0:8], top[:, 0:8], pairs)
                ve.match_replace(pairs_left, top[:, 0:8], pairs, -3e38).then_inc(sem("v_chain"), 1)
                ve.wait_ge(sem("v_chain"), count.take("v_chain"))
                settle()
                ve.max(top[:, 8:16], pairs_left).then_inc(sem("v_chain"), 1)
                ve.wait_ge(sem("v_chain"), count.take("v_chain"))
                settle()
                ve.max_index(top_pair[:, 8:16], top[:, 8:16], pairs_left).then_inc(sem("v_chain"), 1)
                ve.wait_ge(sem("v_chain"), count.take("v_chain"))
                ve.tensor_scalar(neg_top, top[:, 0:1], -1.0, None, ALU.mult).then_inc(sem("top_ready"), 1)
                ve.tensor_scalar(place[:, 0:16], top_pair, 4, None, ALU.logical_shift_right)
                then(ve.tensor_scalar(place[:, 16:32], top_pair, 15, None, ALU.bitwise_and))
                then(ve.tensor_copy(place_f, place))
                for half in range(2):
                    at = slice(16 * half, 16 * half + 16)
                    grid = spread(match, (16, 16), (1, 16))
                    then(ve.tensor_tensor(grid, spread(place_f[:, at], (1, 16), (0, 16)),
                                          spread(counter, (0, 16), (1, 16)), ALU.is_equal))
                    then(ve.tensor_tensor(grid, grid, spread(best_key_f[:, at], (0, 16), (1, 16)), ALU.mult))
                    then(ve.tensor_reduce(picked[:, at], grid, X, ALU.add))
                then(ve.scalar_tensor_tensor(out=expert_u[:, 16 * t:16 * t + 16], in0=picked[:, 0:16],
                                             scalar=float(N_KEYS), in1=picked[:, 16:32], op0=ALU.mult, op1=ALU.add))
                ve.sem_inc(sem("experts_ready"), 1)

            def dot(t, ks):
                for k in ks:
                    ve.wait_ge(sem(f"u{k % RING}_landed"), count.take(f"u{k % RING}_landed", 16))
                    row = arena_u[:, k % RING, :]
                    ve.tensor_tensor_reduce(row, row, nat[:, t, :], 1.0, 0.0, ALU.mult, ALU.add, dots[:, k:k + 1])\
                        .then_inc(sem("dot_done"), 1)

            def weights_of(t):
                then(ve.reciprocal(mass[:, t:t + 1], mass[:, t:t + 1]))
                ve.wait_ge(sem("gelu_ready"), count.take("gelu_ready"))
                ve.tensor_copy(expert_v[:, 16 * t:16 * t + 16], expert_u[:, 16 * t:16 * t + 16])
                then(ve.scalar_tensor_tensor(out=weight[:, 16 * t:16 * t + 16], in0=gate_w[:, 16 * t:16 * t + 16],
                                             scalar=mass[:, t:t + 1], in1=gelu, op0=ALU.mult, op1=ALU.mult))
                ve.sem_inc(sem("weight_ready"), 1)

            def unit(t, ahead=True, more=False):
                dot(t, range(8))
                ve.wait_ge(sem("gate_w_ready"), count.take("gate_w_ready"))
                if ahead:
                    choose(1 - t)
                dot(t, range(8, TOPK))
                weights_of(t)
                if more:
                    query_rms()

            def peer():
                ve.memset(zeros, 0.0)
                then(ve.memset(ones, 1.0))
                ve.sem_inc(sem("peer_set"), 1)
                query_rms()
                choose(0)
                unit(0, more=True)
                per = {f"u{k}_landed": 64 for k in range(RING)}
                with count.loop(P_HEADS - 2, gate_w_ready=2, gelu_ready=2, rms_ready=1, key_scores_done=1,
                            peer_sq_done=1, v_chain=CHOOSE_STEPS, **per):
                    unit(1)
                    unit(0, more=True)
                unit(1)
                unit(0)
                unit(1, ahead=False)
                for t in range(NT):
                    ve.wait_ge(sem("v_used"), count.take("v_used", (N_UNITS - 1) * TOPK if t == 0 else TOPK))
                    for k in range(2):
                        part = h[:, t, k * HALF:(k + 1) * HALF]
                        last = ve.tensor_tensor(part, part, ps[2 * t + k][:, :], ALU.add)
                    last.then_inc(sem("y_ready"), 1)

            ve.wait_ge(sem("lam_landed"), count.take("lam_landed", 16))
            for n in range(2):
                ve.tensor_tensor_reduce(lam_prod, lam_in[:, 128 * n:128 * n + 64], lam_in[:, 128 * n + 64:128 * n + 128],
                                        1.0, 0.0, ALU.mult, ALU.add, lam_sum[:, n:n + 1]).then_inc(sem("lam_summed"), 1)
                ve.wait_ge(sem("lam_summed"), count.take("lam_summed"))
            ve.wait_ge(sem("bias_in_landed"), count.take("bias_in_landed", 32))
            then(ve.tensor_scalar(relb_sb[0:32, :], relb_sb[0:32, :], -1.0, None, ALU.mult))
            ve.memset(relb_sb[32:33, :], BIG).then_inc(sem("relb_set"), 1)
            take_turned()
            ve.wait_ge(sem("lam_exp"), count.take("lam_exp"))
            then(ve.scalar_tensor_tensor(out=lam_exp[:, 2:3], in0=lam_exp[:, 1:2], scalar=-LAM_INIT,
                                         in1=lam_exp[:, 0:1], op0=ALU.add, op1=ALU.subtract))
            ve.wait_ge(sem("subln_landed"), count.take("subln_landed", 16))
            then(ve.tensor_scalar(subln, subln, 1.0 - LAM_INIT, None, ALU.mult))
            ve.wait_ge(sem("bias_landed"), count.take("bias_landed", 32))
            attention_layer(differential, 14)
            heads = nat[:, :, :].rearrange("p t (g d) -> p (t g) d", d=P)
            tmp_h = tmp[:, :, :].rearrange("p t (g d) -> p (t g) d", d=P)
            then(ve.tensor_tensor(tmp[:, :, :], nat[:, :, :], nat[:, :, :], ALU.mult))
            then(ve.tensor_reduce(sq_sum[:, 0:16], tmp_h, X, ALU.add))
            ve.tensor_scalar(ms_in[:, 0:16], sq_sum[:, 0:16], 1.0 / P, LN_EPS, ALU.mult, ALU.add)\
                .then_inc(sem("ms_ready"), 1)
            ve.wait_ge(sem("rms_ready"), count.take("rms_ready"))
            for t in range(NT):
                part = nat[:, t, :].rearrange("p (g d) -> p g d", d=P)
                r = ms_out[:, 8 * t:8 * t + 8]
                then(ve.tensor_tensor(part, part, spread(r, (1, 8), (0, P)), ALU.mult))
                ve.tensor_tensor(part, part, spread(subln, (0, 8), (1, P)), ALU.mult).then_inc(sem("nat_ready"), 1)
            take_turned()
            layer_norm(0)
            take_turned()
            mlp()
            layer_norm(1)
            take_turned()
            attention_layer(plain, 8)
            ve.sem_inc(sem("nat_ready"), 2)
            take_turned()
            layer_norm(2)
            take_turned()
            mlp()
            layer_norm(3)
            ve.wait_ge(sem("small_landed"), count.take("small_landed", 16 * N_SMALL))
            wide_norm(0)
            angles()
            for gain, scale in ((gain_q, -(HD ** -0.5)), (gain_mq, -(QK ** -0.5))):
                then(ve.tensor_scalar(gain, gain, scale, None, ALU.mult))
            take_turned()
            hybrid_attention()
            ve.sem_inc(sem("attention_done"), 1)
            take_turned()
            add_residual(1.0)
            wide_norm(2)
            take_turned()
            peer()


def kernel(**inputs):
    import concourse.bacc as bacc
    from concourse.bass_utils import run_bass_kernel_spmd

    nc = bacc.Bacc("TRN2", target_bir_lowering=False, num_devices=1)
    arrays = {name: np.ascontiguousarray(value) for name, value in inputs.items()}
    arrays.update(const=shape_constants(), buckets=bucket_table(), freqs=rope_frequencies())
    dram = {}
    for name, a in arrays.items():
        dram[name] = nc.dram_tensor("in_" + name, a.shape, mybir.dt.from_np(a.dtype), kind="ExternalInput").ap()
    out = nc.dram_tensor("out_y", (1, S, D), F32, kind="ExternalOutput").ap()
    build(nc, dram, out)
    result = run_bass_kernel_spmd(nc, [{"in_" + n: a for n, a in arrays.items()}], core_ids=[0])
    return result.results[0]["out_y"]
```

```python
from contextlib import ExitStack, contextmanager
import math

import numpy as np

import concourse.bass as bass
from concourse import mybir

F32 = mybir.dt.float32
F32R = mybir.dt.float32r
U32 = mybir.dt.uint32
I32 = mybir.dt.int32
ALU = mybir.AluOpType
ACT = mybir.ActivationFunctionType
X = mybir.AxisListType.X

P = 128
D = 1024
S = 256
NT = S // P
NB = D // P
HALF = 512
HEADS = 16
HD = 64
DFF = 4 * D
N_CHUNK = DFF // 256
ALPHA = 4 ** 0.25
LN_EPS = 1e-5
EPS = 1e-6
LAM_INIT = 0.8 - 0.6 * math.exp(-0.3 * 0)
BIG = 1e30

N_SMALL = 20
C_Q, C_KC, C_VC, C_KS, C_VS, C_KW, C_VW, C_GATE, C_CQ, C_CKV, C_KR, C_END = np.cumsum(
    [0, 512, 128, 128, 128, 128, 128, 128, 24, 256, 128, 32]).tolist()
N_CMP = 15
MLA_HEADS = 8
QK = 96

P_HEADS = 8
TOPK = 16
N_KEYS = 128
RING = 8
N_UNITS = P_HEADS * NT
CHOOSE_STEPS = 49
U_LEAD = 4
PEER_SLOT = 2


def bucket_table():
    rel = 255 - np.arange(384)
    n = np.maximum(rel, 0)
    nf = np.maximum(n, 16).astype(np.float32)
    large = np.minimum(16 + (np.log(nf / 16) / math.log(8) * 16).astype(np.int32), 31)
    bucket = np.where(n < 16, n, large)
    table = np.zeros((33, 384), np.float32)
    table[bucket[rel >= 0], np.flatnonzero(rel >= 0)] = 1.0
    table[32, rel < 0] = 1.0
    return table


def rope_frequencies():
    return np.concatenate([
        (500000.0 ** (-np.arange(0, dim, 2) / dim)).astype(np.float32) for dim in (16, 32)])


def shape_constants():
    t = np.arange(S)
    causal = np.where(t[None, :] > t[:, None], BIG, 0.0)
    causal = np.concatenate([causal[:P, :P], causal[P:, :]], axis=1)
    end = 16 * np.arange(N_CMP) + 31
    seen = end[None, :] <= t[:, None]
    cmp_mask = np.full((P, 2, NT, 2, N_CMP), BIG)
    for g in range(2):
        for tile in range(NT):
            cmp_mask[:, g, tile, g, :] = np.where(seen[tile * P:(tile + 1) * P], 0.0, BIG)
    row_seen = seen.any(axis=1).reshape(NT, P).T
    count = np.broadcast_to(np.arange(TOPK), (P, TOPK))
    return np.concatenate([np.eye(P), causal, cmp_mask.reshape(P, -1), row_seen, count],
                          axis=1).astype(np.float32)


CO_ID, CO_CAUSAL, CO_CMP, CO_SEEN, CO_COUNT, CO_END = np.cumsum(
    [0, P, 384, 2 * NT * 2 * N_CMP, NT, TOPK]).tolist()


class Count:

    def __init__(self, engine):
        self.engine = engine
        self.seen, self.trip, self.per = {}, None, {}

    def skip(self, name, n=1):
        self.seen[name] = self.seen.get(name, 0) + n

    def take(self, name, n=1):
        self.skip(name, n)
        return self.seen[name] if self.trip is None else self.trip * self.per[name] + self.seen[name]

    @contextmanager
    def loop(self, trips, **per):
        before = dict(self.seen)
        with self.engine.Fori(0, trips) as i:
            self.trip, self.per = i, per
            yield i
            self.trip = None
        for name in self.seen:
            taken = self.seen[name] - before.get(name, 0)
            assert taken == per.get(name, 0), (name, taken)
            self.seen[name] += taken * (trips - 1)


def spread(ap, *dims):
    return bass.AP(ap.tensor, ap.offset, [list(ap.ap[0])] + [list(d) for d in dims])


def to_partitions(row, n=P):
    return bass.AP(row.tensor, row.offset, [[0, n]] + [list(d) for d in row.ap])


def build(nc, T, out):
    with ExitStack() as ctx:
        sems = {}

        def sem(name):
            if name not in sems:
                sems[name] = ctx.enter_context(nc.semaphore(name))
            return sems[name]

        def sb(name, shape, dt=F32):
            return ctx.enter_context(nc.sbuf_tensor(name, shape, dt))

        const = sb("const", [P, CO_END])
        ident = const[:, CO_ID:CO_CAUSAL]
        causal = const[:, CO_CAUSAL:CO_CMP]
        cmp_mask = const[:, CO_CMP:CO_SEEN]
        row_seen = const[:, CO_SEEN:CO_COUNT]
        counter = const[:, CO_COUNT:CO_END]
        h = sb("h", [P, NT, D])
        nat = sb("nat", [P, NT, D])
        with ExitStack() as over:
            def split(name, shape, dt=F32R):
                return over.enter_context(nc.sbuf_tensor(name, shape, dt))

            w_split = [[split("w0_high", [P, 2048]), split("w0_low", [P, 2048])]]
            act_low = split("act_low", [P, 2, HALF])
            act_sq = split("act_sq", [P, 2, HALF], F32)
            split("unused", [P, 7280 - 6144], F32)
            w_split.append([split("w1_high", [P, 2048]), split("w1_low", [P, 2048])])
            hT_low = split("hT_low", [P, NB, S])
            hT_high = split("hT_high", [P, NB, S])
            act_high = split("act_high", [P, 2, HALF])
        proj = sb("proj", [P, NT, C_END])
        prob = sb("prob", [P, 2, 2, 384])
        probT = sb("probT", [P, 2, 384])
        sco = sb("sco", [P, 2, 2, 384])
        qkring = sb("qkring", [P, 2, 2048])
        val = sb("val", [P, NT, D])
        hT = sb("hT", [P, NB, S])
        act = sb("act", [P, 2, HALF])
        ring = sb("ring", [P, 4, 2048])
        qkT = sb("qkT", [P, 2, 2, S])
        relu = sb("relu", [P, 2, HALF])
        peak = sb("peak", [P, 2, 2, NT])
        total = sb("total", [P, 2, 2, NT])
        share = sb("share", [P, 2, 2, NT])
        omap = sb("omap", [P, NT, P])
        arena_u = sb("arena_u", [P, RING, D])
        ln_gb = arena_u[:, :, :].rearrange("p (s g) d -> p s g d", g=2)
        arena_v = sb("arena_v", [P, RING, D])
        av = arena_v[:, :, :].rearrange("p r d -> p (r d)")
        bias = av[:, 0:HEADS * 384].rearrange("p (m k) -> p m k", m=HEADS)
        tmp = av[:, HEADS * 384:HEADS * 384 + 2048].rearrange("p (t d) -> p t d", t=NT)
        bucket_sb = tmp[0:33, 0, 0:384]
        relb_sb = tmp[0:33, 0, 384:400]
        bias_rows = tmp[0:HEADS, 0, 512:896]
        small = sb("small", [P, 1952])
        small_at = [0]

        def piece(n):
            small_at[0] += n
            return small[:, small_at[0] - n:small_at[0]]

        lam_in, lam_prod = tmp[:, 1, 0:256], tmp[:, 1, 256:320]
        lam_sum, lam_exp = piece(2), piece(3)
        stats, moments, var_eps, rstd = piece(24), piece(4), piece(2), piece(2)
        subln = piece(128)
        ms_in, ms_out = piece(24 * NT), piece(24 * NT)
        sq_sum = piece(24 * NT)
        neg_half = piece(24 * NT)
        wide_gain = sb("wide_gain", [P, 3, D])
        pos_i = sb("pos_i", [P, 3], I32)
        pos_f, freqs = piece(3), piece(24)
        angle, trig = piece(72), piece(144)
        cos, sin = trig[:, 0:72], trig[:, 72:144]
        gain_q, gain_ks, gain_kw, gain_kc = piece(64), piece(64), piece(64), piece(64)
        gain_mq, gain_mk, gain_cq, gain_ckv = piece(QK), piece(QK), piece(256), piece(128)
        cmp_posT = piece(16)
        cmp_w2 = piece(256).rearrange("p (a b n) -> p a b n", a=2, b=2)
        gates = piece(24 * NT)
        c_peak, c_total, c_share = piece(16), piece(16), piece(16)
        sq = av[:, 0:2 * C_END].rearrange("p (t n) -> p t n", t=NT)
        flow_x0 = av[:, 3440:3952].rearrange("p (a r i) -> p a r i", a=2, r=2)
        flow_x = av[:, 3952:4464].rearrange("p (a g i) -> p a g i", a=2, g=2)
        blocks = av[:, 4464:5424].rearrange("p (a j n) -> p a j n", a=2, j=16)
        hidden = av[:, 5424:5544].rearrange("p (a b n) -> p a b n", a=2, b=2)
        kcv = av[0:30, 5544:5672]
        kc_twice = av[0:30, 5672:5800]
        kc_sq = av[0:30, 5800:5864]
        kcT = av[:, 5864:5894]
        c_sco = av[:, 5894:6374]
        c_prob = av[:, 6374:6854]
        lora = av[:, 6854:7622].rearrange("p (t n) -> p t n", t=NT)
        au = arena_u[:, :, :].rearrange("p r d -> p (r d)")
        c_probT = au[0:30, 0:2048]
        mq = au[:, 2048:3584].rearrange("p (t h n) -> p t h n", t=NT, n=QK)
        mk = au[:, 3584:5120].rearrange("p (t h n) -> p t h n", t=NT, n=QK)
        rope_tmp = au[:, 5120:6144].rearrange("p (k n) -> p k n", k=4)
        cycles, reduced = au[:, 6144:6288], au[:, 6288:6432]
        loraT = relu[:, :, :].rearrange("p a n -> p (a n)")[:, 0:768].rearrange("p (c s) -> p c s", c=3)
        mqT = qkring[0:QK, 0, :].rearrange("p (h s) -> p h s", s=S)
        mkT = qkring[0:QK, 1, :].rearrange("p (h s) -> p h s", s=S)

        ones, settled = piece(1), piece(1)
        keysT = qkring[:, 0, :]
        keys = qkring[:, 1, :].rearrange("p (b d) -> p b d", d=P)
        pq, pq_sq = act[:, 0, :], act[:, 1, :]
        zeros = omap[:, 0, :]
        flat_sco = sco[:, :, :, :].rearrange("p a b n -> p (a b n)")
        diag = flat_sco[:, 0:512].rearrange("p (s n) -> p s n", s=4)
        key_sco = flat_sco[:, 512:1024].rearrange("p (t n) -> p t n", t=NT)
        pairs = flat_sco[:, 1024:1280]
        pairs_left = flat_sco[:, 1280:1536]
        flat_prob = prob[:, :, :, :].rearrange("p a b n -> p (a b n)")
        key_left, match = flat_prob[:, 0:256], flat_prob[:, 256:512]
        pool_of = [flat_prob[:, 512:].rearrange("p n -> p n"), 0]

        def bit(n, dt=F32):
            at = pool_of[1]
            pool_of[1] += n
            part = pool_of[0][:, at:at + n]
            return part if dt is F32 else part.bitcast(dt)

        best, best_key, best_key_f = bit(32), bit(32, U32), bit(32)
        top, top_pair, place, place_f, picked = bit(16), bit(16, U32), bit(32, U32), bit(32), bit(32)
        neg_top, mass = bit(1), bit(2)
        expert_u, expert_v = bit(32, U32), bit(32, U32)
        gate_w, dots, gelu, weight = bit(32), bit(16), bit(16), bit(32)
        ps = [ctx.enter_context(nc.psum_tensor(f"ps{i}", [P, HALF], F32)) for i in range(8)]

        def rows(w, j, n=2):
            return w[j * n * P:(j + 1) * n * P, :].rearrange("(c p) n -> p c n", p=P)

        def cols(w, at, n=256):
            return w[:, at:at + n].rearrange("(c p) n -> p c n", p=P)

        def cols_dyn(w, at, n):
            return w.rearrange("(c p) n -> p c n", p=P)[:, :, bass.ds(at, n)]

        x_t = T["x"][0].rearrange("(t p) d -> p t d", p=P)
        scratch = nc.dram_tensor("bias_scratch", (HEADS, 384), F32, kind="Internal").ap()
        shifted = nc.dram_tensor("bias_shifted", (P * (HEADS * 384 + 1),), F32, kind="Internal").ap()
        w_in, w_out_a = T["w_in_a"][0], T["w_out_a"][0]
        w_kv, w_q, w_out_b = T["w_kv_shared"], T["w_q_b"][0], T["w_out_b"][0]

        block = ctx.enter_context(nc.Block())

        @block.sync
        def _(sp):
            count = Count(sp)
            turn = [0]
            used = {}

            def chunk(dst, *srcs, landed=None):
                slot = turn[0] % 4
                turn[0] += 1
                load(ring, slot, f"ring{slot}", dst, *srcs, landed=landed and f"{landed}{slot}_landed")

            def load(where, slot, name, dst, *srcs, landed=None):
                if used.get(name):
                    sp.wait_ge(sem(name + "_used"), count.take(name + "_used"))
                used[name] = True
                for n, src in enumerate(srcs):
                    sp.dma_start(dst(where[:, slot, :], n), src).then_inc(sem(landed or name + "_landed"), 16)

            def load_raw(slot, dst, src):
                load(ring, slot, f"ring{slot}", dst, src, landed=f"raw{slot}_landed")

            def as_blocks(n):
                return lambda s, i: s.rearrange("p (c n) -> p c n", n=n)

            def two_columns(s, i):
                return s[:, i * 1024:(i + 1) * 1024].rearrange("p (c n) -> p c n", n=P)

            def nat_chunks(w, at=0, landed=None):
                for j in range(4):
                    chunk(as_blocks(D), rows(w[:, at:at + D], j), landed=landed)

            def qk_chunk(wq, wk, f):
                at = f * P
                name = f"qk{f % 2}" if isinstance(f, int) else None
                load(qkring, f % 2, name, two_columns, cols(wq, at, P), cols(wk, at, P))

            def qk_chunks(wq, wk):
                with count.loop(3, qk0_used=1, qk1_used=1) as i:
                    for b in range(2):
                        load(qkring, b, f"qk{b}", two_columns,
                             cols_dyn(wq, i * 256 + 256 + b * P, P), cols_dyn(wk, i * 256 + 256 + b * P, P))

            def mlp_chunks(layer):
                up, down = T["w_up"][layer], T["w_down"][layer]
                load_raw(0, as_blocks(256), cols(up, 0))
                load_raw(2, as_blocks(256), cols(up, 256))
                load_raw(1, as_blocks(D), rows(down, 0))
                with count.loop((N_CHUNK - 2) // 2, ring0_used=1, ring1_used=1, ring2_used=1, ring3_used=1) as i:
                    for b in range(2):
                        load_raw(2 * b, as_blocks(256), cols_dyn(up, i * 512 + (512 + 256 * b), 256))
                        load_raw(3 - 2 * b, as_blocks(D), down_rows(down, i * 2 + (1 + b)))
                load_raw(3, as_blocks(D), rows(down, N_CHUNK - 1))

            def down_rows(down, j):
                return down.rearrange("(j c p) n -> p j c n", p=P, c=2)[:, bass.ds(j, 1), :, :].rearrange(
                    "p j c n -> p (j c) n")

            for t in range(NT):
                sp.dma_start(h[:, t, :], x_t[:, t, :]).then_inc(sem("x_landed"), 16)
            sp.dma_start(const[:, :], T["const"]).then_inc(sem("const_landed"), 16)
            nat_chunks(w_in, 2 * D)
            qk_chunk(w_in, w_in[:, D:], 0)
            qk_chunk(w_in, w_in[:, D:], 1)
            nat_chunks(w_out_a, landed="raw")
            qk_chunks(w_in, w_in[:, D:])
            mlp_chunks(0)
            nat_chunks(w_kv, D)
            sp.wait_ge(sem("mlp_done"), count.take("mlp_done"))
            qk_chunk(w_q, w_kv, 0)
            qk_chunk(w_q, w_kv, 1)
            nat_chunks(w_out_b, landed="raw")
            qk_chunks(w_q, w_kv)
            mlp_chunks(1)
            for j in range(8):
                chunk(lambda s, i: s[:, 0:C_END], T["w_in_2"][0][j * P:(j + 1) * P, :])
            chunk(lambda s, i: s[:, 0:1536].rearrange("p (c n) -> p c n", c=2),
                  T["mla_w_uq_2"][0].rearrange("(c p) n -> p c n", p=P))
            chunk(lambda s, i: s[:, 0:D], T["mla_w_ukv_2"][0])
            for w1 in (T["cmp_k_w1_2"][0], T["cmp_v_w1_2"][0]):
                for j in range(2):
                    chunk(as_blocks(256), w1[j * D:(j + 1) * D, :].rearrange("(c p) n -> p c n", p=P))
            nat_chunks(T["w_out_2"][0])
            sp.wait_ge(sem("attention_done"), count.take("attention_done"))
            sp.dma_start(keys, T["peer_sub_keys_2"][0].rearrange("h t n d -> n (h t) d")).then_inc(sem("keys_landed"), 16)
            for j in range(P_HEADS):
                load(ring, PEER_SLOT, f"ring{PEER_SLOT}", as_blocks(256), cols(T["peer_w_q_2"][0], 256 * j))
            for t in range(NT):
                sp.wait_ge(sem("y_ready"), count.take("y_ready"))
                sp.dma_start(out[0, t * P:(t + 1) * P, :], h[:, t, :]).then_inc(sem("stored"), 16)
            sp.wait_ge(sem("stored"), count.take("stored", 32))

        @block.tensor
        def _(pe):
            count = Count(pe)
            turn = [0]

            def landed(name):
                pe.wait_ge(sem(name + "_landed"), count.take(name + "_landed", 32 if name.startswith("qk") else 16))

            def slot_of_turn():
                slot = turn[0] % 4
                turn[0] += 1
                landed(f"ring{slot}")
                return slot

            def turn_over(src, ready=None, split=False):
                for t in range(NT):
                    if ready:
                        pe.wait_ge(sem(ready), count.take(ready))
                    for c in range(NB):
                        last = pe.transpose(ps[4 + c // 2][:, (c % 2) * S + t * P:(c % 2) * S + t * P + P],
                                            src[:, t, c * P:(c + 1) * P], ident)
                        if t == NT - 1 and c % 2:
                            last.then_inc(sem("turned_s" if split else "turned_v" if c < 4 else "turned_a"), 1)

            def hT_ready():
                pe.wait_ge(sem("hT_v"), count.take("hT_v", 2))
                pe.wait_ge(sem("hT_a"), count.take("hT_a", 2))

            def natural(ready=True):
                if ready:
                    hT_ready()
                for j in range(4):
                    slot = slot_of_turn()
                    w = ring[:, slot, :].rearrange("p (c n) -> p c n", c=2)
                    order = [(cc, k) for k in range(4) for cc in range(2)] if j == 3 else \
                            [(cc, k) for cc in range(2) for k in range(4)]
                    for cc, k in order:
                        c = 2 * j + cc
                        last = pe.matmul(ps[k][:, :], hT[:, c, (k // 2) * P:(k // 2) * P + P],
                                         w[:, cc, (k % 2) * HALF:(k % 2 + 1) * HALF],
                                         start=(c == 0), stop=(c == NB - 1))
                        if c == NB - 1:
                            last.then_inc(sem("acc_ready"), 1)
                    if j < 3:
                        last.then_inc(sem(f"ring{slot}_used"), 1)
                pe.wait_ge(sem("acc_ready"), count.take("acc_ready", 4))
                pe.sem_inc(sem(f"ring{slot}_used"), 1)

            def project(b, part):
                if part == 0:
                    landed(f"qk{b}")
                w = qkring[:, b, :].rearrange("p (q c n) -> p q c n", q=2, c=NB)
                for c in range(NB):
                    last = pe.matmul(ps[4 + part][:, 0:S], w[:, part, c, :], hT[:, c, :],
                                     start=(c == 0), stop=(c == NB - 1))
                last.then_inc(sem("proj_ready"), 1)
                if part == 1:
                    pe.wait_ge(sem("proj_ready"), count.take("proj_ready", 2))
                    pe.sem_inc(sem(f"qk{b}_used"), 1)

            def scores(q, k, banks, rows_of=lambda m: slice(64 * m, 64 * m + 64)):
                for m in range(2):
                    pe.matmul(ps[banks[m]][:, 0:P], q(m)[:, 0:P], k(m)[:, 0:P], start=True, stop=True)
                for m in range(2):
                    pe.matmul(ps[banks[m]][:, P:384], q(m)[:, P:S], k(m)[:, 0:S], start=True, stop=True)\
                        .then_inc(sem("scores_ready"), 1)

            def turn_probs(b):
                for m in range(2):
                    pe.wait_ge(sem("probs_ready"), count.take("probs_ready", 2))
                    for k in range(3):
                        last = pe.transpose(ps[2 + m][:, k * P:(k + 1) * P], prob[:, b, m, k * P:(k + 1) * P], ident)
                    last.then_inc(sem("probT_v_turned" if m == 0 else "probT_a_turned"), 1)

            def weigh(b, v, dv):
                for m in range(2):
                    pe.wait_ge(sem("probT_v" if m == 0 else "probT_a"), count.take("probT_v" if m == 0 else "probT_a"))
                    o = ps[6 + b]
                    at = 2 * m * dv
                    pe.matmul(o[:, at:at + dv], probT[:, m, 0:P], v(m, 0), start=True, stop=True)
                    pe.matmul(o[:, at + dv:at + 2 * dv], probT[:, m, P:2 * P], v(m, 0), start=True, stop=False)
                    last = pe.matmul(o[:, at + dv:at + 2 * dv], probT[:, m, 2 * P:3 * P], v(m, 1),
                                     start=False, stop=True)
                last.then_inc(sem("weighed"), 1)

            def attend_block(f, b, dv, more=True):
                pe.wait_ge(sem("qkT_ready"), count.take("qkT_ready", 2))
                scores(lambda m: qkT[64 * m:64 * m + 64, b, 0, :], lambda m: qkT[64 * m:64 * m + 64, b, 1, :], (0, 1))
                if more:
                    project(1 - b, 0)
                turn_probs(b)
                if more:
                    project(1 - b, 1)
                weigh(b, lambda m, t: val[:, t, bass.ds(f * P + (m * 64 if dv == 64 else 0), dv)], dv)

            def attention_layer(dv):
                natural()
                project(0, 0)
                project(0, 1)
                pe.wait_ge(sem("val_v"), count.take("val_v", 2))
                pe.wait_ge(sem("val_a"), count.take("val_a", 2))
                with count.loop(3, qk0_landed=32, qk1_landed=32, qkT_ready=4, proj_ready=4, probs_ready=8,
                            probT_v=2, probT_a=2) as i:
                    for b in range(2):
                        attend_block(i * 2 + b, b, dv)
                attend_block(6, 0, dv)
                attend_block(7, 1, dv, more=False)

            def take_half(pair, half, slot):
                pe.wait_ge(sem(f"w{pair}_split"), count.take(f"w{pair}_split"))
                if half:
                    pe.sem_inc(sem(f"ring{slot}_used"), 1)

            def product(dst, a, b, start, stop):
                pe.matmul(dst, a[0], b[0], start=start, stop=False, skip_group_check=True)
                pe.matmul(dst, a[0], b[1], start=False, stop=False, skip_group_check=True)
                return pe.matmul(dst, a[1], b[0], start=False, stop=stop, skip_group_check=True)

            def split_natural():
                for j in range(4):
                    pe.wait_ge(sem("hT_split"), count.take("hT_split"))
                    order = [(cc, k) for k in range(4) for cc in range(2)] if j == 3 else \
                            [(cc, k) for cc in range(2) for k in range(4)]
                    for n, (cc, k) in enumerate(order):
                        c = 2 * j + cc
                        if n < 2 and j == 3:
                            take_half(j % 2, n, j)
                        elif n % 4 == 0 and j < 3:
                            take_half(j % 2, n // 4, j)
                        cut = slice(cc * D + (k % 2) * HALF, cc * D + (k % 2 + 1) * HALF)
                        last = product(ps[k][:, :], [x[:, c, (k // 2) * P:(k // 2) * P + P] for x in (hT_high, hT_low)],
                                       [x[:, cut] for x in w_split[j % 2]], start=(c == 0), stop=(c == NB - 1))
                        if c == NB - 1:
                            last.then_inc(sem("acc_ready"), 1)
                    if j < 3:
                        last.then_inc(sem(f"w{j % 2}_used"), 1)
                pe.wait_ge(sem("acc_ready"), count.take("acc_ready", 4))
                pe.sem_inc(sem("w1_used"), 1)

            def up(b, first=False):
                for fb in range(2):
                    for c in range(NB):
                        if first and fb == 0 and c % 2 == 0:
                            pe.wait_ge(sem("hT_split"), count.take("hT_split"))
                        if fb == 0 and c % 4 == 0:
                            take_half(0, c // 4, 2 * b)
                        at = c * 256 + fb * P
                        last = product(ps[4 + b][:, fb * S:(fb + 1) * S], [x[:, at:at + P] for x in w_split[0]],
                                       [x[:, c, :] for x in (hT_high, hT_low)], start=(c == 0), stop=(c == NB - 1))
                last.then_inc(sem("up_ready"), 1)

            def down(b, first=False, final=False):
                pe.wait_ge(sem("act_ready"), count.take("act_ready"))
                order = [(fb, k) for k in range(4) for fb in range(2)] if final else \
                        [(fb, k) for fb in range(2) for k in range(4)]
                for n, (fb, k) in enumerate(order):
                    if (n < 2) if final else (n % 4 == 0):
                        take_half(1, fb, 2 * b + 1)
                    at = fb * S + (k // 2) * P
                    cut = slice(fb * D + (k % 2) * HALF, fb * D + (k % 2 + 1) * HALF)
                    last = product(ps[k][:, :], [x[:, b, at:at + P] for x in (act_high, act_low)],
                                   [x[:, cut] for x in w_split[1]], start=(first and fb == 0), stop=(final and fb == 1))
                    if final and fb == 1:
                        last.then_inc(sem("acc_ready"), 1)
                if final:
                    pe.wait_ge(sem("acc_ready"), count.take("acc_ready", 4))
                    pe.sem_inc(sem("w1_used"), 1)
                    pe.sem_inc(sem("mlp_done"), 1)
                else:
                    last.then_inc(sem("w1_used"), 1)

            def mlp():
                up(0, first=True)
                up(1)
                down(0, first=True)
                with count.loop((N_CHUNK - 2) // 2, w0_split=4, w1_split=4, act_ready=2):
                    up(0)
                    down(1)
                    up(1)
                    down(0)
                down(1, final=True)

            def key_scores(j, more=True):
                landed(f"ring{PEER_SLOT}")
                w = ring[:, PEER_SLOT, :].rearrange("p (c n) -> p c n", n=256)
                for half in range(2):
                    for c in range(NB):
                        last = pe.matmul(ps[4 + half][:, 0:S], w[:, c, half * P:(half + 1) * P], hT[:, c, :],
                                         start=(c == 0), stop=(c == NB - 1))
                    last.then_inc(sem("peer_q_done"), 1)
                pe.wait_ge(sem("pq_ready"), count.take("pq_ready", 4))
                pe.sem_inc(sem(f"ring{PEER_SLOT}_used"), 1)
                for t in range(NT):
                    for half in range(2):
                        last = pe.matmul(ps[7][:, t:t + 1], pq_sq[:, half * S + t * P:half * S + t * P + P], ones,
                                         start=(half == 0), stop=(half == 1))
                last.then_inc(sem("peer_sq_done"), 1)
                for t in range(NT):
                    for half in range(2):
                        last = pe.matmul(ps[6][:, (2 * t + half) * P:(2 * t + half + 1) * P],
                                         pq[:, half * S + t * P:half * S + t * P + P],
                                         keysT[:, bass.ds(j * (2 * P) + half * P, P)], start=True, stop=True)
                last.then_inc(sem("key_scores_done"), 1)

            def add_experts(t, ks, final=False):
                for k in ks:
                    pe.wait_ge(sem(f"v{k % RING}_landed"), count.take(f"v{k % RING}_landed", 16))
                    pe.wait_ge(sem("diag_ready"), count.take("diag_ready"))
                    for n in range(2):
                        last = pe.matmul(ps[2 * t + n][:, :], diag[:, k % 4, :], arena_v[:, k % RING, n * HALF:(n + 1) * HALF],
                                         start=False, stop=(final and k == TOPK - 1), skip_group_check=True)
                    last.then_inc(sem("v_used"), 1)

            def unit(t, head=None):
                add_experts(1 - t, range(8))
                if head is not None:
                    pe.wait_ge(sem("key_scores_taken"), count.take("key_scores_taken"))
                    key_scores(head)
                add_experts(1 - t, range(8, TOPK))

            def peer():
                hT_ready()
                pe.wait_ge(sem("peer_set"), count.take("peer_set"))
                key_scores(0)
                for k in range(4):
                    pe.matmul(ps[k][:, :], zeros, hT[:, 0:2, :].rearrange("p c s -> p (c s)"), start=True, stop=False,
                              skip_group_check=True)
                pe.wait_ge(sem("key_scores_taken"), count.take("key_scores_taken"))
                key_scores(1)
                per = {f"v{k}_landed": 64 for k in range(RING)}
                with count.loop(P_HEADS - 2, diag_ready=32, key_scores_taken=1, pq_ready=4, ring2_landed=16, **per) as i:
                    unit(1)
                    unit(0, i + 2)
                unit(1)
                unit(0)
                unit(1)
                add_experts(1, range(TOPK), final=True)

            def nsa_unit(branch, f):
                g = f // 2
                at = (C_VS, C_VW)[branch] + g * HD
                return (lambda m: hT[64 * m:64 * m + 64, f, :], lambda m: hT[64 * m:64 * m + 64, 4 + 2 * branch + g, :],
                        lambda m, t: proj[:, t, at:at + HD])

            def mla_unit(f):
                return (lambda m: mqT[:, 2 * f + m, :], lambda m: mkT[:, 2 * f + m, :],
                        lambda m, t: val[:, t, (2 * f + m) * HD:(2 * f + m + 1) * HD])

            def hybrid_attention():
                hT_ready()
                for c in range(NB):
                    slot = slot_of_turn()
                    for k in range(8):
                        a = (k % 4) * HALF
                        z = min(a + HALF, C_END)
                        last = pe.matmul(ps[k][:, 0:z - a], hT[:, c, (k // 4) * P:(k // 4) * P + P],
                                         ring[:, slot, a:z], start=(c == 0), stop=(c == NB - 1))
                        if c == NB - 1:
                            last.then_inc(sem("proj_v_done" if k < 4 else "proj_a_done"), 1)
                    if c < NB - 1:
                        last.then_inc(sem(f"ring{slot}_used"), 1)
                pe.wait_ge(sem("proj_a_done"), count.take("proj_a_done", 4))
                pe.sem_inc(sem(f"ring{slot}_used"), 1)
                pe.wait_ge(sem("proj_v"), count.take("proj_v", 4))
                pe.wait_ge(sem("proj_a"), count.take("proj_a", 4))
                for a in range(2):
                    for t in range(NT):
                        last = pe.transpose(ps[0][:, a * S + t * P:a * S + t * P + P],
                                            proj[:, t, C_KC + a * P:C_KC + a * P + P], ident)
                last.then_inc(sem("flow_turned"), 1)
                pe.wait_ge(sem("lora_ready"), count.take("lora_ready"))
                for c in range(3):
                    for t in range(NT):
                        last = pe.transpose(ps[1 + c // 2][:, (c % 2) * S + t * P:(c % 2) * S + t * P + P],
                                            lora[:, t, c * P:(c + 1) * P], ident)
                    if c:
                        last.then_inc(sem("lora_turned"), 1)
                pe.wait_ge(sem("loraT_ready"), count.take("loraT_ready", 2))
                slot = slot_of_turn()
                for t in range(NT):
                    for n, (a, z) in enumerate(((0, HALF), (HALF, 768))):
                        for c in range(2):
                            last = pe.matmul(ps[4 + 2 * t + n][:, 0:z - a], loraT[:, c, t * P:(t + 1) * P],
                                             ring[:, slot, c * 768 + a:c * 768 + z], start=(c == 0), stop=(c == 1))
                    last.then_inc(sem("mq_v_done" if t == 0 else "mq_a_done"), 1)
                pe.wait_ge(sem("mq_a_done"), count.take("mq_a_done"))
                pe.sem_inc(sem(f"ring{slot}_used"), 1)
                slot = slot_of_turn()
                pe.wait_ge(sem("flow_x0_ready"), count.take("flow_x0_ready"))
                for t in range(NT):
                    for n in range(2):
                        last = pe.matmul(ps[2 * t + n][:, :], loraT[:, 2, t * P:(t + 1) * P],
                                         ring[:, slot, n * HALF:(n + 1) * HALF], start=True, stop=True)
                    last.then_inc(sem("mkv_v_done" if t == 0 else "mkv_a_done"), 1)
                pe.wait_ge(sem("mkv_a_done"), count.take("mkv_a_done"))
                pe.sem_inc(sem(f"ring{slot}_used"), 1)
                pe.wait_ge(sem("mq_v"), count.take("mq_v"))
                pe.wait_ge(sem("mq_a"), count.take("mq_a"))
                turn_over(nat, ready="nat_ready")
                pe.wait_ge(sem("mkv_v"), count.take("mkv_v"))
                pe.wait_ge(sem("mkv_a"), count.take("mkv_a"))
                pe.wait_ge(sem("blocks_ready"), count.take("blocks_ready", 4))
                for a in range(2):
                    slots = (slot_of_turn(), slot_of_turn())
                    for b in range(2):
                        for j in range(16):
                            w = ring[:, slots[j // 8], :].rearrange("p (c n) -> p c n", c=8)[:, j % 8, :]
                            last = pe.matmul(ps[0][:, (2 * a + b) * 30:(2 * a + b + 1) * 30], w[:, b * P:(b + 1) * P],
                                             blocks[:, a, j, :], start=(j == 0), stop=(j == 15))
                    last.then_inc(sem("hidden_done"), 1)
                    pe.wait_ge(sem("hidden_done"), count.take("hidden_done"))
                    for slot in slots:
                        pe.sem_inc(sem(f"ring{slot}_used"), 1)
                pe.wait_ge(sem("hidden_ready"), count.take("hidden_ready"))
                for a in range(2):
                    for b in range(2):
                        last = pe.matmul(ps[1][0:30, a * HD:(a + 1) * HD], hidden[:, a, b, :], cmp_w2[:, a, b, :],
                                         start=(b == 0), stop=(b == 1))
                last.then_inc(sem("kcv_done"), 1)
                pe.wait_ge(sem("mqk_ready"), count.take("mqk_ready", 2))
                for n, bank in enumerate((2, 3, 4, 5, 6, 7, 0, 1)):
                    if bank == 1:
                        pe.wait_ge(sem("kc_ready"), count.take("kc_ready"))
                    src = (mq, mk)[n // 4]
                    for head in range(2):
                        for t in range(NT):
                            last = pe.transpose(ps[bank][0:QK, head * S + t * P:head * S + t * P + P],
                                                src[:, t, 2 * (n % 4) + head, :], ident)
                    last.then_inc(sem("m_turned_v" if n % 2 == 0 else "m_turned_a"), 1)
                pe.wait_ge(sem("mT_v"), count.take("mT_v", 4))
                pe.wait_ge(sem("mT_a"), count.take("mT_a", 4))
                pe.transpose(ps[2][:, 0:30], kc_twice, ident[0:30, 0:30]).then_inc(sem("kc_turned"), 1)
                hT_ready()
                pe.wait_ge(sem("kcT_ready"), count.take("kcT_ready"))
                for n in range(4 * NT):
                    for half in range(2):
                        at = slice(64 * half, 64 * half + 64)
                        last = pe.matmul(ps[2 + half][:, n * 30:(n + 1) * 30],
                                         hT[at, n // NT, (n % NT) * P:(n % NT + 1) * P], kcT[at, :],
                                         start=True, stop=True)
                last.then_inc(sem("c_scores_done"), 1)
                pe.wait_ge(sem("c_prob_ready"), count.take("c_prob_ready"))
                for n in range(8 * NT):
                    last = pe.transpose(ps[4 + n // 4][0:30, (n % 4) * P:(n % 4 + 1) * P],
                                        c_prob[:, n * 30:(n + 1) * 30], ident)
                    if n % 4 == 3:
                        last.then_inc(sem("c_turned_v" if n < 8 else "c_turned_a"), 1)
                pe.wait_ge(sem("c_probT_v"), count.take("c_probT_v", 2))
                pe.wait_ge(sem("c_probT_a"), count.take("c_probT_a", 2))
                for n in range(8 * NT):
                    last = pe.matmul(ps[n // 8][:, (n % 8) * HD:(n % 8 + 1) * HD], c_probT[:, n * P:(n + 1) * P],
                                     kcv[:, HD:2 * HD], start=True, stop=True)
                    if n % 8 == 7:
                        last.then_inc(sem("c_weighed"), 1)
                pe.wait_ge(sem("c_out"), count.take("c_out", 2))
                units = [nsa_unit(branch, f) for branch in range(2) for f in range(4)] + [mla_unit(f) for f in range(4)]
                for u in range(len(units) + 1):
                    if u < len(units):
                        scores(units[u][0], units[u][1], ((0, 1), (4, 5))[u % 2])
                    if u:
                        turn_probs((u - 1) % 2)
                        weigh((u - 1) % 2, units[u - 1][2], HD)

            pe.wait_ge(sem("const_landed"), count.take("const_landed", 16))
            pe.wait_ge(sem("x_landed"), count.take("x_landed", 32))
            pe.wait_ge(sem("bias_in_landed"), count.take("bias_in_landed", 32))
            pe.wait_ge(sem("relb_set"), count.take("relb_set"))
            pe.matmul(ps[0][0:HEADS, 0:384], relb_sb, bucket_sb, start=True, stop=True).then_inc(sem("bias_rows_ready"), 1)
            turn_over(h)
            attention_layer(P)
            turn_over(nat, ready="nat_ready", split=True)
            split_natural()
            turn_over(h, ready="h_ready", split=True)
            mlp()
            turn_over(h, ready="h_ready")
            attention_layer(HD)
            turn_over(nat, ready="nat_ready", split=True)
            split_natural()
            turn_over(h, ready="h_ready", split=True)
            mlp()
            turn_over(nat, ready="nat_ready")
            hybrid_attention()
            turn_over(nat, ready="nat_ready")
            natural()
            pe.wait_ge(sem("keys_landed"), count.take("keys_landed", 16))
            for b in range(2 * P_HEADS):
                last = pe.transpose(ps[4 + b // 4][:, (b % 4) * P:(b % 4 + 1) * P], keys[:, b, :], ident)
                if b % 4 == 3:
                    last.then_inc(sem("keys_turned"), 1)
            pe.wait_ge(sem("keysT_ready"), count.take("keysT_ready", 4))
            turn_over(nat, ready="nat_ready")
            peer()

        @block.scalar
        def _(sc):
            count = Count(sc)

            def take_turned():
                for c in range(2, 4):
                    sc.wait_ge(sem("turned_a"), count.take("turned_a"))
                    sc.activation(hT[:, 2 * c:2 * c + 2, :], ps[4 + c][:, :].rearrange("p (c s) -> p c s", c=2), ACT.Copy)\
                        .then_inc(sem("hT_a"), 1)

            def take_turned_high():
                for c in range(4):
                    sc.wait_ge(sem("turned_s"), count.take("turned_s"))
                    sc.activation(hT_high[:, 2 * c:2 * c + 2, :], ps[4 + c][:, :].rearrange("p (c s) -> p c s", c=2),
                                  ACT.Copy).then_inc(sem("hT_high"), 1)

            def split_high(slot, pair, free=None):
                sc.wait_ge(sem(f"raw{slot}_landed"), count.take(f"raw{slot}_landed", 16))
                if free:
                    sc.wait_ge(sem(free), count.take(free))
                for half in range(2):
                    part = slice(half * D, (half + 1) * D)
                    sc.activation(w_split[pair][0][:, part], ring[:, slot, part], ACT.Copy)\
                        .then_inc(sem("w_high"), 1)

            def exps(b):
                for m in range(2):
                    for t, (a, z) in enumerate(((0, P), (P, 384))):
                        sc.wait_ge(sem("sco_ready"), count.take("sco_ready"))
                        sc.activation(prob[:, b, m, a:z], sco[:, b, m, a:z], ACT.Exp, bias=peak[:, b, m, t:t + 1],
                                      scale=-1.0, accum_out=total[:, b, m, t:t + 1]).then_inc(sem("probs_ready"), 1)

            def take_probT():
                sc.wait_ge(sem("probT_a_turned"), count.take("probT_a_turned"))
                sc.activation(probT[:, 1, :], ps[3][:, 0:384], ACT.Copy).then_inc(sem("probT_a"), 1)

            def take_projection(b, part):
                sc.wait_ge(sem("proj_ready"), count.take("proj_ready"))
                sc.activation(qkT[:, b, part, :], ps[4 + part][:, 0:S], ACT.Copy,
                              scale=-(HD ** -0.5) if part == 0 else 1.0).then_inc(sem("qkT_ready"), 1)

            def attend_block(b, more=True):
                exps(b)
                if more:
                    take_projection(1 - b, 0)
                take_probT()
                if more:
                    take_projection(1 - b, 1)

            def attention_layer():
                count.skip("acc_ready", 2)
                for k in range(2):
                    sc.wait_ge(sem("acc_ready"), count.take("acc_ready"))
                    sc.activation(val[:, 1, k * HALF:(k + 1) * HALF], ps[2 + k][:, :], ACT.Copy).then_inc(sem("val_a"), 1)
                take_projection(0, 0)
                take_projection(0, 1)
                with count.loop(3, sco_ready=8, proj_ready=4, probT_a_turned=2):
                    attend_block(0)
                    attend_block(1)
                attend_block(0)
                attend_block(1, more=False)

            def out_and_mlp(first=False):
                split_high(0, 0)
                split_high(1, 1, None if first else "w1_used")
                take_turned_high()
                split_high(2, 0, "w0_used")
                split_high(3, 1, "w1_used")
                split_high(0, 0, "w0_used")
                count.skip("acc_ready", 4)
                take_turned_high()
                split_high(1, 1, "w1_used")

                def step(b, more=True, first=False):
                    if more:
                        split_high(2 - 2 * b, 0, "up_ready")
                    else:
                        sc.wait_ge(sem("up_ready"), count.take("up_ready"))
                    sc.activation(relu[:, b, :], ps[4 + b][:, :], ACT.Relu).then_inc(sem("relu_ready"), 1)
                    sc.wait_ge(sem("relu_ready"), count.take("relu_ready"))
                    sc.activation(act_high[:, b, :], relu[:, b, :], ACT.Square).then_inc(sem("act_high"), 1)
                    if not first:
                        split_high(2 * b + 1, 1, "w1_used")

                step(0, first=True)
                with count.loop(N_CHUNK // 2 - 1, up_ready=2, relu_ready=2, w1_used=2, raw0_landed=16, raw1_landed=16,
                                raw2_landed=16, raw3_landed=16):
                    step(1)
                    step(0)
                step(1, more=False)
                count.skip("acc_ready", 4)

            def take_queries():
                for half in range(2):
                    sc.wait_ge(sem("peer_q_done"), count.take("peer_q_done"))
                    for dst, func in ((pq, ACT.Copy), (pq_sq, ACT.Square)):
                        sc.activation(dst[:, half * S:(half + 1) * S], ps[4 + half][:, 0:S], func)\
                            .then_inc(sem("pq_ready"), 1)

            def diagonals(b, ks, first=False):
                for k in ks:
                    if k >= 4 or not first:
                        sc.wait_ge(sem("v_used"), count.take("v_used"))
                    sc.activation(diag[:, k % 4, :], ident, ACT.Copy, scale=weight[:, 16 * b + k:16 * b + k + 1])\
                        .then_inc(sem("diag_ready"), 1)

            def gates_of(b):
                sc.wait_ge(sem("top_ready"), count.take("top_ready"))
                sc.activation(gate_w[:, 16 * b:16 * b + 16], top, ACT.Exp, bias=neg_top, accum_out=mass[:, b:b + 1])\
                    .then_inc(sem("gate_w_ready"), 1)

            def gelu_of():
                sc.wait_ge(sem("dot_done"), count.take("dot_done", 16))
                sc.activation(gelu, dots, ACT.Gelu_apprx_tanh).then_inc(sem("gelu_ready"), 1)

            def unit(t, queries=False, ahead=True, first=False):
                sc.wait_ge(sem("weight_ready"), count.take("weight_ready"))
                diagonals(1 - t, range(8), first)
                if queries:
                    take_queries()
                if ahead:
                    gates_of(1 - t)
                diagonals(1 - t, range(8, TOPK))
                gelu_of()

            def peer():
                take_queries()
                gates_of(0)
                take_queries()
                gates_of(1)
                gelu_of()
                unit(1, first=True)
                unit(0, queries=True)
                with count.loop(P_HEADS - 3, weight_ready=2, v_used=32, peer_q_done=2, top_ready=2, dot_done=32):
                    unit(1)
                    unit(0, queries=True)
                unit(1)
                unit(0)
                unit(1, ahead=False)
                sc.wait_ge(sem("weight_ready"), count.take("weight_ready"))
                diagonals(1, range(TOPK))

            def hybrid_attention():
                sc.wait_ge(sem("reduced_ready"), count.take("reduced_ready"))
                sc.activation(trig, reduced, ACT.Sin).then_inc(sem("trig_ready"), 1)
                for k in range(4):
                    a = k * HALF
                    z = min(a + HALF, C_END)
                    sc.wait_ge(sem("proj_a_done"), count.take("proj_a_done"))
                    sc.activation(sq[:, 1, a:z], ps[4 + k][:, 0:z - a], ACT.Square).then_inc(sem("sq_a"), 1)
                    sc.activation(proj[:, 1, a:z], ps[4 + k][:, 0:z - a], ACT.Copy).then_inc(sem("proj_a"), 1)
                sc.wait_ge(sem("proj_v"), count.take("proj_v", 4))
                sc.wait_ge(sem("proj_a"), count.take("proj_a", 4))
                sc.activation(gates.rearrange("p (t n) -> p t n", t=NT), proj[:, :, C_GATE:C_CQ], ACT.Sigmoid)\
                    .then_inc(sem("gates_ready"), 1)
                sc.wait_ge(sem("lora_turned"), count.take("lora_turned"))
                sc.activation(loraT[:, 0:2, :], ps[1][:, :].rearrange("p (c s) -> p c s", c=2), ACT.Copy)\
                    .then_inc(sem("loraT_ready"), 1)
                sc.wait_ge(sem("lora_turned"), count.take("lora_turned"))
                sc.activation(loraT[:, 2, :], ps[2][:, 0:S], ACT.Copy).then_inc(sem("loraT_ready"), 1)
                sc.wait_ge(sem("mq_a_done"), count.take("mq_a_done"))
                q1 = mq[:, 1, :, :].rearrange("p h n -> p (h n)")
                sc.activation(q1[:, 0:HALF], ps[6][:, :], ACT.Copy)
                sc.activation(q1[:, HALF:768], ps[7][:, 0:256], ACT.Copy).then_inc(sem("mq_a"), 1)
                sc.wait_ge(sem("mkv_a_done"), count.take("mkv_a_done"))
                for n in range(2):
                    kv = ps[2 + n][:, :].rearrange("p (h n) -> p h n", n=P)
                    sc.activation(mk[:, 1, 4 * n:4 * n + 4, 0:HD], kv[:, :, 0:HD], ACT.Copy)
                    last = sc.activation(val[:, 1, n * 256:(n + 1) * 256].rearrange("p (h n) -> p h n", n=HD),
                                         kv[:, :, HD:P], ACT.Copy)
                last.then_inc(sem("mkv_a"), 1)
                take_turned()
                sc.wait_ge(sem("hidden_done"), count.take("hidden_done", 2))
                sc.activation(hidden.rearrange("p a b n -> p (a b n)"), ps[0][:, 0:120], ACT.Gelu_apprx_tanh)\
                    .then_inc(sem("hidden_ready"), 1)
                for n in (1, 3, 5, 7):
                    sc.wait_ge(sem("m_turned_a"), count.take("m_turned_a"))
                    bank = (2, 3, 4, 5, 6, 7, 0, 1)[n]
                    sc.activation((mqT, mkT)[n // 4][:, 2 * (n % 4):2 * (n % 4) + 2, :],
                                  ps[bank][0:QK, :].rearrange("p (h s) -> p h s", h=2), ACT.Copy).then_inc(sem("mT_a"), 1)
                sc.wait_ge(sem("c_sco_ready"), count.take("c_sco_ready"))
                sc.activation(c_prob, c_sco, ACT.Exp, scale=-1.0).then_inc(sem("c_prob_ready"), 1)
                for n in range(2):
                    sc.wait_ge(sem("c_turned_a"), count.take("c_turned_a"))
                    sc.activation(c_probT[:, (2 + n) * HALF:(3 + n) * HALF], ps[6 + n][0:30, :], ACT.Copy)\
                        .then_inc(sem("c_probT_a"), 1)
                for u in range(13):
                    if u < 12:
                        exps(u % 2)
                    if u:
                        take_probT()

            sc.wait_ge(sem("lam_summed"), count.take("lam_summed", 2))
            sc.activation(lam_exp[:, 0:2], lam_sum, ACT.Exp).then_inc(sem("lam_exp"), 1)
            sc.wait_ge(sem("bias_rows_ready"), count.take("bias_rows_ready"))
            sc.activation(bias_rows, ps[0][0:HEADS, 0:384], ACT.Copy).then_inc(sem("bias_rows_set"), 1)
            take_turned()
            attention_layer()
            out_and_mlp(first=True)
            take_turned()
            attention_layer()
            out_and_mlp()
            take_turned()
            hybrid_attention()
            take_turned()
            count.skip("acc_ready", 4)
            for n in range(4):
                sc.wait_ge(sem("keys_turned"), count.take("keys_turned"))
                sc.activation(keysT[:, n * HALF:(n + 1) * HALF], ps[4 + n][:, :], ACT.Copy)\
                    .then_inc(sem("keysT_ready"), 1)
            take_turned()
            peer()

        @block.gpsimd
        def _(po):
            count = Count(po)
            po.dma_start(bucket_sb, T["buckets"]).then_inc(sem("bias_in_landed"), 16)
            po.dma_start(relb_sb[0:32, :], T["rel_bias"]).then_inc(sem("bias_in_landed"), 16)
            po.dma_start(lam_in, to_partitions(T["lam_a"][0].rearrange("a d -> (a d)"))).then_inc(sem("lam_landed"), 16)
            po.dma_start(subln, to_partitions(T["subln_a"][0])).then_inc(sem("subln_landed"), 16)
            po.memset(neg_half, -0.5).then_inc(sem("neg_half_set"), 1)
            po.wait_ge(sem("neg_half_set"), count.take("neg_half_set"))
            po.memset(pos_i[:, :], 0).then_inc(sem("pos_cleared"), 1)
            po.wait_ge(sem("pos_cleared"), count.take("pos_cleared"))
            pos = T["positions_2"]
            loads = [(pos_i[:, 0:2], bass.AP(pos.tensor, 0, [[1, P], [P, NT]])),
                     (pos_i[0:15, 2:3], bass.AP(pos.tensor, 31, [[16, N_CMP], [1, 1]])),
                     (pos_i[15:30, 2:3], bass.AP(pos.tensor, 31, [[16, N_CMP], [1, 1]])),
                     (freqs, to_partitions(T["freqs"])), (gain_q, to_partitions(T["nsa_q_gain_2"][0])),
                     (gain_ks, to_partitions(T["nsa_ks_gain_2"][0])), (gain_kw, to_partitions(T["nsa_kw_gain_2"][0])),
                     (gain_kc, to_partitions(T["nsa_kc_gain_2"][0])), (gain_mq, to_partitions(T["mla_q_gain_2"][0])),
                     (gain_mk, to_partitions(T["mla_k_gain_2"][0])), (gain_cq, to_partitions(T["mla_q_lora_gain_2"][0])),
                     (gain_ckv, to_partitions(T["mla_kv_lora_gain_2"][0])),
                     (wide_gain[:, 0, :], to_partitions(T["norm1_gain_2"][0])),
                     (wide_gain[:, 1, 0:HALF], to_partitions(T["out_gain_a_2"][0])),
                     (wide_gain[:, 1, HALF:D], to_partitions(T["out_gain_b_2"][0])),
                     (wide_gain[:, 2, :], to_partitions(T["norm2_gain_2"][0])),
                     (cmp_posT[0:HD, :], bass.AP(T["cmp_pos_2"].tensor, 0, [[1, HD], [2 * HD, 16]])),
                     (cmp_posT[HD:P, :], bass.AP(T["cmp_pos_2"].tensor, HD, [[1, HD], [2 * HD, 16]])),
                     (cmp_w2[:, 0, :, :], T["cmp_k_w2_2"][0].rearrange("(b p) n -> p b n", p=P)),
                     (cmp_w2[:, 1, :, :], T["cmp_v_w2_2"][0].rearrange("(b p) n -> p b n", p=P))]
            assert len(loads) == N_SMALL
            for dst, src in loads:
                po.dma_start(dst, src, allow_slow_non_contiguous=True).then_inc(sem("small_landed"), 16)
            po.wait_ge(sem("bias_rows_set"), count.take("bias_rows_set"))
            po.dma_start(scratch, bias_rows).then_inc(sem("scratch_stored"), 16)
            po.wait_ge(sem("scratch_stored"), count.take("scratch_stored", 16))
            pitch = HEADS * 384
            po.dma_start(bass.AP(shifted.tensor, 0, [[pitch + 1, P], [1, pitch]]),
                         bass.AP(scratch.tensor, 0, [[0, P], [1, pitch]])).then_inc(sem("shifted_stored"), 16)
            po.wait_ge(sem("shifted_stored"), count.take("shifted_stored", 16))
            for first, n, at in ((255, P, 0), (127, S, P)):
                src = bass.AP(shifted.tensor, first, [[pitch, P], [384, HEADS], [1, n]])
                po.dma_start(bias[:, :, at:at + n], src).then_inc(sem("bias_landed"), 16)
            for s, (g, b, layer) in enumerate((("ln1_g", "ln1_b", 0), ("ln2_g", "ln2_b", 0), ("ln1_g", "ln1_b", 1),
                                               ("ln2_g", "ln2_b", 1))):
                po.dma_start(ln_gb[:, s, 0, :], to_partitions(T[g][layer])).then_inc(sem(f"ln{s}_landed"), 16)
                po.dma_start(ln_gb[:, s, 1, :], to_partitions(T[b][layer])).then_inc(sem(f"ln{s}_landed"), 16)

            def power(dst, src, ready, done):
                po.wait_ge(sem(ready), count.take(ready))
                po.tensor_tensor(dst, src, neg_half[:, 0:src.shape[-1]] if len(src.shape) == 2 else neg_half, ALU.pow)\
                    .then_inc(sem(done), 1)

            def layer_norm():
                for t in range(NT):
                    power(rstd[:, t:t + 1], var_eps[:, t:t + 1], "var_ready", "rstd_ready")

            power(ms_out[:, 0:16], ms_in[:, 0:16], "ms_ready", "rms_ready")
            layer_norm()
            layer_norm()
            layer_norm()
            layer_norm()
            def rms(n, w):
                power(ms_out[:, n:n + w], ms_in[:, n:n + w], "ms_ready", "rms_ready")

            po.wait_ge(sem("small_landed"), count.take("small_landed", 16 * N_SMALL))
            rms(0, 1)
            rms(1, 1)
            rms(24, 4)
            po.wait_ge(sem("flow_x0_ready"), count.take("flow_x0_ready"))
            for g in range(2):
                for r in range(2):
                    po.dma_start(flow_x[64 * r:64 * r + 64, :, g, :], flow_x0[64 * g:64 * g + 64, :, r, :])\
                        .then_inc(sem("flow_landed"), 16)
            rms(0, 24)
            po.wait_ge(sem("flow_landed"), count.take("flow_landed", 64))
            for a in range(2):
                for g in range(2):
                    po.tensor_tensor(blocks[:, a, :, 15 * g:15 * g + 15], spread(flow_x[:, a, g, :], (1, 16), (8, 15)),
                                     spread(cmp_posT, (1, 16), (0, 15)), ALU.add).then_inc(sem("blocks_ready"), 1)
            rms(0, 16)
            rms(16, 16)
            po.wait_ge(sem("kc_ms_ready"), count.take("kc_ms_ready"))
            po.tensor_tensor(rstd[0:30, 0:1], var_eps[0:30, 0:1], neg_half[0:30, 0:1], ALU.pow)\
                .then_inc(sem("kc_rms_ready"), 1)
            for n in range(4):
                rms(n, 1)
            rms(0, 1)
            rms(1, 1)
            def gather(table, rows_of, k, ring_of, name, wait):
                if wait:
                    po.wait_ge(sem("dot_done" if name == "u" else "v_used"), count.take("dot_done" if name == "u" else "v_used"))
                    alone()
                po.indirect_dma_start(ring_of[:, k % RING, :], None, table,
                                      bass.IndirectOffsetOnAxis(ap=rows_of[:, k:k + 1], axis=0))\
                    .then_inc(sem(f"{name}{k % RING}_landed"), 16)

            def alone():
                po.sem_inc(sem("gathers_due"), 1)

            peer_u, peer_v = T["peer_u_2"][0], T["peer_v_2"][0]

            def unit(t, add=True, power_at=None, u_first=False, v_first=False, dot=True):
                if dot:
                    po.wait_ge(sem("experts_ready"), count.take("experts_ready"))
                    alone()
                for k in range(TOPK + U_LEAD):
                    if add and k == U_LEAD:
                        po.wait_ge(sem("weight_ready"), count.take("weight_ready"))
                        alone()
                    if dot and k < TOPK:
                        gather(peer_u, expert_u[:, 16 * t:16 * t + 16], k, arena_u, "u", k >= RING or not u_first)
                    if add and k >= U_LEAD:
                        gather(peer_v, expert_v[:, 16 * (1 - t):16 * (1 - t) + 16], k - U_LEAD, arena_v, "v",
                               k - U_LEAD >= RING or not v_first)
                    if k == power_at:
                        power(ms_out[:, 0:2], ms_in[:, 0:2], "ms_ready", "rms_ready")

            power(ms_out[:, 0:2], ms_in[:, 0:2], "ms_ready", "rms_ready")
            po.wait_ge(sem("keysT_ready"), count.take("keysT_ready", 4))
            unit(0, add=False, u_first=True)
            unit(1, power_at=U_LEAD + 3, v_first=True)
            unit(0)
            with count.loop(P_HEADS - 2, experts_ready=2, weight_ready=2, dot_done=32, v_used=32, ms_ready=1):
                unit(1, power_at=U_LEAD + 3)
                unit(0)
            unit(1)
            unit(0, dot=False)

        @block.vector
        def _(ve):
            count = Count(ve)

            def then(ins):
                ins.then_inc(sem("v_chain"), 1)
                ve.wait_ge(sem("v_chain"), count.take("v_chain"))

            def take_turned():
                for c in range(2):
                    ve.wait_ge(sem("turned_v"), count.take("turned_v"))
                    ve.tensor_copy(hT[:, 2 * c:2 * c + 2, :], ps[4 + c][:, :].rearrange("p (c s) -> p c s", c=2))\
                        .then_inc(sem("hT_v"), 1)

            def take_turned_low():
                for c in range(4):
                    ve.wait_ge(sem("hT_high"), count.take("hT_high"))
                    part = slice(2 * c, 2 * c + 2)
                    ve.tensor_tensor(hT_low[:, part, :], ps[4 + c][:, :].rearrange("p (c s) -> p c s", c=2),
                                     hT_high[:, part, :].bitcast(F32), ALU.subtract).then_inc(sem("hT_split"), 1)

            def split_low(slot, pair):
                for half in range(2):
                    ve.wait_ge(sem("w_high"), count.take("w_high"))
                    part = slice(half * D, (half + 1) * D)
                    ve.tensor_tensor(w_split[pair][1][:, part], ring[:, slot, part],
                                     w_split[pair][0][:, part].bitcast(F32), ALU.subtract)\
                        .then_inc(sem(f"w{pair}_split"), 1)

            def add_bias(b, banks, table):
                for m in range(2):
                    ve.wait_ge(sem("scores_ready"), count.take("scores_ready"))
                    for t, (a, z) in enumerate(((0, P), (P, 384))):
                        ve.tensor_tensor_reduce(sco[:, b, m, a:z], ps[banks[m]][:, a:z], table(m)[:, a:z], 1.0, 3e38,
                                                ALU.add, ALU.min, peak[:, b, m, t:t + 1]).then_inc(sem("sco_ready"), 1)

            def add_moving_bias(b, table):
                for m in range(2):
                    ve.wait_ge(sem("scores_ready"), count.take("scores_ready"))
                    then(ve.tensor_tensor(sco[:, b, m, :], ps[m][:, 0:384], table(m), ALU.add))
                    for t, (a, z) in enumerate(((0, P), (P, 384))):
                        ve.tensor_reduce(peak[:, b, m, t:t + 1], sco[:, b, m, a:z], X, ALU.min)\
                            .then_inc(sem("sco_ready"), 1)

            def take_probT(b):
                ve.wait_ge(sem("probT_v_turned"), count.take("probT_v_turned"))
                ve.tensor_copy(probT[:, 0, :], ps[2][:, 0:384]).then_inc(sem("probT_v"), 1)

            def differential(f, b):
                ve.wait_ge(sem("probs_ready"), count.take("probs_ready", 4))
                then(ve.reciprocal(share[:, b, :, :], total[:, b, :, :]))
                then(ve.tensor_scalar(share[:, b, 1, :], share[:, b, 1, :], lam_exp[:, 2:3], None, ALU.mult))
                ve.wait_ge(sem("weighed"), count.take("weighed"))
                for t in range(NT):
                    then(ve.tensor_scalar(omap[:, t, :], ps[6 + b][:, (2 + t) * P:(3 + t) * P], share[:, b, 1, t:t + 1],
                                          None, ALU.mult))
                for t in range(NT):
                    last = ve.scalar_tensor_tensor(out=nat[:, t, bass.ds(f * P, P)], in0=ps[6 + b][:, t * P:(t + 1) * P],
                                                   scalar=share[:, b, 0, t:t + 1], in1=omap[:, t, :], op0=ALU.mult,
                                                   op1=ALU.add)
                then(last)

            def plain(f, b):
                ve.wait_ge(sem("probs_ready"), count.take("probs_ready", 4))
                then(ve.reciprocal(share[:, b, :, :], total[:, b, :, :]))
                ve.wait_ge(sem("weighed"), count.take("weighed"))
                for m in range(2):
                    for t in range(NT):
                        last = ve.tensor_scalar(nat[:, t, bass.ds(f * P + m * HD, HD)],
                                                ps[6 + b][:, (2 * m + t) * HD:(2 * m + t + 1) * HD],
                                                share[:, b, m, t:t + 1], None, ALU.mult)
                then(last)

            def attend_block(f, b, finish):
                add_moving_bias(b, lambda m: bias[:, bass.ds(f * 2 + m, 1), :].rearrange("p a k -> p (a k)"))
                take_probT(b)
                finish(f, b)

            def attention_layer(finish, chained):
                for k in range(2):
                    ve.wait_ge(sem("acc_ready"), count.take("acc_ready"))
                    ve.tensor_copy(val[:, 0, k * HALF:(k + 1) * HALF], ps[k][:, :]).then_inc(sem("val_v"), 1)
                count.skip("acc_ready", 2)
                with count.loop(4, scores_ready=4, probs_ready=8, probT_v_turned=2, weighed=2, v_chain=chained) as i:
                    for b in range(2):
                        attend_block(i * 2 + b, b, finish)

            def add_residual(scale, then_do=lambda t: None):
                for t in range(NT):
                    for k in range(2):
                        ve.wait_ge(sem("acc_ready"), count.take("acc_ready"))
                        part = h[:, t, k * HALF:(k + 1) * HALF]
                        then(ve.scalar_tensor_tensor(out=part, in0=part, scalar=scale, in1=ps[2 * t + k][:, :],
                                                     op0=ALU.mult, op1=ALU.add))
                    then_do(t)

            def layer_norm(s):
                ve.wait_ge(sem(f"ln{s}_landed"), count.take(f"ln{s}_landed", 32))
                for t in range(NT):
                    for k in range(2):
                        ve.wait_ge(sem("acc_ready"), count.take("acc_ready"))
                        part = h[:, t, k * HALF:(k + 1) * HALF]
                        then(ve.scalar_tensor_tensor(out=part, in0=part, scalar=ALPHA, in1=ps[2 * t + k][:, :],
                                                     op0=ALU.mult, op1=ALU.add))
                        then(ve.bn_stats(stats[:, 6 * k:6 * k + 6], part))
                    then(ve.bn_aggr(moments[:, 2 * t:2 * t + 2], stats[:, 0:12].rearrange("p (k s) -> p k s", k=2)))
                    ve.tensor_scalar(var_eps[:, t:t + 1], moments[:, 2 * t + 1:2 * t + 2], LN_EPS, None, ALU.add)\
                        .then_inc(sem("var_ready"), 1)
                    then(ve.scalar_tensor_tensor(out=h[:, t, :], in0=h[:, t, :], scalar=moments[:, 2 * t:2 * t + 1],
                                                 in1=ln_gb[:, s, 0, :], op0=ALU.subtract, op1=ALU.mult))
                    ve.wait_ge(sem("rstd_ready"), count.take("rstd_ready"))
                    ve.scalar_tensor_tensor(out=h[:, t, :], in0=h[:, t, :], scalar=rstd[:, t:t + 1],
                                            in1=ln_gb[:, s, 1, :], op0=ALU.mult, op1=ALU.add).then_inc(sem("h_ready"), 1)

            def out_and_mlp(s):
                split_low(0, 0)
                split_low(1, 1)
                take_turned_low()
                split_low(2, 0)
                split_low(3, 1)
                split_low(0, 0)
                layer_norm(s)
                take_turned_low()
                split_low(1, 1)

                def step(b, more=True, first=False):
                    if more:
                        split_low(2 - 2 * b, 0)
                    ve.wait_ge(sem("relu_ready"), count.take("relu_ready"))
                    then(ve.tensor_tensor(act_sq[:, b, :], relu[:, b, :], relu[:, b, :], ALU.mult))
                    ve.wait_ge(sem("act_high"), count.take("act_high"))
                    ve.tensor_tensor(act_low[:, b, :], act_sq[:, b, :], act_high[:, b, :].bitcast(F32), ALU.subtract)\
                        .then_inc(sem("act_ready"), 1)
                    if not first:
                        split_low(2 * b + 1, 1)

                step(0, first=True)
                with count.loop(N_CHUNK // 2 - 1, w_high=8, relu_ready=2, act_high=2, v_chain=2):
                    step(1)
                    step(0)
                step(1, more=False)
                layer_norm(s + 1)

            def rms_of(src, at, width, n_cols=1):
                for n in range(n_cols):
                    a = n * width
                    then(ve.tensor_tensor_reduce(tmp[:, 0, 0:width], src[:, a:a + width], src[:, a:a + width], 1.0, 0.0,
                                                 ALU.mult, ALU.add, sq_sum[:, at + n:at + n + 1]))
                ve.tensor_scalar(ms_in[:, at:at + n_cols], sq_sum[:, at:at + n_cols], 1.0 / width, EPS, ALU.mult,
                                 ALU.add).then_inc(sem("ms_ready"), 1)

            def wide_norm(gain, has_rms=False):
                if not has_rms:
                    for t in range(NT):
                        rms_of(h[:, t, :], t, D)
                for t in range(NT):
                    ve.wait_ge(sem("rms_ready"), count.take("rms_ready"))
                    ve.scalar_tensor_tensor(out=nat[:, t, :], in0=h[:, t, :], scalar=ms_out[:, t:t + 1],
                                            in1=wide_gain[:, gain, :], op0=ALU.mult, op1=ALU.mult)\
                        .then_inc(sem("nat_ready"), 1)

            def rope(x1, x2, c, s, shape):
                n = shape[0] * shape[1] * shape[2]
                steps = (shape[1] * shape[2], shape[0]), (shape[2], shape[1]), (1, shape[2])
                t = [spread(rope_tmp[0:x1.shape[0], k, :], *steps) for k in range(4)]
                for k, (u, v) in enumerate(((x1, c), (x2, s), (x2, c), (x1, s))):
                    then(ve.tensor_tensor(t[k], u, v, ALU.mult))
                then(ve.tensor_tensor(x1, t[0], t[1], ALU.subtract))
                then(ve.tensor_tensor(x2, t[2], t[3], ALU.add))

            def angles():
                then(ve.tensor_copy(pos_f, pos_i[:, :]))
                then(ve.tensor_tensor(spread(angle, (24, 3), (1, 24)), spread(pos_f, (1, 3), (0, 24)),
                                      spread(freqs, (0, 3), (1, 24)), ALU.mult))
                for n, phase in enumerate((0.25, 0.0)):
                    then(ve.tensor_scalar(cycles[:, 72 * n:72 * n + 72], angle, 1 / (2 * math.pi), phase, ALU.mult, ALU.add))
                    then(ve.tensor_copy(reduced[:, 72 * n:72 * n + 72], angle))
                then(ve.tensor_scalar(cycles, cycles, 1.5 * 2 ** 23, None, ALU.add))
                then(ve.tensor_scalar(cycles, cycles, -1.5 * 2 ** 23, None, ALU.add))
                rest = 2 * math.pi
                for bits in (2, 10, 18, None):
                    part = rest if bits is None else math.floor(rest * 2 ** bits) / 2 ** bits
                    rest -= part
                    then(ve.scalar_tensor_tensor(out=reduced, in0=cycles, scalar=-part, in1=reduced, op0=ALU.mult,
                                                 op1=ALU.add))
                then(ve.tensor_scalar(reduced[:, 0:72], reduced[:, 0:72], math.pi / 2, None, ALU.add))
                limit = float(np.nextafter(np.float32(math.pi), np.float32(0)))
                ve.tensor_scalar(reduced, reduced, limit, -limit, ALU.min, ALU.max).then_inc(sem("reduced_ready"), 1)

            def hybrid_attention():
                for k in range(4):
                    a = k * HALF
                    z = min(a + HALF, C_END)
                    ve.wait_ge(sem("proj_v_done"), count.take("proj_v_done"))
                    ve.tensor_copy(proj[:, 0, a:z], ps[k][:, 0:z - a]).then_inc(sem("proj_v"), 1)
                    ve.wait_ge(sem("proj_v"), count.take("proj_v"))
                then(ve.tensor_tensor(sq[:, 0, C_CQ:C_KR], proj[:, 0, C_CQ:C_KR], proj[:, 0, C_CQ:C_KR], ALU.mult))
                ve.wait_ge(sem("sq_a"), count.take("sq_a", 4))
                ve.tensor_reduce(sq_sum[:, 24:26], sq[:, :, C_CQ:C_CKV], X, ALU.add)
                then(ve.tensor_reduce(sq_sum[:, 26:28], sq[:, :, C_CKV:C_KR], X, ALU.add))
                then(ve.tensor_scalar(ms_in[:, 24:26], sq_sum[:, 24:26], 1.0 / 256, EPS, ALU.mult, ALU.add))
                ve.tensor_scalar(ms_in[:, 26:28], sq_sum[:, 26:28], 1.0 / 128, EPS, ALU.mult, ALU.add)\
                    .then_inc(sem("ms_ready"), 1)
                ve.wait_ge(sem("flow_turned"), count.take("flow_turned"))
                for a in range(2):
                    last = ve.tensor_copy(flow_x0[:, a, :, :].rearrange("p r i -> p i r"),
                                          ps[0][:, a * S:(a + 1) * S].rearrange("p (i r) -> p i r", r=2))
                then(last)
                ve.sem_inc(sem("flow_x0_ready"), 2)
                ve.tensor_tensor(sq[:, 0, C_Q:C_KC], proj[:, 0, C_Q:C_KC], proj[:, 0, C_Q:C_KC], ALU.mult)
                then(ve.tensor_tensor(sq[:, 0, C_KS:C_VW], proj[:, 0, C_KS:C_VW], proj[:, 0, C_KS:C_VW], ALU.mult))
                for t in range(NT):
                    ve.tensor_reduce(sq_sum[:, 12 * t:12 * t + 8], sq[:, t, C_Q:C_KC].rearrange("p (g d) -> p g d", d=HD),
                                     X, ALU.add)
                    for n, at in enumerate((C_KS, C_KW)):
                        last = ve.tensor_reduce(sq_sum[:, 12 * t + 8 + 2 * n:12 * t + 10 + 2 * n],
                                                sq[:, t, at:at + P].rearrange("p (g d) -> p g d", d=HD), X, ALU.add)
                then(last)
                ve.tensor_scalar(ms_in[:, 0:24], sq_sum[:, 0:24], 1.0 / HD, EPS, ALU.mult, ALU.add)\
                    .then_inc(sem("ms_ready"), 1)
                ve.wait_ge(sem("rms_ready"), count.take("rms_ready"))
                ve.wait_ge(sem("proj_a"), count.take("proj_a", 4))
                for t in range(NT):
                    ve.scalar_tensor_tensor(out=lora[:, t, 0:256], in0=proj[:, t, C_CQ:C_CKV],
                                            scalar=ms_out[:, 24 + t:25 + t], in1=gain_cq, op0=ALU.mult, op1=ALU.mult)
                    last = ve.scalar_tensor_tensor(out=lora[:, t, 256:384], in0=proj[:, t, C_CKV:C_KR],
                                                   scalar=ms_out[:, 26 + t:27 + t], in1=gain_ckv, op0=ALU.mult,
                                                   op1=ALU.mult)
                last.then_inc(sem("lora_ready"), 1)
                ve.wait_ge(sem("rms_ready"), count.take("rms_ready"))
                for t in range(NT):
                    q = nat[:, t, 0:HALF].rearrange("p (g d) -> p g d", d=HD)
                    then(ve.tensor_tensor(q, proj[:, t, C_Q:C_KC].rearrange("p (g d) -> p g d", d=HD),
                                          spread(ms_out[:, 12 * t:12 * t + 8], (1, 8), (0, HD)), ALU.mult))
                    then(ve.tensor_tensor(q, q, spread(gain_q, (0, 8), (1, HD)), ALU.mult))
                    for n, (at, group, gain) in enumerate(((C_KS, 8, gain_ks), (C_KW, 10, gain_kw))):
                        k = nat[:, t, HALF + 256 * n:HALF + 256 * n + 256].rearrange("p (g c d) -> p g c d", g=2, c=2)
                        then(ve.tensor_tensor(k[:, :, 0, :], proj[:, t, at:at + P].rearrange("p (g d) -> p g d", d=HD),
                                              spread(ms_out[:, 12 * t + group:12 * t + group + 2], (1, 2), (0, HD)), ALU.mult))
                        then(ve.tensor_tensor(k[:, :, 0, :], k[:, :, 0, :], spread(gain, (0, 2), (1, HD)), ALU.mult))
                        then(ve.tensor_copy(k[:, :, 1, :], k[:, :, 0, :]))
                ve.wait_ge(sem("trig_ready"), count.take("trig_ready"))
                x = nat[:, :, :].rearrange("p t (g d) -> p t g d", d=HD)
                rope(x[:, :, :, 0:8], x[:, :, :, 8:16], spread(cos, (24, NT), (0, 16), (1, 8)),
                     spread(sin, (24, NT), (0, 16), (1, 8)), (NT, 16, 8))
                ve.sem_inc(sem("nat_ready"), 2)
                ve.wait_ge(sem("mq_v_done"), count.take("mq_v_done"))
                q0 = mq[:, 0, :, :].rearrange("p h n -> p (h n)")
                ve.tensor_copy(q0[:, 0:HALF], ps[4][:, :])
                ve.tensor_copy(q0[:, HALF:768], ps[5][:, 0:256]).then_inc(sem("mq_v"), 1)
                ve.wait_ge(sem("mkv_v_done"), count.take("mkv_v_done"))
                for n in range(2):
                    kv = ps[n][:, :].rearrange("p (h n) -> p h n", n=P)
                    ve.tensor_copy(mk[:, 0, 4 * n:4 * n + 4, 0:HD], kv[:, :, 0:HD])
                    last = ve.tensor_copy(val[:, 0, n * 256:(n + 1) * 256].rearrange("p (h n) -> p h n", n=HD),
                                          kv[:, :, HD:P])
                last.then_inc(sem("mkv_v"), 1)
                for t in range(NT):
                    then(ve.tensor_copy(mk[:, t, :, HD:QK], spread(proj[:, t, C_KR:C_END], (0, MLA_HEADS), (1, 32))))
                take_turned()
                ve.wait_ge(sem("mkv_a"), count.take("mkv_a"))
                ve.wait_ge(sem("mq_a"), count.take("mq_a"))
                ve.wait_ge(sem("mkv_v"), count.take("mkv_v"))
                for n, src in enumerate((mq, mk)):
                    flat = src.rearrange("p t h n -> p (t h n)")
                    then(ve.tensor_tensor(av[:, 1536 * n:1536 * n + 1536], flat, flat, ALU.mult))
                    then(ve.tensor_reduce(sq_sum[:, 16 * n:16 * n + 16],
                                          av[:, 1536 * n:1536 * n + 1536].rearrange("p (g d) -> p g d", d=QK), X, ALU.add))
                    ve.tensor_scalar(ms_in[:, 16 * n:16 * n + 16], sq_sum[:, 16 * n:16 * n + 16], 1.0 / QK, EPS,
                                     ALU.mult, ALU.add).then_inc(sem("ms_ready"), 1)
                for n, (src, gain) in enumerate(((mq, gain_mq), (mk, gain_mk))):
                    flat = src.rearrange("p t h n -> p (t h) n")
                    then(ve.tensor_tensor(flat, flat, spread(gain, (0, 16), (1, QK)), ALU.mult))
                    ve.wait_ge(sem("rms_ready"), count.take("rms_ready"))
                    then(ve.tensor_tensor(flat, flat, spread(ms_out[:, 16 * n:16 * n + 16], (1, 16), (0, QK)), ALU.mult))
                    rope(src[:, :, :, HD:HD + 16], src[:, :, :, HD + 16:QK],
                         spread(cos[:, 8:72], (24, NT), (0, MLA_HEADS), (1, 16)),
                         spread(sin[:, 8:72], (24, NT), (0, MLA_HEADS), (1, 16)), (NT, MLA_HEADS, 16))
                    ve.sem_inc(sem("mqk_ready"), 1)
                ve.wait_ge(sem("kcv_done"), count.take("kcv_done"))
                then(ve.tensor_copy(kcv, ps[1][0:30, 0:P]))
                then(ve.tensor_tensor_reduce(kc_sq, kcv[:, 0:HD], kcv[:, 0:HD], 1.0, 0.0, ALU.mult, ALU.add,
                                             sq_sum[0:30, 0:1]))
                ve.tensor_scalar(var_eps[0:30, 0:1], sq_sum[0:30, 0:1], 1.0 / HD, EPS, ALU.mult, ALU.add)\
                    .then_inc(sem("kc_ms_ready"), 1)
                ve.wait_ge(sem("kc_rms_ready"), count.take("kc_rms_ready"))
                kc = kc_twice[:, 0:HD]
                then(ve.scalar_tensor_tensor(out=kc, in0=kcv[:, 0:HD], scalar=rstd[0:30, 0:1], in1=gain_kc[0:30, :],
                                             op0=ALU.mult, op1=ALU.mult))
                rope(spread(kc[:, 0:8], (0, 1), (0, 1), (1, 8)), spread(kc[:, 8:16], (0, 1), (0, 1), (1, 8)),
                     spread(cos[0:30, 48:56], (0, 1), (0, 1), (1, 8)), spread(sin[0:30, 48:56], (0, 1), (0, 1), (1, 8)),
                     (1, 1, 8))
                ve.tensor_copy(kc_twice[:, HD:P], kc).then_inc(sem("kc_ready"), 1)
                for n in (0, 2, 4, 6):
                    ve.wait_ge(sem("m_turned_v"), count.take("m_turned_v"))
                    bank = (2, 3, 4, 5, 6, 7, 0, 1)[n]
                    ve.tensor_copy((mqT, mkT)[n // 4][:, 2 * (n % 4):2 * (n % 4) + 2, :],
                                   ps[bank][0:QK, :].rearrange("p (h s) -> p h s", h=2)).then_inc(sem("mT_v"), 1)
                ve.wait_ge(sem("kc_turned"), count.take("kc_turned"))
                ve.tensor_copy(kcT, ps[2][:, 0:30]).then_inc(sem("kcT_ready"), 1)
                ve.wait_ge(sem("c_scores_done"), count.take("c_scores_done"))
                for g in range(2):
                    for half in range(2):
                        ve.tensor_tensor(spread(c_sco[:, 240 * g + 60 * half:], (120, 2), (1, 60)),
                                         ps[2 + half][:, 120 * g:120 * g + 120].rearrange("p (f n) -> p f n", f=2),
                                         spread(cmp_mask[:, 60 * g:60 * g + 60], (0, 2), (1, 60)), ALU.add)\
                            .then_inc(sem("v_chain"), 1)
                        ve.wait_ge(sem("v_chain"), count.take("v_chain"))
                by_row = c_sco.rearrange("p (r n) -> p r n", n=30)
                then(ve.tensor_reduce(c_peak, by_row, X, ALU.min))
                ve.tensor_tensor(by_row, by_row, spread(c_peak, (1, 16), (0, 30)), ALU.subtract).then_inc(sem("c_sco_ready"), 1)
                ve.wait_ge(sem("c_prob_ready"), count.take("c_prob_ready"))
                then(ve.tensor_reduce(c_total, c_prob.rearrange("p (r n) -> p r n", n=30), X, ALU.add))
                then(ve.reciprocal(c_share, c_total))
                then(ve.tensor_tensor(spread(c_share, (2, 8), (1, 2)), spread(c_share, (2, 8), (1, 2)),
                                      spread(row_seen, (0, 8), (1, 2)), ALU.mult))
                ve.wait_ge(sem("gates_ready"), count.take("gates_ready"))
                then(ve.tensor_tensor(spread(c_share, (2, 8), (1, 2)), spread(c_share, (2, 8), (1, 2)),
                                      spread(gates, (3, 8), (24, 2)), ALU.mult))
                for n in range(2):
                    ve.wait_ge(sem("c_turned_v"), count.take("c_turned_v"))
                    ve.tensor_copy(c_probT[:, n * HALF:(n + 1) * HALF], ps[4 + n][0:30, :]).then_inc(sem("c_probT_v"), 1)
                for n in range(2):
                    ve.wait_ge(sem("c_weighed"), count.take("c_weighed"))
                    o = nat[:, :, 256 * n:256 * n + 256].rearrange("p t (h d) -> p h t d", d=HD)
                    ve.tensor_tensor(o, ps[n][:, :].rearrange("p (h t d) -> p h t d", h=4, t=NT),
                                     spread(c_share[:, 8 * n:8 * n + 8], (2, 4), (1, 2), (0, HD)), ALU.mult)\
                        .then_inc(sem("c_out"), 1)
                ve.wait_ge(sem("c_out"), count.take("c_out", 2))

                def finish(u, b):
                    ve.wait_ge(sem("probs_ready"), count.take("probs_ready", 4))
                    then(ve.reciprocal(share[:, b, :, :], total[:, b, :, :]))
                    f = u % 4
                    if u < 8:
                        gate = gates[:, 3 * 2 * f + 1 + u // 4:3 * 2 * f + 2 + u // 4]
                        then(ve.tensor_tensor(share[:, b, :, :], share[:, b, :, :], spread(gate, (3, 2), (24, 2)), ALU.mult))
                    ve.wait_ge(sem("weighed"), count.take("weighed"))
                    for m in range(2):
                        for t in range(NT):
                            src = ps[6 + b][:, (2 * m + t) * HD:(2 * m + t + 1) * HD]
                            at = (0 if u < 8 else HALF) + (2 * f + m) * HD
                            dst = nat[:, t, at:at + HD]
                            if u < 8:
                                last = ve.scalar_tensor_tensor(out=dst, in0=src, scalar=share[:, b, m, t:t + 1], in1=dst,
                                                               op0=ALU.mult, op1=ALU.add)
                            else:
                                last = ve.tensor_scalar(dst, src, share[:, b, m, t:t + 1], None, ALU.mult)
                    then(last)

                def out_rms(n):
                    for t in range(NT):
                        rms_of(nat[:, t, n * HALF:(n + 1) * HALF], 2 * n + t, HALF)

                def out_scale(n):
                    for t in range(NT):
                        ve.wait_ge(sem("rms_ready"), count.take("rms_ready"))
                        part = nat[:, t, n * HALF:(n + 1) * HALF]
                        last = ve.scalar_tensor_tensor(out=part, in0=part, scalar=ms_out[:, 2 * n + t:2 * n + t + 1],
                                                       in1=wide_gain[:, 1, n * HALF:(n + 1) * HALF], op0=ALU.mult,
                                                       op1=ALU.mult)
                        if n == 1:
                            last.then_inc(sem("nat_ready"), 1)

                for u in range(13):
                    if u < 12:
                        add_bias(u % 2, ((0, 1), (4, 5))[u % 2], lambda m: causal)
                    if u:
                        take_probT((u - 1) % 2)
                        finish(u - 1, (u - 1) % 2)
                    if u == 8:
                        out_rms(0)
                    if u == 9:
                        out_scale(0)
                out_rms(1)
                out_scale(1)

            def settle():
                ve.memset(settled, 0.0)

            def query_rms():
                ve.wait_ge(sem("peer_sq_done"), count.take("peer_sq_done"))
                ve.tensor_scalar(ms_in[:, 0:2], ps[7][:, 0:2], 1.0 / 256, EPS, ALU.mult, ALU.add)\
                    .then_inc(sem("ms_ready"), 1)

            def choose(t):
                if t == 0:
                    ve.wait_ge(sem("rms_ready"), count.take("rms_ready"))
                    ve.wait_ge(sem("key_scores_done"), count.take("key_scores_done"))
                    for tile in range(NT):
                        last = ve.tensor_scalar(key_sco[:, tile, :], ps[6][:, tile * S:(tile + 1) * S],
                                                ms_out[:, tile:tile + 1], None, ALU.mult)
                    then(last)
                    ve.sem_inc(sem("key_scores_taken"), 1)
                s = [key_sco[:, t, half * P:(half + 1) * P] for half in range(2)]
                left = [key_left[:, half * P:(half + 1) * P] for half in range(2)]

                def eight(half, n):
                    return best[:, 16 * half + 8 * n:16 * half + 8 * n + 8]

                def eight_keys(half, n):
                    return best_key[:, 16 * half + 8 * n:16 * half + 8 * n + 8]

                settle()
                for half in range(2):
                    ve.max(eight(half, 0), s[half]).then_inc(sem("v_chain"), 1)
                ve.wait_ge(sem("v_chain"), count.take("v_chain", 2))
                settle()
                for half in range(2):
                    ve.max_index(eight_keys(half, 0), eight(half, 0), s[half])
                    ve.match_replace(left[half], eight(half, 0), s[half], -3e38).then_inc(sem("v_chain"), 1)
                ve.wait_ge(sem("v_chain"), count.take("v_chain", 2))
                settle()
                for half in range(2):
                    ve.max(eight(half, 1), left[half]).then_inc(sem("v_chain"), 1)
                ve.wait_ge(sem("v_chain"), count.take("v_chain", 2))
                settle()
                for half in range(2):
                    ve.max_index(eight_keys(half, 1), eight(half, 1), left[half]).then_inc(sem("v_chain"), 1)
                ve.wait_ge(sem("v_chain"), count.take("v_chain", 2))
                ve.tensor_copy(best_key_f, best_key)
                then(ve.tensor_tensor(spread(pairs, (16, 16), (1, 16)), spread(best[:, 0:16], (1, 16), (0, 16)),
                                      spread(best[:, 16:32], (0, 16), (1, 16)), ALU.add))
                settle()
                ve.max(top[:, 0:8], pairs).then_inc(sem("v_chain"), 1)
                ve.wait_ge(sem("v_chain"), count.take("v_chain"))
                settle()
                ve.max_index(top_pair[:, 0:8], top[:, 0:8], pairs)
                ve.match_replace(pairs_left, top[:, 0:8], pairs, -3e38).then_inc(sem("v_chain"), 1)
                ve.wait_ge(sem("v_chain"), count.take("v_chain"))
                settle()
                ve.max(top[:, 8:16], pairs_left).then_inc(sem("v_chain"), 1)
                ve.wait_ge(sem("v_chain"), count.take("v_chain"))
                settle()
                ve.max_index(top_pair[:, 8:16], top[:, 8:16], pairs_left).then_inc(sem("v_chain"), 1)
                ve.wait_ge(sem("v_chain"), count.take("v_chain"))
                ve.tensor_scalar(neg_top, top[:, 0:1], -1.0, None, ALU.mult).then_inc(sem("top_ready"), 1)
                ve.tensor_scalar(place[:, 0:16], top_pair, 4, None, ALU.logical_shift_right)
                then(ve.tensor_scalar(place[:, 16:32], top_pair, 15, None, ALU.bitwise_and))
                then(ve.tensor_copy(place_f, place))
                for half in range(2):
                    at = slice(16 * half, 16 * half + 16)
                    grid = spread(match, (16, 16), (1, 16))
                    then(ve.tensor_tensor(grid, spread(place_f[:, at], (1, 16), (0, 16)),
                                          spread(counter, (0, 16), (1, 16)), ALU.is_equal))
                    then(ve.tensor_tensor(grid, grid, spread(best_key_f[:, at], (0, 16), (1, 16)), ALU.mult))
                    then(ve.tensor_reduce(picked[:, at], grid, X, ALU.add))
                then(ve.scalar_tensor_tensor(out=expert_u[:, 16 * t:16 * t + 16], in0=picked[:, 0:16],
                                             scalar=float(N_KEYS), in1=picked[:, 16:32], op0=ALU.mult, op1=ALU.add))
                ve.sem_inc(sem("experts_ready"), 1)

            def dot(t, ks):
                for k in ks:
                    ve.wait_ge(sem(f"u{k % RING}_landed"), count.take(f"u{k % RING}_landed", 16))
                    row = arena_u[:, k % RING, :]
                    ve.tensor_tensor_reduce(row, row, nat[:, t, :], 1.0, 0.0, ALU.mult, ALU.add, dots[:, k:k + 1])\
                        .then_inc(sem("dot_done"), 1)

            def weights_of(t):
                then(ve.reciprocal(mass[:, t:t + 1], mass[:, t:t + 1]))
                ve.wait_ge(sem("gelu_ready"), count.take("gelu_ready"))
                ve.tensor_copy(expert_v[:, 16 * t:16 * t + 16], expert_u[:, 16 * t:16 * t + 16])
                then(ve.scalar_tensor_tensor(out=weight[:, 16 * t:16 * t + 16], in0=gate_w[:, 16 * t:16 * t + 16],
                                             scalar=mass[:, t:t + 1], in1=gelu, op0=ALU.mult, op1=ALU.mult))
                ve.sem_inc(sem("weight_ready"), 1)

            def unit(t, ahead=True, more=False, first=False):
                if not first:
                    dot(t, range(8))
                ve.wait_ge(sem("gate_w_ready"), count.take("gate_w_ready"))
                if ahead:
                    choose(1 - t)
                dot(t, range(0 if first else 8, TOPK))
                weights_of(t)
                if more:
                    query_rms()

            def peer():
                ve.memset(zeros, 0.0)
                then(ve.memset(ones, 1.0))
                ve.sem_inc(sem("peer_set"), 1)
                query_rms()
                choose(0)
                unit(0, more=True, first=True)
                per = {f"u{k}_landed": 64 for k in range(RING)}
                with count.loop(P_HEADS - 2, gate_w_ready=2, gelu_ready=2, rms_ready=1, key_scores_done=1,
                            peer_sq_done=1, v_chain=CHOOSE_STEPS, **per):
                    unit(1)
                    unit(0, more=True)
                unit(1)
                unit(0)
                unit(1, ahead=False)
                for t in range(NT):
                    ve.wait_ge(sem("v_used"), count.take("v_used", (N_UNITS - 1) * TOPK if t == 0 else TOPK))
                    for k in range(2):
                        part = h[:, t, k * HALF:(k + 1) * HALF]
                        last = ve.tensor_tensor(part, part, ps[2 * t + k][:, :], ALU.add)
                    last.then_inc(sem("y_ready"), 1)

            ve.wait_ge(sem("lam_landed"), count.take("lam_landed", 16))
            for n in range(2):
                ve.tensor_tensor_reduce(lam_prod, lam_in[:, 128 * n:128 * n + 64], lam_in[:, 128 * n + 64:128 * n + 128],
                                        1.0, 0.0, ALU.mult, ALU.add, lam_sum[:, n:n + 1]).then_inc(sem("lam_summed"), 1)
                ve.wait_ge(sem("lam_summed"), count.take("lam_summed"))
            ve.wait_ge(sem("bias_in_landed"), count.take("bias_in_landed", 32))
            then(ve.tensor_scalar(relb_sb[0:32, :], relb_sb[0:32, :], -1.0, None, ALU.mult))
            ve.memset(relb_sb[32:33, :], BIG).then_inc(sem("relb_set"), 1)
            take_turned()
            ve.wait_ge(sem("lam_exp"), count.take("lam_exp"))
            then(ve.scalar_tensor_tensor(out=lam_exp[:, 2:3], in0=lam_exp[:, 1:2], scalar=-LAM_INIT,
                                         in1=lam_exp[:, 0:1], op0=ALU.add, op1=ALU.subtract))
            ve.wait_ge(sem("subln_landed"), count.take("subln_landed", 16))
            then(ve.tensor_scalar(subln, subln, 1.0 - LAM_INIT, None, ALU.mult))
            ve.wait_ge(sem("bias_landed"), count.take("bias_landed", 32))
            attention_layer(differential, 14)
            heads = nat[:, :, :].rearrange("p t (g d) -> p (t g) d", d=P)
            tmp_h = tmp[:, :, :].rearrange("p t (g d) -> p (t g) d", d=P)
            then(ve.tensor_tensor(tmp[:, :, :], nat[:, :, :], nat[:, :, :], ALU.mult))
            then(ve.tensor_reduce(sq_sum[:, 0:16], tmp_h, X, ALU.add))
            ve.tensor_scalar(ms_in[:, 0:16], sq_sum[:, 0:16], 1.0 / P, LN_EPS, ALU.mult, ALU.add)\
                .then_inc(sem("ms_ready"), 1)
            ve.wait_ge(sem("rms_ready"), count.take("rms_ready"))
            for t in range(NT):
                part = nat[:, t, :].rearrange("p (g d) -> p g d", d=P)
                r = ms_out[:, 8 * t:8 * t + 8]
                then(ve.tensor_tensor(part, part, spread(r, (1, 8), (0, P)), ALU.mult))
                ve.tensor_tensor(part, part, spread(subln, (0, 8), (1, P)), ALU.mult).then_inc(sem("nat_ready"), 1)
            out_and_mlp(0)
            take_turned()
            attention_layer(plain, 8)
            ve.sem_inc(sem("nat_ready"), 2)
            out_and_mlp(2)
            ve.wait_ge(sem("small_landed"), count.take("small_landed", 16 * N_SMALL))
            wide_norm(0)
            take_turned()
            angles()
            for gain, scale in ((gain_q, -(HD ** -0.5)), (gain_mq, -(QK ** -0.5))):
                then(ve.tensor_scalar(gain, gain, scale, None, ALU.mult))
            hybrid_attention()
            ve.sem_inc(sem("attention_done"), 1)
            take_turned()
            add_residual(1.0, lambda t: rms_of(h[:, t, :], t, D))
            wide_norm(2, has_rms=True)
            take_turned()
            peer()


def kernel(**inputs):
    import concourse.bacc as bacc
    from concourse.bass_utils import run_bass_kernel_spmd

    nc = bacc.Bacc("TRN2", target_bir_lowering=False, num_devices=1)
    arrays = {name: np.ascontiguousarray(value) for name, value in inputs.items()}
    arrays.update(const=shape_constants(), buckets=bucket_table(), freqs=rope_frequencies())
    dram = {}
    for name, a in arrays.items():
        dram[name] = nc.dram_tensor("in_" + name, a.shape, mybir.dt.from_np(a.dtype), kind="ExternalInput").ap()
    out = nc.dram_tensor("out_y", (1, S, D), F32, kind="ExternalOutput").ap()
    build(nc, dram, out)
    result = run_bass_kernel_spmd(nc, [{"in_" + n: a for n, a in arrays.items()}], core_ids=[0])
    return result.results[0]["out_y"]
```

```python
from contextlib import ExitStack, contextmanager
import math

import numpy as np

import concourse.bass as bass
from concourse import mybir

F32 = mybir.dt.float32
F32R = mybir.dt.float32r
U32 = mybir.dt.uint32
I32 = mybir.dt.int32
ALU = mybir.AluOpType
ACT = mybir.ActivationFunctionType
X = mybir.AxisListType.X

P = 128
D = 1024
S = 256
NT = S // P
NB = D // P
HALF = 512
HEADS = 16
HD = 64
DFF = 4 * D
N_CHUNK = DFF // 256
ALPHA = 4 ** 0.25
LN_EPS = 1e-5
EPS = 1e-6
LAM_INIT = 0.8 - 0.6 * math.exp(-0.3 * 0)
BIG = 1e30

N_SMALL = 16
C_Q, C_KC, C_VC, C_KS, C_VS, C_KW, C_VW, C_GATE, C_CQ, C_CKV, C_KR, C_END = np.cumsum(
    [0, 512, 128, 128, 128, 128, 128, 128, 24, 256, 128, 32]).tolist()
N_CMP = 15
MLA_HEADS = 8
QK = 96

P_HEADS = 8
TOPK = 16
N_KEYS = 128
RING = 8
N_UNITS = P_HEADS * NT
CHOOSE_STEPS = 49
U_LEAD = 4
PEER_SLOT = 2


def bucket_table():
    rel = 255 - np.arange(384)
    n = np.maximum(rel, 0)
    nf = np.maximum(n, 16).astype(np.float32)
    large = np.minimum(16 + (np.log(nf / 16) / math.log(8) * 16).astype(np.int32), 31)
    bucket = np.where(n < 16, n, large)
    table = np.zeros((33, 384), np.float32)
    table[bucket[rel >= 0], np.flatnonzero(rel >= 0)] = 1.0
    table[32, rel < 0] = 1.0
    return table


def rope_frequencies():
    return np.concatenate([
        (500000.0 ** (-np.arange(0, dim, 2) / dim)).astype(np.float32) for dim in (16, 32)])


def shape_constants():
    t = np.arange(S)
    causal = np.where(t[None, :] > t[:, None], BIG, 0.0)
    causal = np.concatenate([causal[:P, :P], causal[P:, :]], axis=1)
    end = 16 * np.arange(N_CMP) + 31
    seen = end[None, :] <= t[:, None]
    cmp_mask = np.full((P, 2, NT, 2, N_CMP), BIG)
    for g in range(2):
        for tile in range(NT):
            cmp_mask[:, g, tile, g, :] = np.where(seen[tile * P:(tile + 1) * P], 0.0, BIG)
    row_seen = seen.any(axis=1).reshape(NT, P).T
    count = np.broadcast_to(np.arange(TOPK), (P, TOPK))
    return np.concatenate([np.eye(P), causal, cmp_mask.reshape(P, -1), row_seen, count],
                          axis=1).astype(np.float32)


CO_ID, CO_CAUSAL, CO_CMP, CO_SEEN, CO_COUNT, CO_END = np.cumsum(
    [0, P, 384, 2 * NT * 2 * N_CMP, NT, TOPK]).tolist()


class Count:

    def __init__(self, engine):
        self.engine = engine
        self.seen, self.trip, self.per = {}, None, {}

    def skip(self, name, n=1):
        self.seen[name] = self.seen.get(name, 0) + n

    def take(self, name, n=1):
        self.skip(name, n)
        return self.seen[name] if self.trip is None else self.trip * self.per[name] + self.seen[name]

    @contextmanager
    def loop(self, trips, **per):
        before = dict(self.seen)
        with self.engine.Fori(0, trips) as i:
            self.trip, self.per = i, per
            yield i
            self.trip = None
        for name in self.seen:
            taken = self.seen[name] - before.get(name, 0)
            assert taken == per.get(name, 0), (name, taken)
            self.seen[name] += taken * (trips - 1)


def spread(ap, *dims):
    return bass.AP(ap.tensor, ap.offset, [list(ap.ap[0])] + [list(d) for d in dims])


def to_partitions(row, n=P):
    return bass.AP(row.tensor, row.offset, [[0, n]] + [list(d) for d in row.ap])


def build(nc, T, out):
    with ExitStack() as ctx:
        sems = {}

        def sem(name):
            if name not in sems:
                sems[name] = ctx.enter_context(nc.semaphore(name))
            return sems[name]

        def sb(name, shape, dt=F32):
            return ctx.enter_context(nc.sbuf_tensor(name, shape, dt))

        const = sb("const", [P, CO_END])
        ident = const[:, CO_ID:CO_CAUSAL]
        causal = const[:, CO_CAUSAL:CO_CMP]
        cmp_mask = const[:, CO_CMP:CO_SEEN]
        row_seen = const[:, CO_SEEN:CO_COUNT]
        counter = const[:, CO_COUNT:CO_END]
        h = sb("h", [P, NT, D])
        nat = sb("nat", [P, NT, D])
        with ExitStack() as over:
            def split(name, shape, dt=F32R):
                return over.enter_context(nc.sbuf_tensor(name, shape, dt))

            w_split = [[split("w0_high", [P, 2048]), split("w0_low", [P, 2048])]]
            act_low = split("act_low", [P, 2, HALF])
            act_sq = split("act_sq", [P, 2, HALF], F32)
            split("pad_to_sco_end", [P, 7280 - 6144], F32)
            w_split.append([split("w1_high", [P, 2048]), split("w1_low", [P, 2048])])
            hT_low = split("hT_low", [P, NB, S])
            hT_high = split("hT_high", [P, NB, S])
            act_high = split("act_high", [P, 2, HALF])
        with ExitStack() as over:
            hT_low_qkv = split("hT_low_qkv", [P, NB, S])
            v_split = [[split(f"v{n}_{part}", [P, D]) for part in ("high", "low")] for n in range(2)]
            split("pad_to_hT", [P, 15472 - 6144], F32)
            qk_split = [[split(f"{name}_{part}", [P, D]) for part in ("high", "low")] for name in "qk"]
        proj = sb("proj", [P, NT, C_END])
        prob = sb("prob", [P, 2, 2, 384])
        probT = sb("probT", [P, 2, 384])
        sco = sb("sco", [P, 2, 2, 384])
        qkring = sb("qkring", [P, 2, 2048])
        val = sb("val", [P, NT, D])
        hT = sb("hT", [P, NB, S])
        act = sb("act", [P, 2, HALF])
        relu = sb("relu", [P, 2, HALF])
        wide_gain = sb("wide_gain", [P, 3, D])
        ring = sb("ring", [P, 4, 2048])
        qkT = sb("qkT", [P, 2, 2, S])
        peak = sb("peak", [P, 2, 2, NT])
        total = sb("total", [P, 2, 2, NT])
        share = sb("share", [P, 2, 2, NT])
        omap = sb("omap", [P, NT, P])
        arena_u = sb("arena_u", [P, RING, D])
        ln_gb = arena_u[:, :, :].rearrange("p (s g) d -> p s g d", g=2)
        arena_v = sb("arena_v", [P, RING, D])
        av = arena_v[:, :, :].rearrange("p r d -> p (r d)")
        bias = av[:, 0:HEADS * 384].rearrange("p (m k) -> p m k", m=HEADS)
        tmp = av[:, HEADS * 384:HEADS * 384 + 2048].rearrange("p (t d) -> p t d", t=NT)
        bucket_sb = tmp[0:33, 0, 0:384]
        relb_sb = tmp[0:33, 0, 384:400]
        bias_rows = tmp[0:HEADS, 0, 512:896]
        small = sb("small", [P, 1952])
        small_at = [0]

        def piece(n):
            small_at[0] += n
            return small[:, small_at[0] - n:small_at[0]]

        lam_in, lam_prod = tmp[:, 1, 0:256], tmp[:, 1, 256:320]
        lam_sum, lam_exp = piece(2), piece(3)
        stats, moments, var_eps, rstd = piece(24), piece(4), piece(2), piece(2)
        subln = piece(128)
        ms_in, ms_out = piece(24 * NT), piece(24 * NT)
        sq_sum = piece(24 * NT)
        neg_half = piece(24 * NT)
        pos_i = sb("pos_i", [P, 3], I32)
        pos_f, freqs = piece(3), piece(24)
        angle, trig = piece(72), piece(144)
        cos, sin = trig[:, 0:72], trig[:, 72:144]
        gain_q, gain_ks, gain_kw, gain_kc = piece(64), piece(64), piece(64), piece(64)
        gain_mq, gain_mk, gain_cq, gain_ckv = piece(QK), piece(QK), piece(256), piece(128)
        cmp_posT = piece(16)
        cmp_w2 = piece(256).rearrange("p (a b n) -> p a b n", a=2, b=2)
        gates = piece(24 * NT)
        c_peak, c_total, c_share = piece(16), piece(16), piece(16)
        sq = av[:, 0:2 * C_END].rearrange("p (t n) -> p t n", t=NT)
        flow_x0 = av[:, 3440:3952].rearrange("p (a r i) -> p a r i", a=2, r=2)
        flow_x = av[:, 3952:4464].rearrange("p (a g i) -> p a g i", a=2, g=2)
        blocks = av[:, 4464:5424].rearrange("p (a j n) -> p a j n", a=2, j=16)
        hidden = av[:, 5424:5544].rearrange("p (a b n) -> p a b n", a=2, b=2)
        kcv = av[0:30, 5544:5672]
        kc_twice = av[0:30, 5672:5800]
        kc_sq = av[0:30, 5800:5864]
        kcT = av[:, 5864:5894]
        c_sco = av[:, 5894:6374]
        c_prob = av[:, 6374:6854]
        lora = av[:, 6854:7622].rearrange("p (t n) -> p t n", t=NT)
        au = arena_u[:, :, :].rearrange("p r d -> p (r d)")
        c_probT = au[0:30, 0:2048]
        mq = au[:, 2048:3584].rearrange("p (t h n) -> p t h n", t=NT, n=QK)
        mk = au[:, 3584:5120].rearrange("p (t h n) -> p t h n", t=NT, n=QK)
        rope_tmp = au[:, 5120:6144].rearrange("p (k n) -> p k n", k=4)
        cycles, reduced = au[:, 6144:6288], au[:, 6288:6432]
        loraT = relu[:, :, :].rearrange("p a n -> p (a n)")[:, 0:768].rearrange("p (c s) -> p c s", c=3)
        mqT = qkring[0:QK, 0, :].rearrange("p (h s) -> p h s", s=S)
        mkT = qkring[0:QK, 1, :].rearrange("p (h s) -> p h s", s=S)

        ones, settled = piece(1), piece(1)
        keysT = qkring[:, 0, :]
        keys = av[:, 0:2048].rearrange("p (b d) -> p b d", d=P)
        pq, pq_sq = act[:, 0, :], act[:, 1, :]
        zeros = omap[:, 0, :]
        flat_sco = sco[:, :, :, :].rearrange("p a b n -> p (a b n)")
        diag = flat_sco[:, 0:512].rearrange("p (s n) -> p s n", s=4)
        key_sco = flat_sco[:, 512:1024].rearrange("p (t n) -> p t n", t=NT)
        pairs = flat_sco[:, 1024:1280]
        pairs_left = flat_sco[:, 1280:1536]
        flat_prob = prob[:, :, :, :].rearrange("p a b n -> p (a b n)")
        key_left, match = flat_prob[:, 0:256], flat_prob[:, 256:512]
        pool_of = [flat_prob[:, 512:].rearrange("p n -> p n"), 0]

        def bit(n, dt=F32):
            at = pool_of[1]
            pool_of[1] += n
            part = pool_of[0][:, at:at + n]
            return part if dt is F32 else part.bitcast(dt)

        best, best_key, best_key_f = bit(32), bit(32, U32), bit(32)
        top, top_pair, place, place_f, picked = bit(16), bit(16, U32), bit(32, U32), bit(32), bit(32)
        neg_top, mass = bit(1), bit(2)
        expert_u, expert_v = bit(32, U32), bit(32, U32)
        gate_w, dots, gelu, weight = bit(32), bit(16), bit(16), bit(32)
        ps = [ctx.enter_context(nc.psum_tensor(f"ps{i}", [P, HALF], F32)) for i in range(8)]

        def rows(w, j, n=2):
            return w[j * n * P:(j + 1) * n * P, :].rearrange("(c p) n -> p c n", p=P)

        def cols(w, at, n=256):
            return w[:, at:at + n].rearrange("(c p) n -> p c n", p=P)

        def cols_dyn(w, at, n):
            return w.rearrange("(c p) n -> p c n", p=P)[:, :, bass.ds(at, n)]

        x_t = T["x"][0].rearrange("(t p) d -> p t d", p=P)
        shifted = nc.dram_tensor("bias_shifted", (P * (HEADS * 384 + 1),), F32, kind="Internal").ap()
        w_in, w_out_a = T["w_in_a"][0], T["w_out_a"][0]
        w_kv, w_q, w_out_b = T["w_kv_shared"], T["w_q_b"][0], T["w_out_b"][0]

        block = ctx.enter_context(nc.Block())

        @block.sync
        def _(sp):
            count = Count(sp)
            turn = [0]
            used = {}

            def chunk(dst, *srcs, landed=None):
                slot = turn[0] % 4
                turn[0] += 1
                load(ring, slot, f"ring{slot}", dst, *srcs, landed=landed and f"{landed}{slot}_landed")

            def load(where, slot, name, dst, *srcs, landed=None):
                if used.get(name):
                    sp.wait_ge(sem(name + "_used"), count.take(name + "_used"))
                used[name] = True
                for n, src in enumerate(srcs):
                    sp.dma_start(dst(where[:, slot, :], n), src).then_inc(sem(landed or name + "_landed"), 16)

            def load_raw(slot, dst, src):
                load(ring, slot, f"ring{slot}", dst, src, landed=f"raw{slot}_landed")

            def as_blocks(n):
                return lambda s, i: s.rearrange("p (c n) -> p c n", n=n)

            def two_columns(s, i):
                return s[:, i * 1024:(i + 1) * 1024].rearrange("p (c n) -> p c n", n=P)

            def nat_chunks(w, at=0, landed=None):
                for j in range(4):
                    chunk(as_blocks(D), rows(w[:, at:at + D], j), landed=landed)

            def qk_chunk(wq, wk, f):
                at = f * P
                name = f"qk{f % 2}" if isinstance(f, int) else None
                load(qkring, f % 2, name, two_columns, cols(wq, at, P), cols(wk, at, P))

            def qk_chunks(wq, wk):
                with count.loop(3, qk0_used=1, qk1_used=1) as i:
                    for b in range(2):
                        load(qkring, b, f"qk{b}", two_columns,
                             cols_dyn(wq, i * 256 + 256 + b * P, P), cols_dyn(wk, i * 256 + 256 + b * P, P))

            def mlp_chunks(layer):
                up, down = T["w_up"][layer], T["w_down"][layer]
                load_raw(0, as_blocks(256), cols(up, 0))
                load_raw(2, as_blocks(256), cols(up, 256))
                load_raw(1, as_blocks(D), rows(down, 0))
                with count.loop((N_CHUNK - 2) // 2, ring0_used=1, ring1_used=1, ring2_used=1, ring3_used=1) as i:
                    for b in range(2):
                        load_raw(2 * b, as_blocks(256), cols_dyn(up, i * 512 + (512 + 256 * b), 256))
                        load_raw(3 - 2 * b, as_blocks(D), down_rows(down, i * 2 + (1 + b)))
                load_raw(3, as_blocks(D), rows(down, N_CHUNK - 1))

            def down_rows(down, j):
                return down.rearrange("(j c p) n -> p j c n", p=P, c=2)[:, bass.ds(j, 1), :, :].rearrange(
                    "p j c n -> p (j c) n")

            sp.dma_start(bucket_sb, T["buckets"]).then_inc(sem("bias_in_landed"), 16)
            sp.dma_start(relb_sb[0:32, :], T["rel_bias"]).then_inc(sem("bias_in_landed"), 16)
            for t in range(NT):
                sp.dma_start(h[:, t, :], x_t[:, t, :]).then_inc(sem("x_landed"), 16)
            sp.dma_start(const[:, :], T["const"]).then_inc(sem("const_landed"), 16)
            nat_chunks(w_in, 2 * D, landed="raw")
            qk_chunk(w_in, w_in[:, D:], 0)
            qk_chunk(w_in, w_in[:, D:], 1)
            nat_chunks(w_out_a, landed="raw")
            qk_chunks(w_in, w_in[:, D:])
            mlp_chunks(0)
            nat_chunks(w_kv, D, landed="raw")
            sp.wait_ge(sem("mlp_done"), count.take("mlp_done"))
            qk_chunk(w_q, w_kv, 0)
            qk_chunk(w_q, w_kv, 1)
            nat_chunks(w_out_b, landed="raw")
            qk_chunks(w_q, w_kv)
            mlp_chunks(1)
            for j in range(8):
                chunk(lambda s, i: s[:, 0:C_END], T["w_in_2"][0][j * P:(j + 1) * P, :], landed="raw")
            chunk(lambda s, i: s[:, 0:1536].rearrange("p (c n) -> p c n", c=2),
                  T["mla_w_uq_2"][0].rearrange("(c p) n -> p c n", p=P))
            chunk(lambda s, i: s[:, 0:D], T["mla_w_ukv_2"][0])
            for n, w1 in enumerate((T["cmp_k_w1_2"][0], T["cmp_v_w1_2"][0])):
                for j in range(2):
                    chunk(as_blocks(256), w1[j * D:(j + 1) * D, :].rearrange("(c p) n -> p c n", p=P))
                if n == 0:
                    sp.wait_ge(sem("flow_x0_ready"), count.take("flow_x0_ready"))
                    for g in range(2):
                        for r in range(2):
                            sp.dma_start(flow_x[64 * r:64 * r + 64, :, g, :], flow_x0[64 * g:64 * g + 64, :, r, :])\
                                .then_inc(sem("flow_landed"), 16)
            nat_chunks(T["w_out_2"][0], landed="raw")
            sp.wait_ge(sem("attention_done"), count.take("attention_done"))
            sp.dma_start(keys, T["peer_sub_keys_2"][0].rearrange("h t n d -> n (h t) d")).then_inc(sem("keys_landed"), 16)
            for j in range(P_HEADS):
                load(ring, PEER_SLOT, f"ring{PEER_SLOT}", as_blocks(256), cols(T["peer_w_q_2"][0], 256 * j))
            for t in range(NT):
                sp.wait_ge(sem("y_ready"), count.take("y_ready"))
                sp.dma_start(out[0, t * P:(t + 1) * P, :], h[:, t, :]).then_inc(sem("stored"), 16)
            sp.wait_ge(sem("stored"), count.take("stored", 32))

        @block.tensor
        def _(pe):
            count = Count(pe)
            turn = [0]

            def landed(name):
                pe.wait_ge(sem(name + "_landed"), count.take(name + "_landed", 32 if name.startswith("qk") else 16))

            def slot_of_turn():
                slot = turn[0] % 4
                turn[0] += 1
                landed(f"ring{slot}")
                return slot

            def turn_over(src, ready=None, split=False):
                for t in range(NT):
                    if ready:
                        pe.wait_ge(sem(ready), count.take(ready))
                    for c in range(NB):
                        last = pe.transpose(ps[4 + c // 2][:, (c % 2) * S + t * P:(c % 2) * S + t * P + P],
                                            src[:, t, c * P:(c + 1) * P], ident)
                        if t == NT - 1 and c % 2:
                            last.then_inc(sem("turned_s" if split else "turned_v" if c < 4 else "turned_a"), 1)

            def hT_ready():
                pe.wait_ge(sem("hT_v"), count.take("hT_v", 2))
                pe.wait_ge(sem("hT_a"), count.take("hT_a", 2))

            def project(b, part):
                pe.wait_ge(sem(f"qk_split{part}"), count.take(f"qk_split{part}"))
                if part == 1:
                    pe.sem_inc(sem(f"qk{b}_used"), 1)
                for c in range(NB):
                    last = product(ps[4 + part][:, 0:S], [x[:, c * P:(c + 1) * P] for x in qk_split[part]],
                                   [x[:, c, :] for x in (hT_high, hT_low_qkv)], start=(c == 0), stop=(c == NB - 1))
                last.then_inc(sem("proj_ready"), 1)

            def values():
                for c in range(NB):
                    if c % 2 == 0:
                        pe.wait_ge(sem("hT_split"), count.take("hT_split"))
                    pe.wait_ge(sem(f"w{c % 2}_split"), count.take(f"w{c % 2}_split"))
                    if c % 2:
                        pe.sem_inc(sem(f"ring{c // 2}_used"), 1)
                    if c == NB - 2:
                        continue
                    order = [(cc, k) for k in range(4) for cc in (c - 1, c)] if c == NB - 1 else \
                            [(c, k) for k in range(4)]
                    for cc, k in order:
                        last = product(ps[k][:, :],
                                       [x[:, cc, (k // 2) * P:(k // 2) * P + P] for x in (hT_high, hT_low_qkv)],
                                       [x[:, (k % 2) * HALF:(k % 2 + 1) * HALF] for x in v_split[cc % 2]],
                                       start=(cc == 0), stop=(cc == NB - 1))
                        if cc == NB - 1:
                            last.then_inc(sem("acc_ready"), 1)
                    if c < NB - 2:
                        last.then_inc(sem(f"w{c % 2}_used"), 1)
                count.skip("acc_ready", 4)

            def scores(q, k, banks, rows_of=lambda m: slice(64 * m, 64 * m + 64)):
                for m in range(2):
                    pe.matmul(ps[banks[m]][:, 0:P], q(m)[:, 0:P], k(m)[:, 0:P], start=True, stop=True)
                for m in range(2):
                    pe.matmul(ps[banks[m]][:, P:384], q(m)[:, P:S], k(m)[:, 0:S], start=True, stop=True)\
                        .then_inc(sem("scores_ready"), 1)

            def turn_probs(b):
                for m in range(2):
                    pe.wait_ge(sem("probs_ready"), count.take("probs_ready", 2))
                    for k in range(3):
                        last = pe.transpose(ps[2 + m][:, k * P:(k + 1) * P], prob[:, b, m, k * P:(k + 1) * P], ident)
                    last.then_inc(sem("probT_v_turned" if m == 0 else "probT_a_turned"), 1)

            def weigh(b, v, dv):
                for m in range(2):
                    pe.wait_ge(sem("probT_v" if m == 0 else "probT_a"), count.take("probT_v" if m == 0 else "probT_a"))
                    o = ps[6 + b]
                    at = 2 * m * dv
                    pe.matmul(o[:, at:at + dv], probT[:, m, 0:P], v(m, 0), start=True, stop=True)
                    pe.matmul(o[:, at + dv:at + 2 * dv], probT[:, m, P:2 * P], v(m, 0), start=True, stop=False)
                    last = pe.matmul(o[:, at + dv:at + 2 * dv], probT[:, m, 2 * P:3 * P], v(m, 1),
                                     start=False, stop=True)
                last.then_inc(sem("weighed"), 1)

            def attend_block(f, b, dv, more=True):
                pe.wait_ge(sem("qkT_ready"), count.take("qkT_ready", 2))
                scores(lambda m: qkT[64 * m:64 * m + 64, b, 0, :], lambda m: qkT[64 * m:64 * m + 64, b, 1, :], (0, 1))
                if more:
                    project(1 - b, 0)
                turn_probs(b)
                if more:
                    project(1 - b, 1)
                weigh(b, lambda m, t: val[:, t, bass.ds(f * P + (m * 64 if dv == 64 else 0), dv)], dv)

            def attention_layer(dv):
                values()
                project(0, 0)
                project(0, 1)
                pe.wait_ge(sem("val_v"), count.take("val_v", 2))
                pe.wait_ge(sem("val_a"), count.take("val_a", 2))
                with count.loop(3, qk_split0=2, qk_split1=2, qkT_ready=4, probs_ready=8, probT_v=2, probT_a=2) as i:
                    for b in range(2):
                        attend_block(i * 2 + b, b, dv)
                attend_block(6, 0, dv)
                attend_block(7, 1, dv, more=False)

            def take_half(pair, half, slot):
                pe.wait_ge(sem(f"w{pair}_split"), count.take(f"w{pair}_split"))
                if half:
                    pe.sem_inc(sem(f"ring{slot}_used"), 1)

            def product(dst, a, b, start, stop):
                pe.matmul(dst, a[0], b[0], start=start, stop=False, skip_group_check=True)
                pe.matmul(dst, a[0], b[1], start=False, stop=False, skip_group_check=True)
                return pe.matmul(dst, a[1], b[0], start=False, stop=stop, skip_group_check=True)

            def split_natural():
                for j in range(4):
                    slot = (turn[0] + j) % 4
                    pe.wait_ge(sem("hT_split"), count.take("hT_split"))
                    order = [(cc, k) for k in range(4) for cc in range(2)] if j == 3 else \
                            [(cc, k) for cc in range(2) for k in range(4)]
                    for n, (cc, k) in enumerate(order):
                        c = 2 * j + cc
                        if n < 2 and j == 3:
                            take_half(j % 2, n, slot)
                        elif n % 4 == 0 and j < 3:
                            take_half(j % 2, n // 4, slot)
                        cut = slice(cc * D + (k % 2) * HALF, cc * D + (k % 2 + 1) * HALF)
                        last = product(ps[k][:, :], [x[:, c, (k // 2) * P:(k // 2) * P + P] for x in (hT_high, hT_low)],
                                       [x[:, cut] for x in w_split[j % 2]], start=(c == 0), stop=(c == NB - 1))
                        if c == NB - 1:
                            last.then_inc(sem("acc_ready"), 1)
                    if j < 3:
                        last.then_inc(sem(f"w{j % 2}_used"), 1)
                pe.wait_ge(sem("acc_ready"), count.take("acc_ready", 4))
                pe.sem_inc(sem("w1_used"), 1)

            def up(b, first=False, pair=1):
                for fb in range(2):
                    for c in range(NB):
                        if first and fb == 0 and c % 2 == 0:
                            pe.wait_ge(sem("hT_split"), count.take("hT_split"))
                        if fb == 0 and c % 4 == 0:
                            take_half(pair, c // 4, 2 * b)
                        at = c * 256 + fb * P
                        last = product(ps[4 + b][:, fb * S:(fb + 1) * S], [x[:, at:at + P] for x in w_split[pair]],
                                       [x[:, c, :] for x in (hT_high, hT_low)], start=(c == 0), stop=(c == NB - 1))
                last.then_inc(sem("up_ready"), 1)

            def down(b, first=False, final=False):
                pe.wait_ge(sem("act_ready"), count.take("act_ready"))
                pair = 1 if final else 0
                order = [(fb, k) for k in range(4) for fb in range(2)] if final else \
                        [(fb, k) for fb in range(2) for k in range(4)]
                for n, (fb, k) in enumerate(order):
                    if (n < 2) if final else (n % 4 == 0):
                        take_half(pair, fb, 2 * b + 1)
                    at = fb * S + (k // 2) * P
                    cut = slice(fb * D + (k % 2) * HALF, fb * D + (k % 2 + 1) * HALF)
                    last = product(ps[k][:, :], [x[:, b, at:at + P] for x in (act_high, act_low)],
                                   [x[:, cut] for x in w_split[pair]], start=(first and fb == 0), stop=(final and fb == 1))
                    if final and fb == 1:
                        last.then_inc(sem("acc_ready"), 1)
                if final:
                    pe.wait_ge(sem("acc_ready"), count.take("acc_ready", 4))
                    pe.sem_inc(sem("w1_used"), 1)
                    pe.sem_inc(sem("mlp_done"), 1)
                else:
                    last.then_inc(sem("w0_used"), 1)

            def mlp():
                up(0, first=True, pair=0)
                up(1)
                down(0, first=True)
                with count.loop((N_CHUNK - 2) // 2, w0_split=4, w1_split=4, act_ready=2):
                    up(0)
                    down(1)
                    up(1)
                    down(0)
                down(1, final=True)

            def key_scores(j, more=True):
                landed(f"ring{PEER_SLOT}")
                w = ring[:, PEER_SLOT, :].rearrange("p (c n) -> p c n", n=256)
                for half in range(2):
                    for c in range(NB):
                        last = pe.matmul(ps[4 + half][:, 0:S], w[:, c, half * P:(half + 1) * P], hT[:, c, :],
                                         start=(c == 0), stop=(c == NB - 1))
                    last.then_inc(sem("peer_q_done"), 1)
                pe.wait_ge(sem("pq_ready"), count.take("pq_ready", 4))
                pe.sem_inc(sem(f"ring{PEER_SLOT}_used"), 1)
                for t in range(NT):
                    for half in range(2):
                        last = pe.matmul(ps[7][:, t:t + 1], pq_sq[:, half * S + t * P:half * S + t * P + P], ones,
                                         start=(half == 0), stop=(half == 1))
                last.then_inc(sem("peer_sq_done"), 1)
                for t in range(NT):
                    for half in range(2):
                        last = pe.matmul(ps[6][:, (2 * t + half) * P:(2 * t + half + 1) * P],
                                         pq[:, half * S + t * P:half * S + t * P + P],
                                         keysT[:, bass.ds(j * (2 * P) + half * P, P)], start=True, stop=True)
                last.then_inc(sem("key_scores_done"), 1)

            def add_experts(t, ks, final=False):
                for k in ks:
                    pe.wait_ge(sem(f"v{k % RING}_landed"), count.take(f"v{k % RING}_landed", 16))
                    pe.wait_ge(sem("diag_ready"), count.take("diag_ready"))
                    for n in range(2):
                        last = pe.matmul(ps[2 * t + n][:, :], diag[:, k % 4, :], arena_v[:, k % RING, n * HALF:(n + 1) * HALF],
                                         start=False, stop=(final and k == TOPK - 1), skip_group_check=True)
                    last.then_inc(sem("v_used"), 1)

            def unit(t, head=None):
                add_experts(1 - t, range(8))
                if head is not None:
                    pe.wait_ge(sem("key_scores_taken"), count.take("key_scores_taken"))
                    key_scores(head)
                add_experts(1 - t, range(8, TOPK))

            def peer():
                hT_ready()
                pe.wait_ge(sem("peer_set"), count.take("peer_set"))
                key_scores(0)
                for k in range(4):
                    pe.matmul(ps[k][:, :], zeros, hT[:, 0:2, :].rearrange("p c s -> p (c s)"), start=True, stop=False,
                              skip_group_check=True)
                pe.wait_ge(sem("key_scores_taken"), count.take("key_scores_taken"))
                key_scores(1)
                per = {f"v{k}_landed": 64 for k in range(RING)}
                with count.loop(P_HEADS - 2, diag_ready=32, key_scores_taken=1, pq_ready=4, ring2_landed=16, **per) as i:
                    unit(1)
                    unit(0, i + 2)
                unit(1)
                unit(0)
                unit(1)
                add_experts(1, range(TOPK), final=True)

            def nsa_unit(branch, f):
                g = f // 2
                at = (C_VS, C_VW)[branch] + g * HD
                return (lambda m: hT[64 * m:64 * m + 64, f, :], lambda m: hT[64 * m:64 * m + 64, 4 + 2 * branch + g, :],
                        lambda m, t: proj[:, t, at:at + HD])

            def mla_unit(f):
                return (lambda m: mqT[:, 2 * f + m, :], lambda m: mkT[:, 2 * f + m, :],
                        lambda m, t: val[:, t, (2 * f + m) * HD:(2 * f + m + 1) * HD])

            def hybrid_attention():
                for c in range(NB):
                    for n, k in enumerate((0, 1, 4, 5, 2, 3, 6, 7)):
                        if c == 0 and k in (0, 5, 6, 7):
                            pe.wait_ge(sem("hT_split"), count.take("hT_split"))
                        if n % 4 == 0:
                            take_half(c % 2, n // 4, c % 4)
                        a = (k % 4) * HALF
                        z = min(a + HALF, C_END)
                        last = product(ps[k][:, 0:z - a],
                                       [x[:, c, (k // 4) * P:(k // 4) * P + P] for x in (hT_high, hT_low)],
                                       [x[:, a:z] for x in w_split[c % 2]], start=(c == 0), stop=(c == NB - 1))
                        if c == NB - 1:
                            last.then_inc(sem("proj_v_done" if k < 4 else "proj_a_done"), 1)
                    if c < NB - 1:
                        last.then_inc(sem(f"w{c % 2}_used"), 1)
                pe.wait_ge(sem("proj_a_done"), count.take("proj_a_done", 4))
                pe.sem_inc(sem("w1_used"), 1)
                pe.wait_ge(sem("proj_v"), count.take("proj_v", 4))
                pe.wait_ge(sem("proj_a"), count.take("proj_a", 4))
                for a in range(2):
                    for t in range(NT):
                        last = pe.transpose(ps[0][:, a * S + t * P:a * S + t * P + P],
                                            proj[:, t, C_KC + a * P:C_KC + a * P + P], ident)
                last.then_inc(sem("flow_turned"), 1)
                pe.wait_ge(sem("lora_ready"), count.take("lora_ready"))
                for c in range(3):
                    for t in range(NT):
                        last = pe.transpose(ps[1 + c // 2][:, (c % 2) * S + t * P:(c % 2) * S + t * P + P],
                                            lora[:, t, c * P:(c + 1) * P], ident)
                    if c:
                        last.then_inc(sem("lora_turned"), 1)
                pe.wait_ge(sem("loraT_ready"), count.take("loraT_ready", 2))
                slot = slot_of_turn()
                for t in range(NT):
                    for n, (a, z) in enumerate(((0, HALF), (HALF, 768))):
                        for c in range(2):
                            last = pe.matmul(ps[4 + 2 * t + n][:, 0:z - a], loraT[:, c, t * P:(t + 1) * P],
                                             ring[:, slot, c * 768 + a:c * 768 + z], start=(c == 0), stop=(c == 1))
                    last.then_inc(sem("mq_v_done" if t == 0 else "mq_a_done"), 1)
                pe.wait_ge(sem("mq_a_done"), count.take("mq_a_done"))
                pe.sem_inc(sem(f"ring{slot}_used"), 1)
                slot = slot_of_turn()
                pe.wait_ge(sem("flow_x0_ready"), count.take("flow_x0_ready"))
                for t in range(NT):
                    for n in range(2):
                        last = pe.matmul(ps[2 * t + n][:, :], loraT[:, 2, t * P:(t + 1) * P],
                                         ring[:, slot, n * HALF:(n + 1) * HALF], start=True, stop=True)
                    last.then_inc(sem("mkv_v_done" if t == 0 else "mkv_a_done"), 1)
                pe.wait_ge(sem("mkv_a_done"), count.take("mkv_a_done"))
                pe.sem_inc(sem(f"ring{slot}_used"), 1)
                pe.wait_ge(sem("mq_v"), count.take("mq_v"))
                pe.wait_ge(sem("mq_a"), count.take("mq_a"))
                turn_over(nat, ready="nat_ready")
                pe.wait_ge(sem("mkv_v"), count.take("mkv_v"))
                pe.wait_ge(sem("mkv_a"), count.take("mkv_a"))
                pe.wait_ge(sem("blocks_ready"), count.take("blocks_ready", 4))
                for a in range(2):
                    slots = (slot_of_turn(), slot_of_turn())
                    for b in range(2):
                        for j in range(16):
                            w = ring[:, slots[j // 8], :].rearrange("p (c n) -> p c n", c=8)[:, j % 8, :]
                            last = pe.matmul(ps[0][:, (2 * a + b) * 30:(2 * a + b + 1) * 30], w[:, b * P:(b + 1) * P],
                                             blocks[:, a, j, :], start=(j == 0), stop=(j == 15))
                    last.then_inc(sem("hidden_done"), 1)
                    pe.wait_ge(sem("hidden_done"), count.take("hidden_done"))
                    for slot in slots:
                        pe.sem_inc(sem(f"ring{slot}_used"), 1)
                pe.wait_ge(sem("hidden_ready"), count.take("hidden_ready"))
                for a in range(2):
                    for b in range(2):
                        last = pe.matmul(ps[1][0:30, a * HD:(a + 1) * HD], hidden[:, a, b, :], cmp_w2[:, a, b, :],
                                         start=(b == 0), stop=(b == 1))
                last.then_inc(sem("kcv_done"), 1)
                pe.wait_ge(sem("mqk_ready"), count.take("mqk_ready", 2))
                for n, bank in enumerate((2, 3, 4, 5, 6, 7, 0, 1)):
                    if bank == 1:
                        pe.wait_ge(sem("kc_ready"), count.take("kc_ready"))
                    src = (mq, mk)[n // 4]
                    for head in range(2):
                        for t in range(NT):
                            last = pe.transpose(ps[bank][0:QK, head * S + t * P:head * S + t * P + P],
                                                src[:, t, 2 * (n % 4) + head, :], ident)
                    last.then_inc(sem("m_turned_v" if n % 2 == 0 else "m_turned_a"), 1)
                pe.wait_ge(sem("mT_v"), count.take("mT_v", 4))
                pe.wait_ge(sem("mT_a"), count.take("mT_a", 4))
                pe.transpose(ps[2][:, 0:30], kc_twice, ident[0:30, 0:30]).then_inc(sem("kc_turned"), 1)
                hT_ready()
                pe.wait_ge(sem("kcT_ready"), count.take("kcT_ready"))
                for n in range(4 * NT):
                    for half in range(2):
                        at = slice(64 * half, 64 * half + 64)
                        last = pe.matmul(ps[2 + half][:, n * 30:(n + 1) * 30],
                                         hT[at, n // NT, (n % NT) * P:(n % NT + 1) * P], kcT[at, :],
                                         start=True, stop=True)
                last.then_inc(sem("c_scores_done"), 1)
                units = [nsa_unit(branch, f) for branch in range(2) for f in range(4)] + [mla_unit(f) for f in range(4)]
                scores(units[0][0], units[0][1], (0, 1))
                pe.wait_ge(sem("c_prob_ready"), count.take("c_prob_ready"))
                for n in range(8 * NT):
                    last = pe.transpose(ps[4 + n // 4][0:30, (n % 4) * P:(n % 4 + 1) * P],
                                        c_prob[:, n * 30:(n + 1) * 30], ident)
                    if n % 4 == 3:
                        last.then_inc(sem("c_turned_v" if n < 8 else "c_turned_a"), 1)
                pe.wait_ge(sem("c_probT_v"), count.take("c_probT_v", 2))
                scores(units[1][0], units[1][1], (4, 5))
                pe.wait_ge(sem("c_probT_a"), count.take("c_probT_a", 2))
                for n in range(8 * NT):
                    last = pe.matmul(ps[n // 8][:, (n % 8) * HD:(n % 8 + 1) * HD], c_probT[:, n * P:(n + 1) * P],
                                     kcv[:, HD:2 * HD], start=True, stop=True)
                    if n % 8 == 7:
                        last.then_inc(sem("c_weighed"), 1)
                for u in range(2, len(units) + 2):
                    turn_probs(u % 2)
                    if u == 2:
                        pe.wait_ge(sem("c_out"), count.take("c_out", 2))
                    if u < len(units):
                        scores(units[u][0], units[u][1], ((0, 1), (4, 5))[u % 2])
                    weigh(u % 2, units[u - 2][2], HD)

            pe.wait_ge(sem("bias_in_landed"), count.take("bias_in_landed", 32))
            pe.wait_ge(sem("relb_set"), count.take("relb_set"))
            pe.matmul(ps[0][0:HEADS, 0:384], relb_sb, bucket_sb, start=True, stop=True).then_inc(sem("bias_rows_ready"), 1)
            pe.wait_ge(sem("const_landed"), count.take("const_landed", 16))
            pe.wait_ge(sem("x_landed"), count.take("x_landed", 32))
            turn_over(h, split=True)
            attention_layer(P)
            turn_over(nat, ready="nat_ready", split=True)
            split_natural()
            turn_over(h, ready="h_ready", split=True)
            mlp()
            turn_over(h, ready="h_ready", split=True)
            attention_layer(HD)
            turn_over(nat, ready="nat_ready", split=True)
            split_natural()
            turn_over(h, ready="h_ready", split=True)
            mlp()
            turn_over(nat, ready="nat_ready", split=True)
            hybrid_attention()
            turn_over(nat, ready="nat_ready", split=True)
            split_natural()
            pe.wait_ge(sem("keys_landed"), count.take("keys_landed", 16))
            for b in range(2 * P_HEADS):
                last = pe.transpose(ps[4 + b // 4][:, (b % 4) * P:(b % 4 + 1) * P], keys[:, b, :], ident)
                if b % 4 == 3:
                    last.then_inc(sem("keys_turned"), 1)
            pe.wait_ge(sem("keysT_ready"), count.take("keysT_ready", 4))
            turn_over(nat, ready="nat_ready")
            peer()

        @block.scalar
        def _(sc):
            count = Count(sc)

            def take_turned():
                for c in range(2, 4):
                    sc.wait_ge(sem("turned_a"), count.take("turned_a"))
                    sc.activation(hT[:, 2 * c:2 * c + 2, :], ps[4 + c][:, :].rearrange("p (c s) -> p c s", c=2), ACT.Copy)\
                        .then_inc(sem("hT_a"), 1)

            def take_turned_high():
                for c in range(4):
                    sc.wait_ge(sem("turned_s"), count.take("turned_s"))
                    sc.activation(hT_high[:, 2 * c:2 * c + 2, :], ps[4 + c][:, :].rearrange("p (c s) -> p c s", c=2),
                                  ACT.Copy).then_inc(sem("hT_high"), 1)

            def split_high(slot, pair, free=None, width=2048):
                sc.wait_ge(sem(f"raw{slot}_landed"), count.take(f"raw{slot}_landed", 16))
                if free:
                    sc.wait_ge(sem(free), count.take(free))
                for half in range(2):
                    part = slice(half * D, min((half + 1) * D, width))
                    sc.activation(w_split[pair][0][:, part], ring[:, slot, part], ACT.Copy)\
                        .then_inc(sem("w_high"), 1)

            def v_high(c):
                if c % 2 == 0:
                    sc.wait_ge(sem(f"raw{c // 2}_landed"), count.take(f"raw{c // 2}_landed", 16))
                if c > 1:
                    sc.wait_ge(sem(f"w{c % 2}_used"), count.take(f"w{c % 2}_used"))
                sc.activation(v_split[c % 2][0][:, :], ring[:, c // 2, (c % 2) * D:(c % 2 + 1) * D], ACT.Copy)\
                    .then_inc(sem("w_high"), 1)

            def qk_high(b, part):
                if part == 0:
                    sc.wait_ge(sem(f"qk{b}_landed"), count.take(f"qk{b}_landed", 32))
                sc.activation(qk_split[part][0][:, :], qkring[:, b, part * D:(part + 1) * D], ACT.Copy)\
                    .then_inc(sem("w_high"), 1)

            def square_sum(t):
                sc.wait_ge(sem("norm_due"), count.take("norm_due"))
                sc.activation(tmp[:, t, :], h[:, t, :], ACT.Square, accum_out=sq_sum[:, t:t + 1])\
                    .then_inc(sem("squares_summed"), 1)

            def exps(b):
                for m in range(2):
                    for t, (a, z) in enumerate(((0, P), (P, 384))):
                        sc.wait_ge(sem("sco_ready"), count.take("sco_ready"))
                        sc.activation(prob[:, b, m, a:z], sco[:, b, m, a:z], ACT.Exp, bias=peak[:, b, m, t:t + 1],
                                      scale=-1.0, accum_out=total[:, b, m, t:t + 1]).then_inc(sem("probs_ready"), 1)

            def take_probT():
                sc.wait_ge(sem("probT_a_turned"), count.take("probT_a_turned"))
                sc.activation(probT[:, 1, :], ps[3][:, 0:384], ACT.Copy).then_inc(sem("probT_a"), 1)

            def take_projection(b, part):
                sc.wait_ge(sem("proj_ready"), count.take("proj_ready"))
                sc.activation(qkT[:, b, part, :], ps[4 + part][:, 0:S], ACT.Copy,
                              scale=-(HD ** -0.5) if part == 0 else 1.0).then_inc(sem("qkT_ready"), 1)

            def attend_block(b, more=True, split=True):
                exps(b)
                if more:
                    take_projection(1 - b, 0)
                if split:
                    qk_high(b, 0)
                take_probT()
                if more:
                    take_projection(1 - b, 1)
                if split:
                    qk_high(b, 1)

            def attention_layer(first=False):
                if first:
                    sc.wait_ge(sem("bias_rows_ready"), count.take("bias_rows_ready"))
                    sc.activation(bias_rows, ps[0][0:HEADS, 0:384], ACT.Copy).then_inc(sem("bias_rows_set"), 1)
                if not first:
                    sc.wait_ge(sem("w1_used"), count.take("w1_used"))
                v_high(0)
                if not first:
                    v_high(1)
                take_turned_high()
                if first:
                    v_high(1)
                    sc.wait_ge(sem("lam_summed"), count.take("lam_summed", 2))
                    sc.activation(lam_exp[:, 0:2], lam_sum, ACT.Exp).then_inc(sem("lam_exp"), 1)
                for c in range(2, 6):
                    v_high(c)
                qk_high(0, 0)
                qk_high(0, 1)
                v_high(6)
                v_high(7)
                count.skip("acc_ready", 2)
                for k in range(2):
                    sc.wait_ge(sem("acc_ready"), count.take("acc_ready"))
                    sc.activation(val[:, 1, k * HALF:(k + 1) * HALF], ps[2 + k][:, :], ACT.Copy).then_inc(sem("val_a"), 1)
                take_projection(0, 0)
                qk_high(1, 0)
                take_projection(0, 1)
                qk_high(1, 1)
                with count.loop(3, sco_ready=8, proj_ready=4, probT_a_turned=2, qk0_landed=32, qk1_landed=32):
                    attend_block(0)
                    attend_block(1)
                attend_block(0, split=False)
                attend_block(1, more=False, split=False)

            def out_and_mlp():
                split_high(0, 0)
                split_high(1, 1)
                take_turned_high()
                split_high(2, 0, "w0_used")
                split_high(3, 1, "w1_used")
                split_high(0, 0, "w0_used")
                count.skip("acc_ready", 4)
                take_turned_high()
                split_high(2, 1, "w1_used")

                def step(b, more=True, first=False):
                    if first or not more:
                        split_high(2 * b + 1, 1 - first, "up_ready")
                    else:
                        split_high(2 - 2 * b, 1, "up_ready")
                    sc.activation(relu[:, b, :], ps[4 + b][:, :], ACT.Relu).then_inc(sem("relu_ready"), 1)
                    sc.wait_ge(sem("relu_ready"), count.take("relu_ready"))
                    sc.activation(act_high[:, b, :], relu[:, b, :], ACT.Square).then_inc(sem("act_high"), 1)
                    if more and not first:
                        split_high(2 * b + 1, 0, "w0_used")

                step(0, first=True)
                with count.loop(N_CHUNK // 2 - 1, up_ready=2, relu_ready=2, w0_used=2, raw0_landed=16, raw1_landed=16,
                                raw2_landed=16, raw3_landed=16):
                    step(1)
                    step(0)
                step(1, more=False)
                count.skip("acc_ready", 4)
                count.skip("w0_used")

            def take_queries():
                for half in range(2):
                    sc.wait_ge(sem("peer_q_done"), count.take("peer_q_done"))
                    for dst, func in ((pq, ACT.Copy), (pq_sq, ACT.Square)):
                        sc.activation(dst[:, half * S:(half + 1) * S], ps[4 + half][:, 0:S], func)\
                            .then_inc(sem("pq_ready"), 1)

            def diagonals(b, ks, first=False):
                for k in ks:
                    if k >= 4 or not first:
                        sc.wait_ge(sem("v_used"), count.take("v_used"))
                    sc.activation(diag[:, k % 4, :], ident, ACT.Copy, scale=weight[:, 16 * b + k:16 * b + k + 1])\
                        .then_inc(sem("diag_ready"), 1)

            def gates_of(b):
                sc.wait_ge(sem("top_ready"), count.take("top_ready"))
                sc.activation(gate_w[:, 16 * b:16 * b + 16], top, ACT.Exp, bias=neg_top, accum_out=mass[:, b:b + 1])\
                    .then_inc(sem("gate_w_ready"), 1)

            def gelu_of():
                sc.wait_ge(sem("dot_done"), count.take("dot_done", 16))
                sc.activation(gelu, dots, ACT.Gelu_apprx_tanh).then_inc(sem("gelu_ready"), 1)

            def unit(t, queries=False, ahead=True, first=False):
                sc.wait_ge(sem("weight_ready"), count.take("weight_ready"))
                diagonals(1 - t, range(8), first)
                if queries:
                    take_queries()
                if ahead:
                    gates_of(1 - t)
                diagonals(1 - t, range(8, TOPK))
                gelu_of()

            def peer():
                take_queries()
                gates_of(0)
                take_queries()
                gates_of(1)
                gelu_of()
                unit(1, first=True)
                unit(0, queries=True)
                with count.loop(P_HEADS - 3, weight_ready=2, v_used=32, peer_q_done=2, top_ready=2, dot_done=32):
                    unit(1)
                    unit(0, queries=True)
                unit(1)
                unit(0)
                unit(1, ahead=False)
                sc.wait_ge(sem("weight_ready"), count.take("weight_ready"))
                diagonals(1, range(TOPK))

            def hybrid_attention():
                sc.wait_ge(sem("reduced_ready"), count.take("reduced_ready"))
                sc.activation(trig, reduced, ACT.Sin).then_inc(sem("trig_ready"), 1)
                for k in range(4):
                    a = k * HALF
                    z = min(a + HALF, C_END)
                    sc.wait_ge(sem("proj_a_done"), count.take("proj_a_done"))
                    sc.activation(sq[:, 1, a:z], ps[4 + k][:, 0:z - a], ACT.Square).then_inc(sem("sq_a"), 1)
                    sc.activation(proj[:, 1, a:z], ps[4 + k][:, 0:z - a], ACT.Copy).then_inc(sem("proj_a"), 1)
                sc.wait_ge(sem("proj_v"), count.take("proj_v", 4))
                sc.wait_ge(sem("proj_a"), count.take("proj_a", 4))
                sc.activation(gates.rearrange("p (t n) -> p t n", t=NT), proj[:, :, C_GATE:C_CQ], ACT.Sigmoid)\
                    .then_inc(sem("gates_ready"), 1)
                sc.wait_ge(sem("lora_turned"), count.take("lora_turned"))
                sc.activation(loraT[:, 0:2, :], ps[1][:, :].rearrange("p (c s) -> p c s", c=2), ACT.Copy)\
                    .then_inc(sem("loraT_ready"), 1)
                sc.wait_ge(sem("lora_turned"), count.take("lora_turned"))
                sc.activation(loraT[:, 2, :], ps[2][:, 0:S], ACT.Copy).then_inc(sem("loraT_ready"), 1)
                sc.wait_ge(sem("mq_a_done"), count.take("mq_a_done"))
                q1 = mq[:, 1, :, :].rearrange("p h n -> p (h n)")
                sc.activation(q1[:, 0:HALF], ps[6][:, :], ACT.Copy)
                sc.activation(q1[:, HALF:768], ps[7][:, 0:256], ACT.Copy).then_inc(sem("mq_a"), 1)
                sc.wait_ge(sem("mkv_a_done"), count.take("mkv_a_done"))
                for n in range(2):
                    kv = ps[2 + n][:, :].rearrange("p (h n) -> p h n", n=P)
                    sc.activation(mk[:, 1, 4 * n:4 * n + 4, 0:HD], kv[:, :, 0:HD], ACT.Copy)
                    last = sc.activation(val[:, 1, n * 256:(n + 1) * 256].rearrange("p (h n) -> p h n", n=HD),
                                         kv[:, :, HD:P], ACT.Copy)
                last.then_inc(sem("mkv_a"), 1)
                take_turned()
                sc.wait_ge(sem("hidden_done"), count.take("hidden_done", 2))
                sc.activation(hidden.rearrange("p a b n -> p (a b n)"), ps[0][:, 0:120], ACT.Gelu_apprx_tanh)\
                    .then_inc(sem("hidden_ready"), 1)
                for n in (1, 3, 5, 7):
                    sc.wait_ge(sem("m_turned_a"), count.take("m_turned_a"))
                    bank = (2, 3, 4, 5, 6, 7, 0, 1)[n]
                    sc.activation((mqT, mkT)[n // 4][:, 2 * (n % 4):2 * (n % 4) + 2, :],
                                  ps[bank][0:QK, :].rearrange("p (h s) -> p h s", h=2), ACT.Copy).then_inc(sem("mT_a"), 1)
                sc.wait_ge(sem("c_sco_ready"), count.take("c_sco_ready"))
                sc.activation(c_prob, c_sco, ACT.Exp, scale=-1.0).then_inc(sem("c_prob_ready"), 1)
                for n in range(2):
                    sc.wait_ge(sem("c_turned_a"), count.take("c_turned_a"))
                    sc.activation(c_probT[:, (2 + n) * HALF:(3 + n) * HALF], ps[6 + n][0:30, :], ACT.Copy)\
                        .then_inc(sem("c_probT_a"), 1)
                exps(0)
                exps(1)
                for u in range(2, 14):
                    take_probT()
                    if u < 12:
                        exps(u % 2)

            attention_layer(first=True)
            out_and_mlp()
            attention_layer()
            out_and_mlp()
            split_high(0, 0, "w1_used", width=C_END)
            square_sum(0)
            split_high(1, 1, width=C_END)
            square_sum(1)
            take_turned_high()
            for c in range(2, NB):
                split_high(c % 4, c % 2, f"w{c % 2}_used", width=C_END)
            hybrid_attention()
            split_high(2, 0, "w0_used")
            split_high(3, 1, "w1_used")
            take_turned_high()
            split_high(0, 0, "w0_used")
            split_high(1, 1, "w1_used")
            count.skip("acc_ready", 4)
            square_sum(0)
            square_sum(1)
            for n in range(4):
                sc.wait_ge(sem("keys_turned"), count.take("keys_turned"))
                sc.activation(keysT[:, n * HALF:(n + 1) * HALF], ps[4 + n][:, :], ACT.Copy)\
                    .then_inc(sem("keysT_ready"), 1)
            take_turned()
            peer()

        @block.gpsimd
        def _(po):
            count = Count(po)
            po.dma_start(lam_in, to_partitions(T["lam_a"][0].rearrange("a d -> (a d)"))).then_inc(sem("lam_landed"), 16)
            po.dma_start(subln, to_partitions(T["subln_a"][0])).then_inc(sem("subln_landed"), 16)
            po.memset(neg_half, -0.5).then_inc(sem("neg_half_set"), 1)
            po.wait_ge(sem("neg_half_set"), count.take("neg_half_set"))
            po.wait_ge(sem("bias_rows_set"), count.take("bias_rows_set"))
            pitch = HEADS * 384
            po.dma_start(bass.AP(shifted.tensor, 0, [[384, HEADS], [pitch + 1, P], [1, 384]]),
                         spread(bias_rows, (0, P), (1, 384))).then_inc(sem("shifted_stored"), 16)
            po.wait_ge(sem("shifted_stored"), count.take("shifted_stored", 16))
            for first, n, at in ((255, P, 0), (127, S, P)):
                src = bass.AP(shifted.tensor, first, [[pitch, P], [384, HEADS], [1, n]])
                po.dma_start(bias[:, :, at:at + n], src).then_inc(sem("bias_landed"), 16)
            for s, (g, b, layer) in enumerate((("ln1_g", "ln1_b", 0), ("ln2_g", "ln2_b", 0), ("ln1_g", "ln1_b", 1),
                                               ("ln2_g", "ln2_b", 1))):
                po.dma_start(ln_gb[:, s, 0, :], to_partitions(T[g][layer])).then_inc(sem("ln_landed"), 16)
                po.dma_start(ln_gb[:, s, 1, :], to_partitions(T[b][layer])).then_inc(sem("ln_landed"), 16)
            po.memset(pos_i[:, :], 0).then_inc(sem("pos_cleared"), 1)
            po.wait_ge(sem("pos_cleared"), count.take("pos_cleared"))
            pos = T["positions_2"]
            loads = [(pos_i[:, 0:2], bass.AP(pos.tensor, 0, [[1, P], [P, NT]])),
                     (pos_i[0:15, 2:3], bass.AP(pos.tensor, 31, [[16, N_CMP], [1, 1]])),
                     (pos_i[15:30, 2:3], bass.AP(pos.tensor, 31, [[16, N_CMP], [1, 1]])),
                     (freqs, to_partitions(T["freqs"])), (gain_q, to_partitions(T["nsa_q_gain_2"][0])),
                     (gain_ks, to_partitions(T["nsa_ks_gain_2"][0])), (gain_kw, to_partitions(T["nsa_kw_gain_2"][0])),
                     (gain_kc, to_partitions(T["nsa_kc_gain_2"][0])), (gain_mq, to_partitions(T["mla_q_gain_2"][0])),
                     (gain_mk, to_partitions(T["mla_k_gain_2"][0])), (gain_cq, to_partitions(T["mla_q_lora_gain_2"][0])),
                     (gain_ckv, to_partitions(T["mla_kv_lora_gain_2"][0])),
                     (cmp_posT[0:HD, :], bass.AP(T["cmp_pos_2"].tensor, 0, [[1, HD], [2 * HD, 16]])),
                     (cmp_posT[HD:P, :], bass.AP(T["cmp_pos_2"].tensor, HD, [[1, HD], [2 * HD, 16]])),
                     (cmp_w2[:, 0, :, :], T["cmp_k_w2_2"][0].rearrange("(b p) n -> p b n", p=P)),
                     (cmp_w2[:, 1, :, :], T["cmp_v_w2_2"][0].rearrange("(b p) n -> p b n", p=P))]
            assert len(loads) == N_SMALL
            for dst, src in loads:
                po.dma_start(dst, src, allow_slow_non_contiguous=True).then_inc(sem("small_landed"), 16)

            def power(dst, src, ready, done):
                po.wait_ge(sem(ready), count.take(ready))
                po.tensor_tensor(dst, src, neg_half[:, 0:src.shape[-1]] if len(src.shape) == 2 else neg_half, ALU.pow)\
                    .then_inc(sem(done), 1)

            def layer_norm():
                for t in range(NT):
                    power(rstd[:, t:t + 1], var_eps[:, t:t + 1], "var_ready", "rstd_ready")

            with count.loop(8, ms_ready=1):
                power(ms_out[:, 0:2], ms_in[:, 0:2], "ms_ready", "rms_ready")
            layer_norm()
            layer_norm()
            layer_norm()
            for dst, src in ((wide_gain[:, 0, :], "norm1_gain_2"), (wide_gain[:, 1, 0:HALF], "out_gain_a_2"),
                             (wide_gain[:, 1, HALF:D], "out_gain_b_2"), (wide_gain[:, 2, :], "norm2_gain_2")):
                po.dma_start(dst, to_partitions(T[src][0])).then_inc(sem("gains_landed"), 16)

            def rms(n, w):
                power(ms_out[:, n:n + w], ms_in[:, n:n + w], "ms_ready", "rms_ready")

            def wide_rms(t):
                po.wait_ge(sem("squares_summed"), count.take("squares_summed"))
                po.tensor_scalar(ms_in[:, t:t + 1], sq_sum[:, t:t + 1], 1.0 / D, EPS, ALU.mult, ALU.add)\
                    .then_inc(sem("mean_ready"), 1)
                power(ms_out[:, t:t + 1], ms_in[:, t:t + 1], "mean_ready", "rms_ready")

            for t in range(NT):
                power(rstd[:, t:t + 1], var_eps[:, t:t + 1], "var_ready", "rstd_ready")
                wide_rms(t)
            po.wait_ge(sem("small_landed"), count.take("small_landed", 16 * N_SMALL))
            rms(24, 4)
            rms(0, 24)
            po.wait_ge(sem("flow_landed"), count.take("flow_landed", 64))
            for a in range(2):
                for g in range(2):
                    po.tensor_tensor(blocks[:, a, :, 15 * g:15 * g + 15], spread(flow_x[:, a, g, :], (1, 16), (8, 15)),
                                     spread(cmp_posT, (1, 16), (0, 15)), ALU.add).then_inc(sem("blocks_ready"), 1)
            rms(0, 16)
            rms(16, 16)
            po.wait_ge(sem("kc_ms_ready"), count.take("kc_ms_ready"))
            po.tensor_tensor(rstd[0:30, 0:1], var_eps[0:30, 0:1], neg_half[0:30, 0:1], ALU.pow)\
                .then_inc(sem("kc_rms_ready"), 1)
            for n in range(4):
                rms(n, 1)
            wide_rms(0)
            wide_rms(1)
            def gather(table, rows_of, k, ring_of, name, wait):
                if wait:
                    po.wait_ge(sem("dot_done" if name == "u" else "v_used"), count.take("dot_done" if name == "u" else "v_used"))
                    alone()
                po.indirect_dma_start(ring_of[:, k % RING, :], None, table,
                                      bass.IndirectOffsetOnAxis(ap=rows_of[:, k:k + 1], axis=0))\
                    .then_inc(sem(f"{name}{k % RING}_landed"), 16)

            def alone():
                po.sem_inc(sem("gathers_due"), 1)

            peer_u, peer_v = T["peer_u_2"][0], T["peer_v_2"][0]

            def unit(t, add=True, power_at=None, u_first=False, v_first=False, dot=True):
                if dot:
                    po.wait_ge(sem("experts_ready"), count.take("experts_ready"))
                    alone()
                for k in range(TOPK + U_LEAD):
                    if add and k == U_LEAD:
                        po.wait_ge(sem("weight_ready"), count.take("weight_ready"))
                        alone()
                    if dot and k < TOPK:
                        gather(peer_u, expert_u[:, 16 * t:16 * t + 16], k, arena_u, "u", k >= RING or not u_first)
                    if add and k >= U_LEAD:
                        gather(peer_v, expert_v[:, 16 * (1 - t):16 * (1 - t) + 16], k - U_LEAD, arena_v, "v",
                               k - U_LEAD >= RING or not v_first)
                    if k == power_at:
                        power(ms_out[:, 0:2], ms_in[:, 0:2], "ms_ready", "rms_ready")

            power(ms_out[:, 0:2], ms_in[:, 0:2], "ms_ready", "rms_ready")
            po.wait_ge(sem("keysT_ready"), count.take("keysT_ready", 4))
            unit(0, add=False, u_first=True)
            unit(1, power_at=U_LEAD + 3, v_first=True)
            unit(0)
            with count.loop(P_HEADS - 2, experts_ready=2, weight_ready=2, dot_done=32, v_used=32, ms_ready=1):
                unit(1, power_at=U_LEAD + 3)
                unit(0)
            unit(1)
            unit(0, dot=False)

        @block.vector
        def _(ve):
            count = Count(ve)

            def then(ins):
                ins.then_inc(sem("v_chain"), 1)
                ve.wait_ge(sem("v_chain"), count.take("v_chain"))

            def take_turned():
                for c in range(2):
                    ve.wait_ge(sem("turned_v"), count.take("turned_v"))
                    ve.tensor_copy(hT[:, 2 * c:2 * c + 2, :], ps[4 + c][:, :].rearrange("p (c s) -> p c s", c=2))\
                        .then_inc(sem("hT_v"), 1)

            def take_turned_low(low=hT_low):
                for c in range(4):
                    ve.wait_ge(sem("hT_high"), count.take("hT_high"))
                    part = slice(2 * c, 2 * c + 2)
                    ve.tensor_tensor(low[:, part, :], ps[4 + c][:, :].rearrange("p (c s) -> p c s", c=2),
                                     hT_high[:, part, :].bitcast(F32), ALU.subtract).then_inc(sem("hT_split"), 1)

            def split_low(slot, pair, width=2048):
                for half in range(2):
                    ve.wait_ge(sem("w_high"), count.take("w_high"))
                    part = slice(half * D, min((half + 1) * D, width))
                    ve.tensor_tensor(w_split[pair][1][:, part], ring[:, slot, part],
                                     w_split[pair][0][:, part].bitcast(F32), ALU.subtract)\
                        .then_inc(sem(f"w{pair}_split"), 1)

            def v_low(c):
                ve.wait_ge(sem("w_high"), count.take("w_high"))
                ve.tensor_tensor(v_split[c % 2][1][:, :], ring[:, c // 2, (c % 2) * D:(c % 2 + 1) * D],
                                 v_split[c % 2][0][:, :].bitcast(F32), ALU.subtract).then_inc(sem(f"w{c % 2}_split"), 1)

            def qk_low(b, part):
                ve.wait_ge(sem("w_high"), count.take("w_high"))
                ve.tensor_tensor(qk_split[part][1][:, :], qkring[:, b, part * D:(part + 1) * D],
                                 qk_split[part][0][:, :].bitcast(F32), ALU.subtract).then_inc(sem(f"qk_split{part}"), 1)

            def add_bias(b, banks, table):
                for m in range(2):
                    ve.wait_ge(sem("scores_ready"), count.take("scores_ready"))
                    for t, (a, z) in enumerate(((0, P), (P, 384))):
                        ve.tensor_tensor_reduce(sco[:, b, m, a:z], ps[banks[m]][:, a:z], table(m)[:, a:z], 1.0, 3e38,
                                                ALU.add, ALU.min, peak[:, b, m, t:t + 1]).then_inc(sem("sco_ready"), 1)

            def add_moving_bias(b, table):
                for m in range(2):
                    ve.wait_ge(sem("scores_ready"), count.take("scores_ready"))
                    then(ve.tensor_tensor(sco[:, b, m, :], ps[m][:, 0:384], table(m), ALU.add))
                    for t, (a, z) in enumerate(((0, P), (P, 384))):
                        ve.tensor_reduce(peak[:, b, m, t:t + 1], sco[:, b, m, a:z], X, ALU.min)\
                            .then_inc(sem("sco_ready"), 1)

            def take_probT(b):
                ve.wait_ge(sem("probT_v_turned"), count.take("probT_v_turned"))
                ve.tensor_copy(probT[:, 0, :], ps[2][:, 0:384]).then_inc(sem("probT_v"), 1)

            def differential(f, b, meanwhile=lambda: None):
                ve.wait_ge(sem("probs_ready"), count.take("probs_ready", 4))
                then(ve.reciprocal(share[:, b, :, :], total[:, b, :, :]))
                then(ve.tensor_scalar(share[:, b, 1, :], share[:, b, 1, :], lam_exp[:, 2:3], None, ALU.mult))
                ve.wait_ge(sem("weighed"), count.take("weighed"))
                for t in range(NT):
                    then(ve.tensor_scalar(omap[:, t, :], ps[6 + b][:, (2 + t) * P:(3 + t) * P], share[:, b, 1, t:t + 1],
                                          None, ALU.mult))
                for t in range(NT):
                    then(ve.scalar_tensor_tensor(out=omap[:, t, :], in0=ps[6 + b][:, t * P:(t + 1) * P],
                                                 scalar=share[:, b, 0, t:t + 1], in1=omap[:, t, :], op0=ALU.mult,
                                                 op1=ALU.add))
                for t in range(NT):
                    then(ve.tensor_tensor_reduce(tmp[:, 1, t * P:(t + 1) * P], omap[:, t, :], omap[:, t, :], 1.0, 0.0,
                                                 ALU.mult, ALU.add, sq_sum[:, t:t + 1]))
                ve.tensor_scalar(ms_in[:, 0:2], sq_sum[:, 0:2], 1.0 / P, LN_EPS, ALU.mult, ALU.add)\
                    .then_inc(sem("ms_ready"), 1)
                meanwhile()
                ve.wait_ge(sem("rms_ready"), count.take("rms_ready"))
                for t in range(NT):
                    last = ve.scalar_tensor_tensor(out=nat[:, t, bass.ds(f * P, P)], in0=omap[:, t, :],
                                                   scalar=ms_out[:, t:t + 1], in1=subln, op0=ALU.mult, op1=ALU.mult)
                then(last)

            def plain(f, b, meanwhile=lambda: None):
                ve.wait_ge(sem("probs_ready"), count.take("probs_ready", 4))
                then(ve.reciprocal(share[:, b, :, :], total[:, b, :, :]))
                ve.wait_ge(sem("weighed"), count.take("weighed"))
                for m in range(2):
                    for t in range(NT):
                        last = ve.tensor_scalar(nat[:, t, bass.ds(f * P + m * HD, HD)],
                                                ps[6 + b][:, (2 * m + t) * HD:(2 * m + t + 1) * HD],
                                                share[:, b, m, t:t + 1], None, ALU.mult)
                then(last)
                meanwhile()

            def attend_block(f, b, finish, first=False, split=True):
                add_moving_bias(b, lambda m: bias[:, bass.ds(f * 2 + m, 1), :].rearrange("p a k -> p (a k)"))
                if first:
                    take_probT(b)
                else:
                    finish(f - 1, 1 - b, lambda: take_probT(b))
                if split:
                    qk_low(b, 0)
                    qk_low(b, 1)

            def attention_layer(finish, **per):
                v_low(0)
                if finish is not differential:
                    v_low(1)
                take_turned_low(hT_low_qkv)
                if finish is differential:
                    v_low(1)
                    differential_weight()
                for c in range(2, 6):
                    v_low(c)
                qk_low(0, 0)
                qk_low(0, 1)
                v_low(6)
                v_low(7)
                for k in range(2):
                    ve.wait_ge(sem("acc_ready"), count.take("acc_ready"))
                    ve.tensor_copy(val[:, 0, k * HALF:(k + 1) * HALF], ps[k][:, :]).then_inc(sem("val_v"), 1)
                count.skip("acc_ready", 2)
                qk_low(1, 0)
                qk_low(1, 1)
                if finish is differential:
                    ve.wait_ge(sem("bias_landed"), count.take("bias_landed", 32))
                attend_block(0, 0, finish, first=True)
                with count.loop(2, scores_ready=4, probs_ready=8, probT_v_turned=2, weighed=2, w_high=4, **per) as i:
                    attend_block(i * 2 + 1, 1, finish)
                    attend_block(i * 2 + 2, 0, finish)
                attend_block(5, 1, finish)
                attend_block(6, 0, finish, split=False)
                attend_block(7, 1, finish, split=False)
                finish(7, 1)

            def add_residual(scale, then_do=lambda t: None):
                for t in range(NT):
                    for k in range(2):
                        ve.wait_ge(sem("acc_ready"), count.take("acc_ready"))
                        part = h[:, t, k * HALF:(k + 1) * HALF]
                        then(ve.scalar_tensor_tensor(out=part, in0=part, scalar=scale, in1=ps[2 * t + k][:, :],
                                                     op0=ALU.mult, op1=ALU.add))
                    then_do(t)

            def layer_norm(s, then_do=None):
                if s == 0:
                    ve.wait_ge(sem("ln_landed"), count.take("ln_landed", 128))
                for t in range(NT):
                    for k in range(2):
                        ve.wait_ge(sem("acc_ready"), count.take("acc_ready"))
                        part = h[:, t, k * HALF:(k + 1) * HALF]
                        then(ve.scalar_tensor_tensor(out=part, in0=part, scalar=ALPHA, in1=ps[2 * t + k][:, :],
                                                     op0=ALU.mult, op1=ALU.add))
                        then(ve.bn_stats(stats[:, 6 * k:6 * k + 6], part))
                    then(ve.bn_aggr(moments[:, 2 * t:2 * t + 2], stats[:, 0:12].rearrange("p (k s) -> p k s", k=2)))
                    ve.tensor_scalar(var_eps[:, t:t + 1], moments[:, 2 * t + 1:2 * t + 2], LN_EPS, None, ALU.add)\
                        .then_inc(sem("var_ready"), 1)
                    then(ve.scalar_tensor_tensor(out=h[:, t, :], in0=h[:, t, :], scalar=moments[:, 2 * t:2 * t + 1],
                                                 in1=ln_gb[:, s, 0, :], op0=ALU.subtract, op1=ALU.mult))
                    ve.wait_ge(sem("rstd_ready"), count.take("rstd_ready"))
                    last = ve.scalar_tensor_tensor(out=h[:, t, :], in0=h[:, t, :], scalar=rstd[:, t:t + 1],
                                                   in1=ln_gb[:, s, 1, :], op0=ALU.mult, op1=ALU.add)
                    if then_do:
                        then(last)
                        then_do(t)
                    else:
                        last.then_inc(sem("h_ready"), 1)

            def out_and_mlp(s, then_do=None):
                split_low(0, 0)
                split_low(1, 1)
                take_turned_low()
                split_low(2, 0)
                split_low(3, 1)
                split_low(0, 0)
                layer_norm(s)
                take_turned_low()
                split_low(2, 1)

                def step(b, more=True, first=False):
                    if first or not more:
                        split_low(2 * b + 1, 1 - first)
                    else:
                        split_low(2 - 2 * b, 1)
                    ve.wait_ge(sem("relu_ready"), count.take("relu_ready"))
                    then(ve.tensor_tensor(act_sq[:, b, :], relu[:, b, :], relu[:, b, :], ALU.mult))
                    ve.wait_ge(sem("act_high"), count.take("act_high"))
                    ve.tensor_tensor(act_low[:, b, :], act_sq[:, b, :], act_high[:, b, :].bitcast(F32), ALU.subtract)\
                        .then_inc(sem("act_ready"), 1)
                    if more and not first:
                        split_low(2 * b + 1, 0)

                step(0, first=True)
                with count.loop(N_CHUNK // 2 - 1, w_high=8, relu_ready=2, act_high=2, v_chain=2):
                    step(1)
                    step(0)
                step(1, more=False)
                layer_norm(s + 1, then_do)

            def rms_of(src, at, width, n_cols=1):
                for n in range(n_cols):
                    a = n * width
                    then(ve.tensor_tensor_reduce(tmp[:, 0, 0:width], src[:, a:a + width], src[:, a:a + width], 1.0, 0.0,
                                                 ALU.mult, ALU.add, sq_sum[:, at + n:at + n + 1]))
                ve.tensor_scalar(ms_in[:, at:at + n_cols], sq_sum[:, at:at + n_cols], 1.0 / width, EPS, ALU.mult,
                                 ALU.add).then_inc(sem("ms_ready"), 1)

            def wide_scale(t, gain):
                ve.wait_ge(sem("rms_ready"), count.take("rms_ready"))
                ve.scalar_tensor_tensor(out=nat[:, t, :], in0=h[:, t, :], scalar=ms_out[:, t:t + 1],
                                        in1=wide_gain[:, gain, :], op0=ALU.mult, op1=ALU.mult)\
                    .then_inc(sem("nat_ready"), 1)

            def norm1(t):
                if t == 0:
                    ve.wait_ge(sem("small_landed"), count.take("small_landed", 16 * N_SMALL))
                    ve.wait_ge(sem("gains_landed"), count.take("gains_landed", 64))
                ve.sem_inc(sem("norm_due"), 1)
                if t == 1:
                    wide_scale(0, 0)
                    wide_scale(1, 0)

            def norm2(t):
                ve.sem_inc(sem("norm_due"), 1)
                if t == 1:
                    wide_scale(0, 2)
                    wide_scale(1, 2)

            def rope(x1, x2, c, s, shape):
                n = shape[0] * shape[1] * shape[2]
                steps = (shape[1] * shape[2], shape[0]), (shape[2], shape[1]), (1, shape[2])
                t = [spread(rope_tmp[0:x1.shape[0], k, :], *steps) for k in range(4)]
                for k, (u, v) in enumerate(((x1, c), (x2, s), (x2, c), (x1, s))):
                    then(ve.tensor_tensor(t[k], u, v, ALU.mult))
                then(ve.tensor_tensor(x1, t[0], t[1], ALU.subtract))
                then(ve.tensor_tensor(x2, t[2], t[3], ALU.add))

            def angles():
                then(ve.tensor_copy(pos_f, pos_i[:, :]))
                then(ve.tensor_tensor(spread(angle, (24, 3), (1, 24)), spread(pos_f, (1, 3), (0, 24)),
                                      spread(freqs, (0, 3), (1, 24)), ALU.mult))
                for n, phase in enumerate((0.25, 0.0)):
                    then(ve.tensor_scalar(cycles[:, 72 * n:72 * n + 72], angle, 1 / (2 * math.pi), phase, ALU.mult, ALU.add))
                    then(ve.tensor_copy(reduced[:, 72 * n:72 * n + 72], angle))
                then(ve.tensor_scalar(cycles, cycles, 1.5 * 2 ** 23, None, ALU.add))
                then(ve.tensor_scalar(cycles, cycles, -1.5 * 2 ** 23, None, ALU.add))
                rest = 2 * math.pi
                for bits in (2, 10, 18, None):
                    part = rest if bits is None else math.floor(rest * 2 ** bits) / 2 ** bits
                    rest -= part
                    then(ve.scalar_tensor_tensor(out=reduced, in0=cycles, scalar=-part, in1=reduced, op0=ALU.mult,
                                                 op1=ALU.add))
                then(ve.tensor_scalar(reduced[:, 0:72], reduced[:, 0:72], math.pi / 2, None, ALU.add))
                limit = float(np.nextafter(np.float32(math.pi), np.float32(0)))
                ve.tensor_scalar(reduced, reduced, limit, -limit, ALU.min, ALU.max).then_inc(sem("reduced_ready"), 1)

            def hybrid_attention():
                for k in range(4):
                    a = k * HALF
                    z = min(a + HALF, C_END)
                    ve.wait_ge(sem("proj_v_done"), count.take("proj_v_done"))
                    ve.tensor_copy(proj[:, 0, a:z], ps[k][:, 0:z - a]).then_inc(sem("proj_v"), 1)
                    ve.wait_ge(sem("proj_v"), count.take("proj_v"))
                then(ve.tensor_tensor(sq[:, 0, C_CQ:C_KR], proj[:, 0, C_CQ:C_KR], proj[:, 0, C_CQ:C_KR], ALU.mult))
                ve.wait_ge(sem("sq_a"), count.take("sq_a", 4))
                ve.tensor_reduce(sq_sum[:, 24:26], sq[:, :, C_CQ:C_CKV], X, ALU.add)
                then(ve.tensor_reduce(sq_sum[:, 26:28], sq[:, :, C_CKV:C_KR], X, ALU.add))
                then(ve.tensor_scalar(ms_in[:, 24:26], sq_sum[:, 24:26], 1.0 / 256, EPS, ALU.mult, ALU.add))
                ve.tensor_scalar(ms_in[:, 26:28], sq_sum[:, 26:28], 1.0 / 128, EPS, ALU.mult, ALU.add)\
                    .then_inc(sem("ms_ready"), 1)
                ve.wait_ge(sem("flow_turned"), count.take("flow_turned"))
                for a in range(2):
                    last = ve.tensor_copy(flow_x0[:, a, :, :].rearrange("p r i -> p i r"),
                                          ps[0][:, a * S:(a + 1) * S].rearrange("p (i r) -> p i r", r=2))
                then(last)
                ve.sem_inc(sem("flow_x0_ready"), 2)
                ve.tensor_tensor(sq[:, 0, C_Q:C_KC], proj[:, 0, C_Q:C_KC], proj[:, 0, C_Q:C_KC], ALU.mult)
                then(ve.tensor_tensor(sq[:, 0, C_KS:C_VW], proj[:, 0, C_KS:C_VW], proj[:, 0, C_KS:C_VW], ALU.mult))
                for t in range(NT):
                    ve.tensor_reduce(sq_sum[:, 12 * t:12 * t + 8], sq[:, t, C_Q:C_KC].rearrange("p (g d) -> p g d", d=HD),
                                     X, ALU.add)
                    for n, at in enumerate((C_KS, C_KW)):
                        last = ve.tensor_reduce(sq_sum[:, 12 * t + 8 + 2 * n:12 * t + 10 + 2 * n],
                                                sq[:, t, at:at + P].rearrange("p (g d) -> p g d", d=HD), X, ALU.add)
                then(last)
                ve.tensor_scalar(ms_in[:, 0:24], sq_sum[:, 0:24], 1.0 / HD, EPS, ALU.mult, ALU.add)\
                    .then_inc(sem("ms_ready"), 1)
                ve.wait_ge(sem("rms_ready"), count.take("rms_ready"))
                ve.wait_ge(sem("proj_a"), count.take("proj_a", 4))
                for t in range(NT):
                    ve.scalar_tensor_tensor(out=lora[:, t, 0:256], in0=proj[:, t, C_CQ:C_CKV],
                                            scalar=ms_out[:, 24 + t:25 + t], in1=gain_cq, op0=ALU.mult, op1=ALU.mult)
                    last = ve.scalar_tensor_tensor(out=lora[:, t, 256:384], in0=proj[:, t, C_CKV:C_KR],
                                                   scalar=ms_out[:, 26 + t:27 + t], in1=gain_ckv, op0=ALU.mult,
                                                   op1=ALU.mult)
                last.then_inc(sem("lora_ready"), 1)
                ve.wait_ge(sem("rms_ready"), count.take("rms_ready"))
                for t in range(NT):
                    q = nat[:, t, 0:HALF].rearrange("p (g d) -> p g d", d=HD)
                    then(ve.tensor_tensor(q, proj[:, t, C_Q:C_KC].rearrange("p (g d) -> p g d", d=HD),
                                          spread(ms_out[:, 12 * t:12 * t + 8], (1, 8), (0, HD)), ALU.mult))
                    then(ve.tensor_tensor(q, q, spread(gain_q, (0, 8), (1, HD)), ALU.mult))
                    for n, (at, group, gain) in enumerate(((C_KS, 8, gain_ks), (C_KW, 10, gain_kw))):
                        k = nat[:, t, HALF + 256 * n:HALF + 256 * n + 256].rearrange("p (g c d) -> p g c d", g=2, c=2)
                        then(ve.tensor_tensor(k[:, :, 0, :], proj[:, t, at:at + P].rearrange("p (g d) -> p g d", d=HD),
                                              spread(ms_out[:, 12 * t + group:12 * t + group + 2], (1, 2), (0, HD)), ALU.mult))
                        then(ve.tensor_tensor(k[:, :, 0, :], k[:, :, 0, :], spread(gain, (0, 2), (1, HD)), ALU.mult))
                        then(ve.tensor_copy(k[:, :, 1, :], k[:, :, 0, :]))
                ve.wait_ge(sem("trig_ready"), count.take("trig_ready"))
                x = nat[:, :, :].rearrange("p t (g d) -> p t g d", d=HD)
                rope(x[:, :, :, 0:8], x[:, :, :, 8:16], spread(cos, (24, NT), (0, 16), (1, 8)),
                     spread(sin, (24, NT), (0, 16), (1, 8)), (NT, 16, 8))
                ve.sem_inc(sem("nat_ready"), 2)
                ve.wait_ge(sem("mq_v_done"), count.take("mq_v_done"))
                q0 = mq[:, 0, :, :].rearrange("p h n -> p (h n)")
                ve.tensor_copy(q0[:, 0:HALF], ps[4][:, :])
                ve.tensor_copy(q0[:, HALF:768], ps[5][:, 0:256]).then_inc(sem("mq_v"), 1)
                ve.wait_ge(sem("mkv_v_done"), count.take("mkv_v_done"))
                for n in range(2):
                    kv = ps[n][:, :].rearrange("p (h n) -> p h n", n=P)
                    ve.tensor_copy(mk[:, 0, 4 * n:4 * n + 4, 0:HD], kv[:, :, 0:HD])
                    last = ve.tensor_copy(val[:, 0, n * 256:(n + 1) * 256].rearrange("p (h n) -> p h n", n=HD),
                                          kv[:, :, HD:P])
                last.then_inc(sem("mkv_v"), 1)
                for t in range(NT):
                    then(ve.tensor_copy(mk[:, t, :, HD:QK], spread(proj[:, t, C_KR:C_END], (0, MLA_HEADS), (1, 32))))
                take_turned()
                ve.wait_ge(sem("mkv_a"), count.take("mkv_a"))
                ve.wait_ge(sem("mq_a"), count.take("mq_a"))
                ve.wait_ge(sem("mkv_v"), count.take("mkv_v"))
                for n, src in enumerate((mq, mk)):
                    flat = src.rearrange("p t h n -> p (t h n)")
                    then(ve.tensor_tensor(av[:, 1536 * n:1536 * n + 1536], flat, flat, ALU.mult))
                    then(ve.tensor_reduce(sq_sum[:, 16 * n:16 * n + 16],
                                          av[:, 1536 * n:1536 * n + 1536].rearrange("p (g d) -> p g d", d=QK), X, ALU.add))
                    ve.tensor_scalar(ms_in[:, 16 * n:16 * n + 16], sq_sum[:, 16 * n:16 * n + 16], 1.0 / QK, EPS,
                                     ALU.mult, ALU.add).then_inc(sem("ms_ready"), 1)
                for n, (src, gain) in enumerate(((mq, gain_mq), (mk, gain_mk))):
                    flat = src.rearrange("p t h n -> p (t h) n")
                    then(ve.tensor_tensor(flat, flat, spread(gain, (0, 16), (1, QK)), ALU.mult))
                    ve.wait_ge(sem("rms_ready"), count.take("rms_ready"))
                    then(ve.tensor_tensor(flat, flat, spread(ms_out[:, 16 * n:16 * n + 16], (1, 16), (0, QK)), ALU.mult))
                    rope(src[:, :, :, HD:HD + 16], src[:, :, :, HD + 16:QK],
                         spread(cos[:, 8:72], (24, NT), (0, MLA_HEADS), (1, 16)),
                         spread(sin[:, 8:72], (24, NT), (0, MLA_HEADS), (1, 16)), (NT, MLA_HEADS, 16))
                    ve.sem_inc(sem("mqk_ready"), 1)
                ve.wait_ge(sem("kcv_done"), count.take("kcv_done"))
                then(ve.tensor_copy(kcv, ps[1][0:30, 0:P]))
                then(ve.tensor_tensor_reduce(kc_sq, kcv[:, 0:HD], kcv[:, 0:HD], 1.0, 0.0, ALU.mult, ALU.add,
                                             sq_sum[0:30, 0:1]))
                ve.tensor_scalar(var_eps[0:30, 0:1], sq_sum[0:30, 0:1], 1.0 / HD, EPS, ALU.mult, ALU.add)\
                    .then_inc(sem("kc_ms_ready"), 1)
                ve.wait_ge(sem("kc_rms_ready"), count.take("kc_rms_ready"))
                kc = kc_twice[:, 0:HD]
                then(ve.scalar_tensor_tensor(out=kc, in0=kcv[:, 0:HD], scalar=rstd[0:30, 0:1], in1=gain_kc[0:30, :],
                                             op0=ALU.mult, op1=ALU.mult))
                rope(spread(kc[:, 0:8], (0, 1), (0, 1), (1, 8)), spread(kc[:, 8:16], (0, 1), (0, 1), (1, 8)),
                     spread(cos[0:30, 48:56], (0, 1), (0, 1), (1, 8)), spread(sin[0:30, 48:56], (0, 1), (0, 1), (1, 8)),
                     (1, 1, 8))
                ve.tensor_copy(kc_twice[:, HD:P], kc).then_inc(sem("kc_ready"), 1)
                for n in (0, 2, 4, 6):
                    ve.wait_ge(sem("m_turned_v"), count.take("m_turned_v"))
                    bank = (2, 3, 4, 5, 6, 7, 0, 1)[n]
                    ve.tensor_copy((mqT, mkT)[n // 4][:, 2 * (n % 4):2 * (n % 4) + 2, :],
                                   ps[bank][0:QK, :].rearrange("p (h s) -> p h s", h=2)).then_inc(sem("mT_v"), 1)
                ve.wait_ge(sem("kc_turned"), count.take("kc_turned"))
                ve.tensor_copy(kcT, ps[2][:, 0:30]).then_inc(sem("kcT_ready"), 1)
                ve.wait_ge(sem("c_scores_done"), count.take("c_scores_done"))
                for g in range(2):
                    for half in range(2):
                        ve.tensor_tensor(spread(c_sco[:, 240 * g + 60 * half:], (120, 2), (1, 60)),
                                         ps[2 + half][:, 120 * g:120 * g + 120].rearrange("p (f n) -> p f n", f=2),
                                         spread(cmp_mask[:, 60 * g:60 * g + 60], (0, 2), (1, 60)), ALU.add)\
                            .then_inc(sem("v_chain"), 1)
                        ve.wait_ge(sem("v_chain"), count.take("v_chain"))
                by_row = c_sco.rearrange("p (r n) -> p r n", n=30)
                then(ve.tensor_reduce(c_peak, by_row, X, ALU.min))
                ve.tensor_tensor(by_row, by_row, spread(c_peak, (1, 16), (0, 30)), ALU.subtract).then_inc(sem("c_sco_ready"), 1)
                add_bias(0, (0, 1), lambda m: causal)
                ve.wait_ge(sem("c_prob_ready"), count.take("c_prob_ready"))
                then(ve.tensor_reduce(c_total, c_prob.rearrange("p (r n) -> p r n", n=30), X, ALU.add))
                then(ve.reciprocal(c_share, c_total))
                then(ve.tensor_tensor(spread(c_share, (2, 8), (1, 2)), spread(c_share, (2, 8), (1, 2)),
                                      spread(row_seen, (0, 8), (1, 2)), ALU.mult))
                ve.wait_ge(sem("gates_ready"), count.take("gates_ready"))
                then(ve.tensor_tensor(spread(c_share, (2, 8), (1, 2)), spread(c_share, (2, 8), (1, 2)),
                                      spread(gates, (3, 8), (24, 2)), ALU.mult))
                for n in range(2):
                    ve.wait_ge(sem("c_turned_v"), count.take("c_turned_v"))
                    ve.tensor_copy(c_probT[:, n * HALF:(n + 1) * HALF], ps[4 + n][0:30, :]).then_inc(sem("c_probT_v"), 1)
                add_bias(1, (4, 5), lambda m: causal)
                for n in range(2):
                    ve.wait_ge(sem("c_weighed"), count.take("c_weighed"))
                    o = nat[:, :, 256 * n:256 * n + 256].rearrange("p t (h d) -> p h t d", d=HD)
                    ve.tensor_tensor(o, ps[n][:, :].rearrange("p (h t d) -> p h t d", h=4, t=NT),
                                     spread(c_share[:, 8 * n:8 * n + 8], (2, 4), (1, 2), (0, HD)), ALU.mult)\
                        .then_inc(sem("c_out"), 1)
                ve.wait_ge(sem("c_out"), count.take("c_out", 2))

                def share_of(u, b):
                    ve.wait_ge(sem("probs_ready"), count.take("probs_ready", 4))
                    then(ve.reciprocal(share[:, b, :, :], total[:, b, :, :]))
                    f = u % 4
                    if u < 8:
                        gate = gates[:, 3 * 2 * f + 1 + u // 4:3 * 2 * f + 2 + u // 4]
                        then(ve.tensor_tensor(share[:, b, :, :], share[:, b, :, :], spread(gate, (3, 2), (24, 2)), ALU.mult))

                def finish(u, b):
                    f = u % 4
                    ve.wait_ge(sem("weighed"), count.take("weighed"))
                    for m in range(2):
                        for t in range(NT):
                            src = ps[6 + b][:, (2 * m + t) * HD:(2 * m + t + 1) * HD]
                            at = (0 if u < 8 else HALF) + (2 * f + m) * HD
                            dst = nat[:, t, at:at + HD]
                            if u < 8:
                                last = ve.scalar_tensor_tensor(out=dst, in0=src, scalar=share[:, b, m, t:t + 1], in1=dst,
                                                               op0=ALU.mult, op1=ALU.add)
                            else:
                                last = ve.tensor_scalar(dst, src, share[:, b, m, t:t + 1], None, ALU.mult)
                    then(last)

                def out_rms(n):
                    for t in range(NT):
                        rms_of(nat[:, t, n * HALF:(n + 1) * HALF], 2 * n + t, HALF)

                def out_scale(n):
                    for t in range(NT):
                        ve.wait_ge(sem("rms_ready"), count.take("rms_ready"))
                        part = nat[:, t, n * HALF:(n + 1) * HALF]
                        last = ve.scalar_tensor_tensor(out=part, in0=part, scalar=ms_out[:, 2 * n + t:2 * n + t + 1],
                                                       in1=wide_gain[:, 1, n * HALF:(n + 1) * HALF], op0=ALU.mult,
                                                       op1=ALU.mult)
                        if n == 1:
                            last.then_inc(sem("nat_ready"), 1)

                for u in range(2, 14):
                    take_probT(u % 2)
                    share_of(u - 2, u % 2)
                    if u == 12:
                        out_rms(0)
                    if u == 13:
                        out_scale(0)
                    if u < 12:
                        add_bias(u % 2, ((0, 1), (4, 5))[u % 2], lambda m: causal)
                    finish(u - 2, u % 2)
                out_rms(1)
                out_scale(1)

            def settle():
                ve.memset(settled, 0.0)

            def query_rms():
                ve.wait_ge(sem("peer_sq_done"), count.take("peer_sq_done"))
                ve.tensor_scalar(ms_in[:, 0:2], ps[7][:, 0:2], 1.0 / 256, EPS, ALU.mult, ALU.add)\
                    .then_inc(sem("ms_ready"), 1)

            def choose(t):
                if t == 0:
                    ve.wait_ge(sem("rms_ready"), count.take("rms_ready"))
                    ve.wait_ge(sem("key_scores_done"), count.take("key_scores_done"))
                    for tile in range(NT):
                        last = ve.tensor_scalar(key_sco[:, tile, :], ps[6][:, tile * S:(tile + 1) * S],
                                                ms_out[:, tile:tile + 1], None, ALU.mult)
                    then(last)
                    ve.sem_inc(sem("key_scores_taken"), 1)
                s = [key_sco[:, t, half * P:(half + 1) * P] for half in range(2)]
                left = [key_left[:, half * P:(half + 1) * P] for half in range(2)]

                def eight(half, n):
                    return best[:, 16 * half + 8 * n:16 * half + 8 * n + 8]

                def eight_keys(half, n):
                    return best_key[:, 16 * half + 8 * n:16 * half + 8 * n + 8]

                settle()
                for half in range(2):
                    ve.max(eight(half, 0), s[half]).then_inc(sem("v_chain"), 1)
                ve.wait_ge(sem("v_chain"), count.take("v_chain", 2))
                settle()
                for half in range(2):
                    ve.max_index(eight_keys(half, 0), eight(half, 0), s[half])
                    ve.match_replace(left[half], eight(half, 0), s[half], -3e38).then_inc(sem("v_chain"), 1)
                ve.wait_ge(sem("v_chain"), count.take("v_chain", 2))
                settle()
                for half in range(2):
                    ve.max(eight(half, 1), left[half]).then_inc(sem("v_chain"), 1)
                ve.wait_ge(sem("v_chain"), count.take("v_chain", 2))
                settle()
                for half in range(2):
                    ve.max_index(eight_keys(half, 1), eight(half, 1), left[half]).then_inc(sem("v_chain"), 1)
                ve.wait_ge(sem("v_chain"), count.take("v_chain", 2))
                ve.tensor_copy(best_key_f, best_key)
                then(ve.tensor_tensor(spread(pairs, (16, 16), (1, 16)), spread(best[:, 0:16], (1, 16), (0, 16)),
                                      spread(best[:, 16:32], (0, 16), (1, 16)), ALU.add))
                settle()
                ve.max(top[:, 0:8], pairs).then_inc(sem("v_chain"), 1)
                ve.wait_ge(sem("v_chain"), count.take("v_chain"))
                settle()
                ve.max_index(top_pair[:, 0:8], top[:, 0:8], pairs)
                ve.match_replace(pairs_left, top[:, 0:8], pairs, -3e38).then_inc(sem("v_chain"), 1)
                ve.wait_ge(sem("v_chain"), count.take("v_chain"))
                settle()
                ve.max(top[:, 8:16], pairs_left).then_inc(sem("v_chain"), 1)
                ve.wait_ge(sem("v_chain"), count.take("v_chain"))
                settle()
                ve.max_index(top_pair[:, 8:16], top[:, 8:16], pairs_left).then_inc(sem("v_chain"), 1)
                ve.wait_ge(sem("v_chain"), count.take("v_chain"))
                ve.tensor_scalar(neg_top, top[:, 0:1], -1.0, None, ALU.mult).then_inc(sem("top_ready"), 1)
                ve.tensor_scalar(place[:, 0:16], top_pair, 4, None, ALU.logical_shift_right)
                then(ve.tensor_scalar(place[:, 16:32], top_pair, 15, None, ALU.bitwise_and))
                then(ve.tensor_copy(place_f, place))
                for half in range(2):
                    at = slice(16 * half, 16 * half + 16)
                    grid = spread(match, (16, 16), (1, 16))
                    then(ve.tensor_tensor(grid, spread(place_f[:, at], (1, 16), (0, 16)),
                                          spread(counter, (0, 16), (1, 16)), ALU.is_equal))
                    then(ve.tensor_tensor(grid, grid, spread(best_key_f[:, at], (0, 16), (1, 16)), ALU.mult))
                    then(ve.tensor_reduce(picked[:, at], grid, X, ALU.add))
                then(ve.scalar_tensor_tensor(out=expert_u[:, 16 * t:16 * t + 16], in0=picked[:, 0:16],
                                             scalar=float(N_KEYS), in1=picked[:, 16:32], op0=ALU.mult, op1=ALU.add))
                ve.sem_inc(sem("experts_ready"), 1)

            def dot(t, ks):
                for k in ks:
                    ve.wait_ge(sem(f"u{k % RING}_landed"), count.take(f"u{k % RING}_landed", 16))
                    row = arena_u[:, k % RING, :]
                    ve.tensor_tensor_reduce(row, row, nat[:, t, :], 1.0, 0.0, ALU.mult, ALU.add, dots[:, k:k + 1])\
                        .then_inc(sem("dot_done"), 1)

            def weights_of(t):
                then(ve.reciprocal(mass[:, t:t + 1], mass[:, t:t + 1]))
                ve.wait_ge(sem("gelu_ready"), count.take("gelu_ready"))
                ve.tensor_copy(expert_v[:, 16 * t:16 * t + 16], expert_u[:, 16 * t:16 * t + 16])
                then(ve.scalar_tensor_tensor(out=weight[:, 16 * t:16 * t + 16], in0=gate_w[:, 16 * t:16 * t + 16],
                                             scalar=mass[:, t:t + 1], in1=gelu, op0=ALU.mult, op1=ALU.mult))
                ve.sem_inc(sem("weight_ready"), 1)

            def unit(t, ahead=True, more=False, first=False):
                if not first:
                    dot(t, range(8))
                ve.wait_ge(sem("gate_w_ready"), count.take("gate_w_ready"))
                if ahead:
                    choose(1 - t)
                dot(t, range(0 if first else 8, TOPK))
                weights_of(t)
                if more:
                    query_rms()

            def peer():
                ve.memset(zeros, 0.0)
                then(ve.memset(ones, 1.0))
                ve.sem_inc(sem("peer_set"), 1)
                query_rms()
                choose(0)
                unit(0, more=True, first=True)
                per = {f"u{k}_landed": 64 for k in range(RING)}
                with count.loop(P_HEADS - 2, gate_w_ready=2, gelu_ready=2, rms_ready=1, key_scores_done=1,
                            peer_sq_done=1, v_chain=CHOOSE_STEPS, **per):
                    unit(1)
                    unit(0, more=True)
                unit(1)
                unit(0)
                unit(1, ahead=False)
                for t in range(NT):
                    ve.wait_ge(sem("v_used"), count.take("v_used", (N_UNITS - 1) * TOPK if t == 0 else TOPK))
                    for k in range(2):
                        part = h[:, t, k * HALF:(k + 1) * HALF]
                        last = ve.tensor_tensor(part, part, ps[2 * t + k][:, :], ALU.add)
                    last.then_inc(sem("y_ready"), 1)

            def differential_weight():
                ve.wait_ge(sem("lam_landed"), count.take("lam_landed", 16))
                for n in range(2):
                    ve.tensor_tensor_reduce(lam_prod, lam_in[:, 128 * n:128 * n + 64], lam_in[:, 128 * n + 64:128 * n + 128],
                                            1.0, 0.0, ALU.mult, ALU.add, lam_sum[:, n:n + 1]).then_inc(sem("lam_summed"), 1)
                    ve.wait_ge(sem("lam_summed"), count.take("lam_summed"))
                ve.wait_ge(sem("lam_exp"), count.take("lam_exp"))
                then(ve.scalar_tensor_tensor(out=lam_exp[:, 2:3], in0=lam_exp[:, 1:2], scalar=-LAM_INIT,
                                             in1=lam_exp[:, 0:1], op0=ALU.add, op1=ALU.subtract))
                ve.wait_ge(sem("subln_landed"), count.take("subln_landed", 16))
                then(ve.tensor_scalar(subln, subln, 1.0 - LAM_INIT, None, ALU.mult))

            ve.wait_ge(sem("bias_in_landed"), count.take("bias_in_landed", 32))
            then(ve.tensor_scalar(relb_sb[0:32, :], relb_sb[0:32, :], -1.0, None, ALU.mult))
            ve.memset(relb_sb[32:33, :], BIG).then_inc(sem("relb_set"), 1)
            attention_layer(differential, v_chain=22, rms_ready=2)
            ve.sem_inc(sem("nat_ready"), 2)
            out_and_mlp(0)
            attention_layer(plain, v_chain=8)
            ve.sem_inc(sem("nat_ready"), 2)
            out_and_mlp(2, norm1)
            split_low(0, 0, width=C_END)
            take_turned_low()
            split_low(1, 1, width=C_END)
            split_low(2, 0, width=C_END)
            angles()
            for gain, scale in ((gain_q, -(HD ** -0.5)), (gain_mq, -(QK ** -0.5))):
                then(ve.tensor_scalar(gain, gain, scale, None, ALU.mult))
            for c in range(3, NB):
                split_low(c % 4, c % 2, width=C_END)
            hybrid_attention()
            ve.sem_inc(sem("attention_done"), 1)
            split_low(2, 0)
            take_turned_low()
            split_low(3, 1)
            split_low(0, 0)
            split_low(1, 1)
            add_residual(1.0, norm2)
            take_turned()
            peer()


def kernel(**inputs):
    import concourse.bacc as bacc
    from concourse.bass_utils import run_bass_kernel_spmd

    nc = bacc.Bacc("TRN2", target_bir_lowering=False, num_devices=1)
    arrays = {name: np.ascontiguousarray(value) for name, value in inputs.items()}
    arrays.update(const=shape_constants(), buckets=bucket_table(), freqs=rope_frequencies())
    dram = {}
    for name, a in arrays.items():
        dram[name] = nc.dram_tensor("in_" + name, a.shape, mybir.dt.from_np(a.dtype), kind="ExternalInput").ap()
    out = nc.dram_tensor("out_y", (1, S, D), F32, kind="ExternalOutput").ap()
    build(nc, dram, out)
    result = run_bass_kernel_spmd(nc, [{"in_" + n: a for n, a in arrays.items()}], core_ids=[0])
    return result.results[0]["out_y"]
```
